# Optimizing a Trainium2 kernel written in Bass

```python
import math
import jax, jax.numpy as jnp
from jax import lax
import numpy as np
import jax
import jax.numpy as jnp

D_MODEL = 1024
BATCH = 1
SEQ = 256
DEPTH = 1

N_META = 16
BLOCK = 128
D_FF = 2816
EPS = 1e-6
NEG_INF = -1e30
MLA_HEADS = 8
MLA_Q_RANK = 256
MLA_KV_RANK = 128
MLA_NOPE_DIM = 64
MLA_ROPE_DIM = 32
MLA_QK_DIM = MLA_NOPE_DIM + MLA_ROPE_DIM
MLA_V_DIM = 64
ROPE_THETA = 10000.0
FOX_HEADS = 8
FOX_HEAD_DIM = 64
D_MIX = MLA_HEADS * MLA_V_DIM + FOX_HEADS * FOX_HEAD_DIM
IN_SPLITS = (MLA_Q_RANK, MLA_KV_RANK, MLA_ROPE_DIM, 3 * FOX_HEADS * FOX_HEAD_DIM, FOX_HEADS)
D_IN = sum(IN_SPLITS)


def rms_norm(x, g):
    xf = x.astype(jnp.float32)
    y = xf * lax.rsqrt(jnp.mean(xf * xf, axis=-1, keepdims=True) + EPS)
    return (y * g.astype(jnp.float32)).astype(x.dtype)

def swiglu(x, w_gate, w_up, w_down):
    return (jax.nn.silu(x @ w_gate) * (x @ w_up)) @ w_down

def rope(x, pos):
    half = x.shape[-1] // 2
    inv_freq = 1.0 / (ROPE_THETA ** (jnp.arange(half, dtype=jnp.float32) / half))
    ang = pos.astype(jnp.float32)[:, None] * inv_freq[None, :]
    cos = jnp.cos(ang)[None, :, None, :].astype(x.dtype)
    sin = jnp.sin(ang)[None, :, None, :].astype(x.dtype)
    x1, x2 = x[..., :half], x[..., half:]
    return jnp.concatenate([x1 * cos - x2 * sin, x2 * cos + x1 * sin], axis=-1)

def block_causal_attention(q, k, v, scale, key_valid, cum=None):
    L = q.shape[1]
    outs = []
    for i in range(L // BLOCK):
        q0, q1 = i * BLOCK, (i + 1) * BLOCK
        s = jnp.einsum('bqhd,bkhd->bhqk', q[:, q0:q1], k[:, :q1],
                       preferred_element_type=jnp.float32) * scale
        if cum is not None:
            cq = jnp.transpose(cum[:, q0:q1], (0, 2, 1))[:, :, :, None]
            ck = jnp.transpose(cum[:, :q1], (0, 2, 1))[:, :, None, :]
            s = s + (cq - ck)
        q_pos = q0 + jnp.arange(BLOCK)
        k_pos = jnp.arange(q1)
        mask = (k_pos[None, :] <= q_pos[:, None]) & key_valid[None, :q1]
        s = jnp.where(mask[None, None], s, NEG_INF)
        p = jax.nn.softmax(s, axis=-1).astype(v.dtype)
        outs.append(jnp.einsum('bhqk,bkhd->bqhd', p, v[:, :q1]))
    return jnp.concatenate(outs, axis=1)

def hybrid_mixer(u, pos, key_valid, w_in, g_cq, w_uq, g_ckv, w_ukv, g_q_mla, g_k_mla,
                 b_forget, g_q_fox, g_k_fox, w_out):
    B, L, _ = u.shape
    proj = u @ w_in
    offs = [int(o) for o in np.cumsum(IN_SPLITS)[:-1]]
    c_q, c_kv, k_pe, fox_qkv, f_logit = jnp.split(proj, offs, axis=-1)

    q = (rms_norm(c_q, g_cq) @ w_uq).reshape(B, L, MLA_HEADS, MLA_QK_DIM)
    q = rms_norm(q, g_q_mla)
    q = jnp.concatenate([q[..., :MLA_NOPE_DIM], rope(q[..., MLA_NOPE_DIM:], pos)], axis=-1)
    kv = (rms_norm(c_kv, g_ckv) @ w_ukv).reshape(B, L, MLA_HEADS, MLA_NOPE_DIM + MLA_V_DIM)
    k_nope, v = kv[..., :MLA_NOPE_DIM], kv[..., MLA_NOPE_DIM:]
    k_pe_b = jnp.broadcast_to(k_pe[:, :, None, :], (B, L, MLA_HEADS, MLA_ROPE_DIM))
    k = rms_norm(jnp.concatenate([k_nope, k_pe_b], axis=-1), g_k_mla)
    k = jnp.concatenate([k[..., :MLA_NOPE_DIM], rope(k[..., MLA_NOPE_DIM:], pos)], axis=-1)
    o_mla = block_causal_attention(q, k, v, 1.0 / math.sqrt(MLA_QK_DIM), key_valid)

    fq, fk, fv = jnp.split(fox_qkv.reshape(B, L, 3, FOX_HEADS, FOX_HEAD_DIM), 3, axis=2)
    fq = rms_norm(fq[:, :, 0], g_q_fox)
    fk = rms_norm(fk[:, :, 0], g_k_fox)
    fv = fv[:, :, 0]
    log_f = jax.nn.log_sigmoid(f_logit.astype(jnp.float32) + b_forget.astype(jnp.float32))
    cum = jnp.cumsum(log_f, axis=1)
    o_fox = block_causal_attention(fq, fk, fv, 1.0 / math.sqrt(FOX_HEAD_DIM), key_valid, cum)

    o = jnp.concatenate([o_mla.reshape(B, L, MLA_HEADS * MLA_V_DIM),
                         o_fox.reshape(B, L, FOX_HEADS * FOX_HEAD_DIM)], axis=-1)
    return o @ w_out

def first_inputs(seed: int = 0) -> dict:
    key = jax.random.key(seed)
    ks = jax.random.split(key, 24)
    f32 = jnp.float32

    def nrm(k, shape, fan_in):
        return jax.random.normal(k, shape, f32) * (fan_in ** -0.5)

    def gain(k, n):
        return 1.0 + 0.02 * jax.random.normal(k, (DEPTH, n), f32)

    return {
        "x": jax.random.normal(ks[0], (BATCH, SEQ, D_MODEL), f32),
        "meta_tokens": jax.random.normal(ks[1], (N_META, D_MODEL), f32),
        "g_ffn1": gain(ks[2], D_MODEL),
        "w1_gate": nrm(ks[3], (DEPTH, D_MODEL, D_FF), D_MODEL),
        "w1_up": nrm(ks[4], (DEPTH, D_MODEL, D_FF), D_MODEL),
        "w1_down": nrm(ks[5], (DEPTH, D_FF, D_MODEL), D_FF),
        "g_mix": gain(ks[6], D_MODEL),
        "w_in": nrm(ks[7], (DEPTH, D_MODEL, D_IN), D_MODEL),
        "g_cq": gain(ks[8], MLA_Q_RANK),
        "w_uq": nrm(ks[9], (DEPTH, MLA_Q_RANK, MLA_HEADS * MLA_QK_DIM), MLA_Q_RANK),
        "g_ckv": gain(ks[10], MLA_KV_RANK),
        "w_ukv": nrm(ks[11], (DEPTH, MLA_KV_RANK, MLA_HEADS * (MLA_NOPE_DIM + MLA_V_DIM)), MLA_KV_RANK),
        "g_q_mla": gain(ks[12], MLA_QK_DIM),
        "g_k_mla": gain(ks[13], MLA_QK_DIM),
        "b_forget": jax.random.uniform(ks[14], (DEPTH, FOX_HEADS), f32, 1.0, 4.0),
        "g_q_fox": gain(ks[15], FOX_HEAD_DIM),
        "g_k_fox": gain(ks[16], FOX_HEAD_DIM),
        "w_out": nrm(ks[17], (DEPTH, D_MIX, D_MODEL), D_MIX),
        "g_ffn2": gain(ks[18], D_MODEL),
        "w2_gate": nrm(ks[19], (DEPTH, D_MODEL, D_FF), D_MODEL),
        "w2_up": nrm(ks[20], (DEPTH, D_MODEL, D_FF), D_MODEL),
        "w2_down": nrm(ks[21], (DEPTH, D_FF, D_MODEL), D_FF),
    }

def first_block(x, meta_tokens, g_ffn1, w1_gate, w1_up, w1_down, g_mix, w_in, g_cq, w_uq,
              g_ckv, w_ukv, g_q_mla, g_k_mla, b_forget, g_q_fox, g_k_fox, w_out,
              g_ffn2, w2_gate, w2_up, w2_down):
    B = x.shape[0]
    pad = BLOCK - N_META
    meta = jnp.broadcast_to(meta_tokens.astype(x.dtype)[None], (B, N_META, D_MODEL))
    h = jnp.concatenate([jnp.zeros((B, pad, D_MODEL), x.dtype), meta, x], axis=1)
    L = h.shape[1]
    idx = jnp.arange(L)
    key_valid = idx >= pad
    pos = jnp.maximum(idx - pad, 0).astype(jnp.int32)
    for l in range(DEPTH):
        h = h + 0.5 * swiglu(rms_norm(h, g_ffn1[l]), w1_gate[l], w1_up[l], w1_down[l])
        h = h + hybrid_mixer(rms_norm(h, g_mix[l]), pos, key_valid, w_in[l], g_cq[l], w_uq[l],
                             g_ckv[l], w_ukv[l], g_q_mla[l], g_k_mla[l], b_forget[l],
                             g_q_fox[l], g_k_fox[l], w_out[l])
        h = h + 0.5 * swiglu(rms_norm(h, g_ffn2[l]), w2_gate[l], w2_up[l], w2_down[l])
    return h[:, BLOCK:]


HG_HEADS = 8
HG_DK = 128
HG_DV = D_MODEL // HG_HEADS
HG_KW = HG_HEADS * HG_DK
HG_VW = HG_HEADS * HG_DV
HG_CHUNK = 32
CONV_WIDTH = D_MODEL
CONV_K = 31
IN_SIZES = (HG_KW, HG_KW, HG_VW, HG_VW, CONV_WIDTH, CONV_WIDTH, D_MODEL, D_MODEL)
IN_SPLITS_2 = tuple(int(s) for s in np.cumsum(IN_SIZES)[:-1])
N_IN = sum(IN_SIZES)
PEER_HEADS = 8
PEER_NKEYS = 128
PEER_EXPERTS = PEER_NKEYS * PEER_NKEYS
PEER_DQ = 256
PEER_TOPK = 16
PEER_BLOCK = 128


def rms_norm_2(x, g):
    xf = x.astype(jnp.float32)
    y = xf * lax.rsqrt(jnp.mean(xf * xf, axis=-1, keepdims=True) + EPS)
    return (y * g.astype(jnp.float32)).astype(x.dtype)

def layer_norm(x, g, b):
    xf = x.astype(jnp.float32)
    mu = jnp.mean(xf, axis=-1, keepdims=True)
    xc = xf - mu
    y = xc * lax.rsqrt(jnp.mean(xc * xc, axis=-1, keepdims=True) + EPS)
    return (y * g.astype(jnp.float32) + b.astype(jnp.float32)).astype(x.dtype)

def hgrn2_chunkwise(q, k, v, logf):
    B, S, H, dk = q.shape
    dv = v.shape[-1]
    n = S // HG_CHUNK

    def to_chunks(t):
        return t.reshape(B, n, HG_CHUNK, H, t.shape[-1]).transpose(1, 0, 3, 2, 4)

    causal = jnp.tril(jnp.ones((HG_CHUNK, HG_CHUNK), dtype=bool))

    def step(state, inp):
        qt, kt, vt, lt = inp
        bcum = jnp.cumsum(lt, axis=2)
        rel = bcum[:, :, :, None, :] - bcum[:, :, None, :, :]
        decay = jnp.exp(jnp.where(causal[:, :, None], rel, -jnp.inf))
        scores = jnp.einsum('bhtk,bhsk,bhtsk->bhts', qt, kt, decay)
        o = jnp.einsum('bhts,bhsv->bhtv', scores, vt)
        o = o + jnp.einsum('bhtk,bhkv->bhtv', qt * jnp.exp(bcum), state)
        blast = bcum[:, :, -1:, :]
        state = (jnp.exp(blast[:, :, 0, :])[..., None] * state
                 + jnp.einsum('bhsk,bhsv->bhkv', kt * jnp.exp(blast - bcum), vt))
        return state, o

    s0 = jnp.zeros((B, H, dk, dv), jnp.float32)
    _, o = lax.scan(step, s0, (to_chunks(q), to_chunks(k), to_chunks(v), to_chunks(logf)))
    return o.transpose(1, 0, 3, 2, 4).reshape(B, S, H, dv)

def causal_depthwise_conv(u, w, b):
    y = lax.conv_general_dilated(
        u, w[:, None, :].astype(u.dtype), window_strides=(1,),
        padding=((CONV_K - 1, 0),), dimension_numbers=('NWC', 'WIO', 'NWC'),
        feature_group_count=u.shape[-1])
    return y + b

def peer_layer(h, w_q, sub_keys, u_tab, v_tab):
    B, S, D = h.shape
    T = B * S
    hf = h.reshape(T, D)
    q = (hf @ w_q).reshape(T, PEER_HEADS, 2, PEER_DQ // 2)
    s = jnp.einsum('thpd,hpnd->thpn', q, sub_keys)
    sc, idx = lax.top_k(s, PEER_TOPK)
    cand = (sc[:, :, 0, :, None] + sc[:, :, 1, None, :]).reshape(T, PEER_HEADS, PEER_TOPK * PEER_TOPK)
    cidx = (idx[:, :, 0, :, None] * PEER_NKEYS + idx[:, :, 1, None, :]).reshape(T, PEER_HEADS, PEER_TOPK * PEER_TOPK)
    top_sc, pos = lax.top_k(cand, PEER_TOPK)
    eidx = jnp.take_along_axis(cidx, pos, axis=-1)
    gate = jax.nn.softmax(top_sc.astype(jnp.float32), axis=-1).astype(h.dtype)
    nb = T // PEER_BLOCK

    def block(args):
        hb, eb, gb = args
        act = jax.nn.gelu(jnp.einsum('thkd,td->thk', u_tab[eb], hb), approximate=False)
        return jnp.einsum('thk,thkd->td', gb * act, v_tab[eb])

    y = lax.map(block, (hf.reshape(nb, PEER_BLOCK, D),
                        eidx.reshape(nb, PEER_BLOCK, PEER_HEADS, PEER_TOPK),
                        gate.reshape(nb, PEER_BLOCK, PEER_HEADS, PEER_TOPK)))
    return y.reshape(B, S, D)

def second_inputs(seed: int = 0) -> dict:
    key = jax.random.key(seed)
    ks = jax.random.split(key, 24)
    L = DEPTH

    def nrm(k, shape, scale):
        return jax.random.normal(k, shape, jnp.float32) * scale

    return {
        'x': nrm(ks[0], (BATCH, SEQ, D_MODEL), 1.0),
        'c': nrm(ks[1], (BATCH, D_MODEL), 1.0),
        'ada_w': nrm(ks[2], (L, D_MODEL, 6 * D_MODEL), 0.5 * D_MODEL ** -0.5),
        'ada_b': nrm(ks[3], (L, 6 * D_MODEL), 0.02),
        'norm1_g': 1.0 + nrm(ks[4], (L, D_MODEL), 0.02),
        'w_in': nrm(ks[5], (L, D_MODEL, N_IN), D_MODEL ** -0.5),
        'lb_logits': nrm(ks[6], (L + 1, HG_KW), 0.5),
        'hg_norm_g': 1.0 + nrm(ks[7], (L, HG_VW), 0.02),
        'w_a': nrm(ks[8], (L, HG_VW, D_MODEL), HG_VW ** -0.5),
        'conv_w': nrm(ks[9], (L, CONV_K, CONV_WIDTH), CONV_K ** -0.5),
        'conv_b': nrm(ks[10], (L, CONV_WIDTH), 0.02),
        'conv_ln_g': 1.0 + nrm(ks[11], (L, CONV_WIDTH), 0.02),
        'conv_ln_b': nrm(ks[12], (L, CONV_WIDTH), 0.02),
        'w_b': nrm(ks[13], (L, CONV_WIDTH, D_MODEL), CONV_WIDTH ** -0.5),
        'w_out': nrm(ks[14], (L, D_MODEL, D_MODEL), D_MODEL ** -0.5),
        'norm2_g': 1.0 + nrm(ks[15], (L, D_MODEL), 0.02),
        'peer_wq': nrm(ks[16], (L, D_MODEL, PEER_HEADS * PEER_DQ), D_MODEL ** -0.5),
        'peer_keys': nrm(ks[17], (L, PEER_HEADS, 2, PEER_NKEYS, PEER_DQ // 2), (PEER_DQ // 2) ** -0.5),
        'peer_u': nrm(ks[18], (L, PEER_EXPERTS, D_MODEL), D_MODEL ** -0.5),
        'peer_v': nrm(ks[19], (L, PEER_EXPERTS, D_MODEL), PEER_HEADS ** -0.5),
        'final_g': 1.0 + nrm(ks[20], (D_MODEL,), 0.02),
    }

def second_block(x, c, ada_w, ada_b, norm1_g, w_in, lb_logits, hg_norm_g, w_a, conv_w, conv_b,
              conv_ln_g, conv_ln_b, w_b, w_out, norm2_g, peer_wq, peer_keys, peer_u, peer_v,
              final_g):
    B, S, D = x.shape
    lower_bounds = jnp.cumsum(jax.nn.softmax(lb_logits.astype(jnp.float32), axis=0), axis=0)

    def heads(t):
        return t.reshape(B, S, HG_HEADS, -1)

    h = x
    for l in range(DEPTH):
        ada = (jax.nn.silu(c) @ ada_w[l] + ada_b[l])[:, None, :]
        sh1, sc1, g1, sh2, sc2, g2 = jnp.split(ada, 6, axis=-1)

        u = rms_norm_2(h, norm1_g[l]) * (1 + sc1) + sh1
        z = u @ w_in[l]
        zq, zf, zi, zg, zca, zcb, zga, zgb = jnp.split(z, IN_SPLITS_2, axis=-1)

        lb = lower_bounds[l]
        f = lb + (1.0 - lb) * jax.nn.sigmoid(zf.astype(jnp.float32))
        o = hgrn2_chunkwise(heads(zq.astype(jnp.float32)), heads(1.0 - f),
                            heads(zi.astype(jnp.float32)), heads(jnp.log(f)))
        o = rms_norm_2(o, hg_norm_g[l].reshape(HG_HEADS, HG_DV)).reshape(B, S, HG_VW).astype(x.dtype)
        y_a = (o * jax.nn.silu(zg)) @ w_a[l]

        glu = zca * jax.nn.sigmoid(zcb)
        cv = causal_depthwise_conv(glu, conv_w[l], conv_b[l])
        cv = jax.nn.silu(layer_norm(cv, conv_ln_g[l], conv_ln_b[l]))
        y_b = cv @ w_b[l]

        merged = jax.nn.sigmoid(zga) * y_a + jax.nn.sigmoid(zgb) * y_b
        h = h + g1 * (merged @ w_out[l])

        u2 = rms_norm_2(h, norm2_g[l]) * (1 + sc2) + sh2
        h = h + g2 * peer_layer(u2, peer_wq[l], peer_keys[l], peer_u[l], peer_v[l])

    return rms_norm_2(h, final_g)


def setup_inputs(seed=0):
    out = dict(first_inputs(seed))
    for name, value in second_inputs(seed + 1).items():
        if name != "x":
            out[name + "_2"] = value
    return out


def reference(
    x, meta_tokens, g_ffn1, w1_gate, w1_up, w1_down, g_mix, w_in, g_cq, w_uq, g_ckv, w_ukv,
    g_q_mla, g_k_mla, b_forget, g_q_fox, g_k_fox, w_out, g_ffn2, w2_gate, w2_up, w2_down, c_2,
    ada_w_2, ada_b_2, norm1_g_2, w_in_2, lb_logits_2, hg_norm_g_2, w_a_2, conv_w_2, conv_b_2,
    conv_ln_g_2, conv_ln_b_2, w_b_2, w_out_2, norm2_g_2, peer_wq_2, peer_keys_2, peer_u_2,
    peer_v_2, final_g_2,
):
    x = first_block(
        x, meta_tokens, g_ffn1, w1_gate, w1_up, w1_down, g_mix, w_in, g_cq, w_uq, g_ckv, w_ukv,
        g_q_mla, g_k_mla, b_forget, g_q_fox, g_k_fox, w_out, g_ffn2, w2_gate, w2_up, w2_down,
    )
    return second_block(
        x, c_2, ada_w_2, ada_b_2, norm1_g_2, w_in_2, lb_logits_2, hg_norm_g_2, w_a_2, conv_w_2,
        conv_b_2, conv_ln_g_2, conv_ln_b_2, w_b_2, w_out_2, norm2_g_2, peer_wq_2, peer_keys_2,
        peer_u_2, peer_v_2, final_g_2,
    )


_drawn_inputs = setup_inputs


def setup_inputs(seed=0):
    import zlib

    import numpy as np

    out = dict(_drawn_inputs(seed))
    spreads = {}
    factors = {'g_ffn1': 5.328,
     'g_mix': 5.182,
     'g_cq': 8.0,
     'g_ckv': 8.0,
     'g_q_mla': 8.0,
     'g_k_mla': 8.0,
     'g_q_fox': 8.0,
     'g_k_fox': 8.0,
     'g_ffn2': 6.301,
     'ada_b_2': 3.912,
     'norm1_g_2': 8.0,
     'hg_norm_g_2': 45.881,
     'conv_b_2': 64.0,
     'conv_ln_g_2': 64.0,
     'conv_ln_b_2': 64.0,
     'norm2_g_2': 59.456,
     'final_g_2': 7.932}
    for name, (base, spread) in spreads.items():
        noise = np.random.default_rng([zlib.crc32(name.encode()), seed]).standard_normal(out[name].shape)
        drawn = base * np.exp(spread * noise) if base else spread * noise
        out[name] = jnp.asarray(drawn.astype(out[name].dtype))
    for name, factor in factors.items():
        out[name] = (out[name] * factor).astype(out[name].dtype)
    return out
```

```python
from contextlib import ExitStack

import numpy as np

import concourse.bass as bass
from concourse import mybir

F32 = mybir.dt.float32
U32 = mybir.dt.uint32
I32 = mybir.dt.int32
ACT = mybir.ActivationFunctionType
ALU = mybir.AluOpType
AX_X = mybir.AxisListType.X

P = 128
D = 1024
KT = D // P
SEQ = 256
N_META = 16
T = N_META + SEQ
X0 = N_META
TT = SEQ // P
D_FF = 2816
FT = D_FF // P
EPS = 1e-6
HEADS = 8
QK = 96
NOPE = 64
ROPE = 32
HD = 64
PE_ROW = 64
FL_ROW = 96
CONV_K = 31
PAD = CONV_K - 1
TOPK = 16
NKEYS = 128
SLOTS = HEADS * TOPK
RING = 4
BLOCKS = 16
PIECE = BLOCKS * P
ADA_Q = 4
ADA_W = 6 * D // ADA_Q
GR = 16
FOX_SCALE = HD ** -0.5
MLA_SCALE = QK ** -0.5
NEG = -1e30

FFN_P = FT + FT * KT // BLOCKS
PARTS = [("ffn1", FFN_P), ("w_in", 8), ("w_out", 4), ("ffn2", FFN_P), ("zi", 4), ("z", 28),
         ("w_a", 4), ("w_b", 4), ("w_out_2", 4), ("wq", 8)]
BASE = {}
_at = 0
for _name, _n in PARTS:
    BASE[_name] = _at
    _at += _n
N_PIECES = _at

VECS = [("g_ffn1", 8), ("g_mix", 8), ("g_ffn2", 8), ("norm1", 8), ("lb0", 8), ("lb1", 8), ("hg_g", 8),
        ("conv_b", 8), ("ln_g", 8), ("ln_b", 8), ("norm2", 8), ("c", 8), ("ada_b", 48), ("g_cq", 2),
        ("g_ckv", 1), ("g_q", 1), ("g_k", 1), ("g_fq", 1), ("g_fk", 1), ("b_f", 1), ("conv_w", 8 * CONV_K)]
COL = {}
_at = 0
for _name, _n in VECS:
    COL[_name] = _at
    _at += _n
N_COLS = _at

CONSTS = [("ident", P), ("mean_d", P), ("mean_256", P), ("mean_128", P), ("mean_64", P), ("mean_96", P),
          ("ones", P), ("rot", P), ("cos", T), ("sin", T), ("neg_mask", P), ("iota", TOPK)]
CON = {}
_at = 0
for _name, _n in CONSTS:
    CON[_name] = (_at, _n)
    _at += _n
N_CONSTS = _at
LEVELS = [0, 1, 2, 4, 8, 16, 32, 64]


def constants():
    c = np.zeros((P, N_CONSTS), np.float32)

    def put(name, a):
        at = CON[name][0]
        c[:a.shape[0], at:at + a.shape[1]] = a

    put("ident", np.eye(P, dtype=np.float32))
    for name, n in (("mean_d", D), ("mean_256", 256), ("mean_128", 128)):
        put(name, np.full((P, P), 1.0 / n, np.float32))
    put("mean_96", np.full((QK, QK), 1.0 / QK, np.float32))
    put("mean_64", np.kron(np.eye(2), np.full((HD, HD), 1.0 / HD)).astype(np.float32))
    put("ones", np.ones((P, P), np.float32))
    half = ROPE // 2
    rot = np.zeros((QK, QK), np.float32)
    for i in range(half):
        rot[NOPE + half + i, NOPE + i] = -1.0
        rot[NOPE + i, NOPE + half + i] = 1.0
    put("rot", rot)
    freq = (1.0 / (np.float32(10000.0) ** (np.arange(half, dtype=np.float32) / np.float32(half)))).astype(np.float32)
    ang = (np.arange(T, dtype=np.float32)[None, :] * freq[:, None]).astype(np.float32).astype(np.float64)
    cos = np.ones((QK, T), np.float32)
    sin = np.zeros((QK, T), np.float32)
    for at in (NOPE, NOPE + half):
        cos[at:at + half] = np.cos(ang)
        sin[at:at + half] = np.sin(ang)
    put("cos", cos)
    put("sin", sin)
    put("neg_mask", np.where(np.arange(P)[None, :] > np.arange(P)[:, None], NEG, 0.0).astype(np.float32))
    sel = np.zeros((P, HEADS, T), np.float32)
    for h in range(HEADS):
        sel[FL_ROW + h, h] = 1.0 / FOX_SCALE
    put("iota", np.broadcast_to(np.arange(TOPK, dtype=np.float32), (P, TOPK)))
    masks = np.zeros((P, len(LEVELS), P), np.uint32)
    s, t = np.arange(P)[:, None], np.arange(P)[None, :]
    for n, b in enumerate(LEVELS):
        masks[:, n] = (s == t) if b == 0 else ((t // b) % 2 == 1) & (s // b == t // b - 1)
    return c, sel, masks.reshape(P, -1)


def runs(base, n, peel=0):
    at, out = base, []
    while at < base + n:
        left = base + n - at
        if at % RING == 0 and left >= 2 * RING and at - base >= peel:
            out.append((at, left // RING))
            at += left // RING * RING
        else:
            out.append((at, 0))
            at += 1
    return out


def each_piece(eng, base, n, body, peel=0):
    for at, turns in runs(base, n, peel):
        if not turns:
            body(at, at % RING)
            continue
        with eng.Fori(0, turns) as i:
            for slot in range(RING):
                body(i * RING + (at + slot), slot)


def each_turn(eng, n, body):
    with eng.Fori(0, n) as i:
        body(i)


def program(nc, a, out):
    ctx = ExitStack()
    with ctx:
        def sb(name, shape, dt=F32):
            return ctx.enter_context(nc.sbuf_tensor(name, shape, dt))

        def sem(name):
            return ctx.enter_context(nc.semaphore(name))

        ps = ctx.enter_context(nc.psum_tensor("ps", [P, 8, 512], F32))
        ring = sb("ring", [P, RING, PIECE])
        h = sb("h", [P, KT, T])
        u_all = sb("u", [P, KT * T])
        u = u_all[:, :].rearrange("p (k t) -> p k t", t=T)
        cols = sb("cols", [P, N_COLS])
        con = sb("con", [P, N_CONSTS])
        masks = sb("masks", [P, len(LEVELS) * P], U32)
        keys = sb("keys", [P, 2 * HEADS, NKEYS])
        rstd = sb("rstd", [P, T])
        silu_c = sb("silu_c", [P, KT])
        ada = sb("ada", [P, 48])
        lb = sb("lb", [P, 6, KT])
        gain1 = sb("gain1", [P, KT])
        gain2 = sb("gain2", [P, KT])
        eps = sb("eps", [P, 1])
        ARENA = 32256
        arena = sb("arena", [P, ARENA])
        spot = [0]

        def place(at=None):
            if at is not None:
                spot[0] = at

        def view(*shape):
            n = int(np.prod(shape))
            assert spot[0] + n <= ARENA, (spot[0], n)
            v = arena[:, spot[0]:spot[0] + n]
            spot[0] += n
            names = "abcd"[:len(shape)]
            if len(shape) == 1:
                return v
            return v.rearrange(f"p ({' '.join(names)}) -> p {' '.join(names)}",
                               **dict(zip(names, shape)))

        def C(name):
            at, n = CON[name]
            return con[:, at:at + n]

        def V(name, k=0, n=1):
            return cols[:, COL[name] + k:COL[name] + k + n]

        ident = C("ident")

        place(0)
        glu = view(FT, T)
        sq = view(KT, T)
        act_g = view(RING, T)
        ada_ring = view(ADA_Q, ADA_W)
        ada_acc = view(ADA_Q, ADA_W)
        wuq = view(2, HEADS * QK)
        wuk = view(HEADS * NOPE)
        wuv = view(HEADS * HD)
        w_end = spot[0]
        place(0)
        praw = view(12, T)
        fqz = view(HEADS, SEQ)
        fk = view(HEADS // 2, T)
        m_rstd = act_g
        place(FT * T + KT * T + RING * T)
        cqn = view(2, SEQ)
        ckvn = view(T)
        cumz = view(T)
        ncumz = view(T)
        logf = view(4, T)
        vM = view(3, HEADS * HD)
        vF = view(3, HEADS * HD)
        assert spot[0] <= FT * T + KT * T + RING * T + ADA_Q * ADA_W, spot[0]
        place(w_end)
        qm = view(HEADS, SEQ)
        km = view(HEADS, T)
        mrs = view(4, T)
        mx = view(64)
        nmx = view(64)
        rsum = view(64)
        rinv = view(64)
        msq = probs = m_rstd
        probsT = sq[:, 2:8, 0:P].rearrange("p (a b) t -> p a b t", a=2)
        sel = view(HEADS, T)
        oT = glu[:, 0:KT, 0:SEQ]

        place(0)
        z = view(7, KT, SEQ)
        pad_glu = view(KT, PAD + SEQ)
        zi = view(TT, D)
        suf = view(KT, SEQ)
        qt = [view(KT, SEQ), u_all[:, 0:KT * SEQ].rearrange("p (k t) -> p k t", t=SEQ)]
        kt_ = view(2, KT, SEQ)
        AT = view(HEADS, 3, P)
        sq2 = view(KT, SEQ)
        o_h = qt[0]
        place(0)
        qT = view(2 * HEADS, SEQ)
        scores = view(TT, 2 * HEADS, NKEYS)
        cand = view(HEADS, TOPK * TOPK)
        work = view(TOPK * TOPK)
        onehot = view(HEADS, TOPK, TOPK)
        hf = view(TT, D)
        h_tok = view(TT, D)
        more_rows = view(GR // 2, D)
        rows = [ring[:, r // 2, r % 2 * D:r % 2 * D + D] if r < GR // 2 else more_rows[:, r - GR // 2, :]
                for r in range(GR)]
        top = view(TT, 2 * HEADS, TOPK)
        top_i = view(TT, 2 * HEADS, TOPK)
        best = view(TT, HEADS, TOPK)
        pos_f = view(HEADS, TOPK)
        pos_hi = view(HEADS, TOPK)
        part_i = view(2, HEADS, TOPK)
        gate = view(TT, HEADS, TOPK)
        gate_s = view(TT, HEADS)
        dots = view(TT, SLOTS)
        wts = view(TT, SLOTS)
        dot8 = view(2, 8)
        fin = view(16)
        final_g = view(D)
        place(0)
        junk = view(D)
        acc = view(TT, D)
        y_gain = view(D)
        place(D * 4)
        top_u = sb("top_u", [P, 4, 8], U32)
        pos_u = sb("pos_u", [P, HEADS, TOPK], U32)
        hi_u = sb("hi_u", [P, HEADS, TOPK], U32)
        eidx = sb("eidx", [P, TT, SLOTS], U32)
        stage = sb("stage", [P, 2, 8], U32)

        landed = [sem(f"weights_landed{i}") for i in range(RING)]
        used = sem("weights_used")
        x_in = sem("x_in")
        cols_in = sem("cols_in")
        con_in = sem("con_in")
        mask_in = sem("mask_in")
        small_in = sem("small_in")
        final_in = sem("final_in")
        ada_in = [sem(f"ada_in{i}") for i in range(ADA_Q)]
        ada_step = sem("ada_step")
        ada_mm = sem("ada_mm")
        ada_done = sem("ada_done")
        set_up = sem("set_up")
        lb_e = sem("lb_e")
        lb_step = sem("lb_step")
        silu_c_done = sem("silu_c_done")
        sq_done = sem("sq_done")
        ss_done = sem("ss_done")
        sqrt_done = sem("sqrt_done")
        rstd_done = sem("rstd_done")
        u_scaled = sem("u_scaled")
        u_done = sem("u_done")
        gate_mm = sem("gate_mm")
        silu_done = sem("silu_done")
        glu_done = sem("glu_done")
        down_mm = sem("down_mm")
        h_done = sem("h_done")
        proj_mm = sem("proj_mm")
        proj_ev = sem("proj_ev")
        fv_mm = sem("fv_mm")
        fv_ev = sem("fv_ev")
        msq_done = sem("msq_done")
        mss_done = sem("mss_done")
        msqrt_done = sem("msqrt_done")
        mrec_done = sem("mrec_done")
        lat_done = sem("lat_done")
        fox_done = sem("fox_done")
        z_done = sem("z_done")
        f_exp = sem("f_exp")
        f_ln = sem("f_ln")
        cum_done = sem("cum_done")
        raw_mm = sem("raw_mm")
        raw_ev = sem("raw_ev")
        kpe_done = sem("kpe_done")
        hsq_done = sem("hsq_done")
        hss_mm = sem("hss_mm")
        hsqrt = sem("hsqrt")
        hrec = sem("hrec")
        hn_done = sem("hn_done")
        rot_mm = sem("rot_mm")
        rope_step = sem("rope_step")
        vm_mm = sem("vm_mm")
        vm_ev = sem("vm_ev")
        s_mm = sem("s_mm")
        max_done = sem("max_done")
        nmax_done = sem("nmax_done")
        exp_done = sem("exp_done")
        rinv_done = sem("rinv_done")
        p_done = sem("p_done")
        pT_mm = sem("pT_mm")
        pT_ev = sem("pT_ev")
        o_mm = sem("o_mm")
        o_ev = sem("o_ev")
        wo_mm = sem("wo_mm")
        zi_mm = sem("zi_mm")
        zi_ev = sem("zi_ev")
        z_mm = sem("z_mm")
        z_ev = sem("z_ev")
        sig_done = sem("sig_done")
        dve2 = sem("dve2")
        conv_step = sem("conv_step")
        ln_mm = sem("ln_mm")
        ln_act = sem("ln_act")
        lev_mm = sem("lev_mm")
        lev_in = sem("lev_in")
        lev_out = sem("lev_out")
        lev_up = sem("lev_up")
        oh_mm = sem("oh_mm")
        oh_ev = sem("oh_ev")
        on_mm = sem("on_mm")
        on_act = sem("on_act")
        dense_mm = sem("dense_mm")
        dense_ev = sem("dense_ev")
        q_mm = sem("q_mm")
        q_ev = sem("q_ev")
        tok_mm = sem("tok_mm")
        tok_ev = sem("tok_ev")
        sc_mm = sem("sc_mm")
        sc_ev = sem("sc_ev")
        tk = sem("topk_step")
        idx_done = sem("idx_done")
        gate_e = sem("gate_e")
        staged = sem("staged")
        idx_staged = sem("idx_staged")
        row_in = [sem(f"row_in{i}") for i in range(GR)]
        row_used = sem("row_used")
        dot_out = sem("dot_out")
        gelu_done = sem("gelu_done")
        w_done = sem("w_done")
        fin_step = sem("fin_step")
        fin_act = sem("fin_act")
        gain_mm = sem("gain_mm")
        out_done = sem("out_done")
        assert N_PIECES % RING == 2

        block = ctx.enter_context(nc.Block())
        xc = slice(X0, T)
        NORM_COLS = [slice(0, T), slice(0, T), xc, xc, xc]

        @block.sync
        def _(sp):
            sp.dma_start(h[:, :, :], a["x_t"]).then_inc(x_in, 16)

            def load(piece, slot):
                sp.wait_ge(used, piece - (RING - 1))
                src = a["stream"][piece] if isinstance(piece, int) else \
                    a["stream"][bass.ds(piece, 1)].rearrange("o p m -> p (o m)")
                sp.dma_start(ring[:, slot, :], src).then_inc(landed[slot], 16)

            for n in range(RING):
                sp.dma_start(ring[:, n, :], a["stream"][n]).then_inc(landed[n], 16)
            each_piece(sp, RING, N_PIECES - RING, load)
            sp.wait_ge(fin_step, 2 * 6)
            for t in range(TT):
                sp.dma_start(out[0, t * P:(t + 1) * P, :], acc[:, t, :]).then_inc(out_done, 16)
            sp.wait_ge(out_done, 16 * TT)

        @block.gpsimd
        def _(pool):
            pool.memset(eps[:, :], EPS).then_inc(set_up, 1)
            for n in range(KT * ADA_Q):
                kt, q = divmod(n, ADA_Q)
                if kt:
                    pool.wait_ge(ada_step, n - ADA_Q + 1)
                pool.dma_start(ada_ring[:, q, :], a["ada"][n]).then_inc(ada_in[q], 16)

            def gather(table, n, first, t, par, slot0):
                if not first:
                    pool.wait_ge(row_used, n * 8 - GR + 8)
                pool.tensor_copy(stage[:, par, :], eidx[:, t, bass.ds(slot0, 8)]).then_inc(staged, 1)
                pool.wait_ge(staged, n + 1)
                pool.sem_inc(idx_staged, 1)
                for j in range(8):
                    r = par * 8 + j
                    pool.indirect_dma_start(rows[r], None, table,
                                            bass.IndirectOffsetOnAxis(ap=stage[:, par, j:j + 1], axis=0)
                                            ).then_inc(row_in[r], 16)

            n0 = 0
            for table in (a["peer_u"], a["peer_v"]):
                for t in range(TT):
                    if n0 < TT * SLOTS // 8:
                        pool.wait_ge(idx_done, t + 1)
                    start = 0
                    if n0 == 0:
                        for par in range(2):
                            gather(table, par, True, t, par, par * 8)
                        start = 1
                    with pool.Fori(start, SLOTS // GR) as i:
                        for par in range(2):
                            gather(table, i * 2 + (n0 + par), False, t, par, i * GR + par * 8)
                    n0 += SLOTS // 8

        @block.scalar
        def _(act):
            act.dma_start(cols[:, :], a["cols"]).then_inc(cols_in, 16)
            act.dma_start(con[:, :], a["con"]).then_inc(con_in, 16)
            act.dma_start(wuq[:, :, :], a["wuq"]).then_inc(small_in, 16)
            act.dma_start(wuk, a["wuk"]).then_inc(small_in, 16)
            act.dma_start(wuv, a["wuv"]).then_inc(small_in, 16)
            act.dma_start(masks[:, :], a["masks"]).then_inc(mask_in, 16)
            act.dma_start(keys[:, :, :], a["keys"]).then_inc(small_in, 16)
            act.dma_start(sel, a["sel"]).then_inc(small_in, 16)
            act.wait_ge(cols_in, 16)
            act.activation(silu_c[:, :], V("c", 0, KT), ACT.Silu).then_inc(silu_c_done, 1)
            act.wait_ge(lb_step, 3)
            for r in (1, 2):
                act.activation(lb[:, r], lb[:, r], ACT.Exp).then_inc(lb_e, 1)

            def norm(n):
                c = NORM_COLS[n]
                w = c.stop - c.start
                if n == 0:
                    act.wait_ge(x_in, 16)
                    act.wait_ge(set_up, 1)
                else:
                    act.wait_ge(h_done, KT * n)
                dst = sq if n < 3 else sq2
                act.activation(dst[:, :, 0:w], h[:, :, c], ACT.Square).then_inc(sq_done, 1)
                act.wait_ge(ss_done, n + 1)
                act.activation(rstd[:, 0:w], ps[:, 7, 0:w], ACT.Sqrt, bias=eps[:, :]).then_inc(sqrt_done, 1)

            def ffn(k):
                base = BASE["ffn2" if k else "ffn1"]
                w = SEQ if k else T

                def body(piece, slot):
                    f = piece - (base - FT * k)
                    act.wait_ge(gate_mm, f + 1)
                    act.activation(act_g[:, slot, 0:w], ps[:, 2 * slot, 0:w], ACT.Silu).then_inc(silu_done, 1)

                each_piece(act, base, FT, body, peel=0 if k else RING)

            def attn_evac(act, n):
                hd, t = divmod(n, TT)
                half = HD * (hd % 2)
                act.wait_ge(pT_mm, n + 1)
                if n >= 2:
                    act.wait_ge(o_mm, n - 1)
                full = t + 1
                bank = 3 + n % 2
                act.activation(probsT[:, n % 2, 0:full, :],
                               ps[:, bank, 0:full * P].rearrange("p (a b) -> p a b", b=P), ACT.Copy)
                act.activation(probsT[0:N_META, n % 2, full, :], ps[0:N_META, bank, full * P:full * P + P], ACT.Copy
                               ).then_inc(pT_ev, 1)
                act.wait_ge(o_mm, n + 1)
                act.activation(oT[half:half + HD, hd // 2, t * P:(t + 1) * P],
                               ps[half:half + HD, 5 + n % 2, 0:P], ACT.Copy).then_inc(o_ev, 1)

            norm(0)
            ffn(0)
            norm(1)
            for i in range(12):
                act.wait_ge(proj_mm, i + 1)
                act.activation(praw[:, i, :], ps[:, i % 8, 0:T], ACT.Copy).then_inc(proj_ev, 1)
            act.wait_ge(ada_step, KT * ADA_Q)
            for t in range(3):
                n = P if t < 2 else N_META
                act.wait_ge(fv_mm, 1)
                act.activation(vF[0:n, t, :], ps[0:n, 4 + t, :], ACT.Copy).then_inc(fv_ev, 1)
            act.wait_ge(proj_ev, 12)
            act.activation(sq[:, 0:3, :], praw[:, 0:3, :], ACT.Square).then_inc(msq_done, 1)
            act.wait_ge(mss_done, 1)
            act.activation(m_rstd[:, :, :], ps[:, 0:4, 0:T], ACT.Sqrt, bias=eps[:, :]).then_inc(msqrt_done, 1)
            act.activation(sq[:, 0:8, :], praw[:, 4:12, :], ACT.Square).then_inc(msq_done, 1)
            for b in range(2):
                act.wait_ge(mss_done, b + 2)
                if b == 0:
                    act.wait_ge(lat_done, 3)
                else:
                    act.wait_ge(fox_done, 8)
                act.activation(m_rstd[:, :, :], ps[:, 4 - 4 * b:8 - 4 * b, 0:T], ACT.Sqrt, bias=eps[:, :]
                               ).then_inc(msqrt_done, 1)
            fr = slice(FL_ROW, FL_ROW + HEADS)
            act.wait_ge(z_done, 3)
            act.activation(logf[fr, 1, :], logf[fr, 1, :], ACT.Exp, scale=-1.0).then_inc(f_exp, 1)
            act.wait_ge(f_exp, 1)
            act.activation(logf[fr, 2, :], logf[fr, 1, :], ACT.Ln, bias=1.0).then_inc(f_ln, 1)
            for b in range(4):
                act.wait_ge(raw_mm, b + 1)
                g = 4 * (b % 2)
                if b < 2:
                    act.activation(qm[0:QK, g:g + 4, :], ps[0:QK, g:g + 4, 0:SEQ], ACT.Copy).then_inc(raw_ev, 1)
                else:
                    act.activation(km[0:NOPE, g:g + 4, :], ps[0:NOPE, g:g + 4, 0:T], ACT.Copy).then_inc(raw_ev, 1)
            for t in range(3):
                n = P if t < 2 else N_META
                act.wait_ge(vm_mm, 1)
                act.activation(vM[0:n, t, :], ps[0:n, t, :], ACT.Copy).then_inc(vm_ev, 1)
            for b in range(4):
                g = 4 * (b % 2)
                w = SEQ if b < 2 else T
                src = qm if b < 2 else km
                if b == 0:
                    act.wait_ge(raw_ev, 4)
                    act.wait_ge(fox_done, 12)
                    act.wait_ge(kpe_done, 1)
                else:
                    act.wait_ge(hss_mm, b)
                act.activation(msq[0:QK, :, 0:w], src[0:QK, g:g + 4, :], ACT.Square).then_inc(hsq_done, 1)
                act.wait_ge(hss_mm, b + 1)
                if b:
                    act.wait_ge(rope_step, 3 * b)
                act.activation(mrs[0:QK, :, 0:w], ps[0:QK, g:g + 4, 0:w], ACT.Sqrt, bias=eps[0:QK, :]
                               ).then_inc(hsqrt, 1)
            for n in range(2 * HEADS * TT):
                hd, t = divmod(n, TT)
                keys_n = X0 + P * (t + 1)
                act.wait_ge(nmax_done, n + 1)
                if n >= 4:
                    act.wait_ge(pT_mm, n - 3)
                act.activation(probs[:, n % 4, 0:keys_n], ps[:, n % 3, 0:keys_n], ACT.Exp,
                               bias=nmx[:, n:n + 1], scale=MLA_SCALE if hd < HEADS else FOX_SCALE,
                               accum_out=rsum[:, n:n + 1]).then_inc(exp_done, 1)
                if n >= 2:
                    attn_evac(act, n - 2)
            attn_evac(act, 2 * HEADS * TT - 2)
            attn_evac(act, 2 * HEADS * TT - 1)
            norm(2)
            ffn(1)
            norm(3)
            for t in range(TT):
                for half in range(2):
                    act.wait_ge(zi_mm, 1)
                    act.activation(zi[:, t, half * 512:(half + 1) * 512], ps[:, t * 2 + half, :], ACT.Copy
                                   ).then_inc(zi_ev, 1)

            def z_copy(seg):
                for m in range(KT):
                    act.wait_ge(z_mm, seg * KT + (m + 1))
                    act.activation(z[:, bass.ds(seg, 1), m, :].rearrange("p o t -> p (o t)"),
                                   ps[:, m, 0:SEQ], ACT.Copy).then_inc(z_ev, 1)

            with act.Fori(0, 7) as seg:
                z_copy(seg)
            act.wait_ge(z_ev, 7 * KT)
            for seg in (1, 2, 5, 6):
                act.activation(z[:, seg], z[:, seg], ACT.Sigmoid).then_inc(sig_done, 1)
            act.activation(z[:, 4], z[:, 4], ACT.Silu).then_inc(sig_done, 1)
            act.wait_ge(dve2, 3)
            act.activation(sq2[:, :, :], z[:, 0], ACT.Square).then_inc(ln_act, 1)
            act.wait_ge(ln_mm, 2)
            act.activation(rstd[:, 0:SEQ], ps[:, 1, 0:SEQ], ACT.Sqrt, bias=eps[:, :]).then_inc(ln_act, 1)
            act.wait_ge(dve2, 5)
            for m in range(KT):
                act.activation(z[:, 0, m, :], z[:, 0, m, :], ACT.Silu, scale=V("ln_g", m), bias=V("ln_b", m)
                               ).then_inc(ln_act, 1)
            act.wait_ge(oh_mm, 1)
            act.activation(o_h.rearrange("p h t -> p (h t)"), ps[:, 0:4, :].rearrange("p b t -> p (b t)"),
                           ACT.Copy).then_inc(oh_ev, 1)
            act.activation(sq2[:, :, :].rearrange("p h t -> p (h t)"), ps[:, 0:4, :].rearrange("p b t -> p (b t)"),
                           ACT.Square).then_inc(oh_ev, 1)
            act.wait_ge(on_mm, 1)
            act.activation(kt_[:, 0].rearrange("p h t -> p (h t)"), ps[:, 4:8, :].rearrange("p b t -> p (b t)"),
                           ACT.Sqrt, bias=eps[:, :]).then_inc(on_act, 1)
            norm(4)
            act.dma_start(final_g, a["final_g"].rearrange("(o d) -> o d", o=1).broadcast_to([P, D])
                          ).then_inc(final_in, 16)

            def q_copy(piece, slot):
                for e in range(2):
                    n = (piece - BASE["wq"]) * 2 + e
                    act.wait_ge(q_mm, n + 1)
                    act.activation(qT[:, bass.ds(n, 1), :].rearrange("p o t -> p (o t)"),
                                   ps[:, 2 * slot + e, 0:SEQ], ACT.Copy).then_inc(q_ev, 1)

            each_piece(act, BASE["wq"], 8, q_copy)
            for n in range(8):
                act.wait_ge(sc_mm, n + 1)
                t, g = divmod(n, 4)
                act.activation(scores[:, t, g * 4:g * 4 + 4, :].rearrange("p a b -> p (a b)"), ps[:, n, :],
                               ACT.Copy).then_inc(sc_ev, 1)
            for n in range(8):
                src, t, half = n // 4, n // 2 % 2, n % 2
                act.wait_ge(tok_mm, n + 1)
                act.activation((hf, h_tok)[src][:, t, half * 512:half * 512 + 512], ps[:, n, :], ACT.Copy
                               ).then_inc(tok_ev, 1)
            act.wait_ge(gain_mm, 1)
            act.wait_ge(sc_mm, 8)
            for half in range(2):
                act.activation(y_gain[:, half * 512:half * 512 + 512], ps[:, half, :], ACT.Copy).then_inc(tok_ev, 1)
            for t in range(TT):
                act.wait_ge(gate_e, 2 * t + 1)
                act.activation(gate[:, t], gate[:, t], ACT.Exp).then_inc(fin_act, 1)
            for t in range(TT):
                act.wait_ge(dot_out, (t + 1) * SLOTS // 8)
                act.activation(dots[:, t, :], dots[:, t, :], ACT.Gelu).then_inc(gelu_done, 1)
            for t in range(TT):
                act.wait_ge(fin_step, 6 * t + 3)
                act.activation(fin[:, 2 * t + 1:2 * t + 2], fin[:, 2 * t:2 * t + 1], ACT.Sqrt, bias=eps[:, :],
                               scale=1.0 / D).then_inc(fin_act, 1)

        @block.vector
        def _(dve):
            steps = {}

            def then(ins, s):
                steps[s.name] = steps.get(s.name, 0) + 1
                ins.then_inc(s, 1)
                dve.wait_ge(s, steps[s.name])

            dve.wait_ge(cols_in, 16)
            then(dve.tensor_tensor(lb[:, 0], V("lb0", 0, KT), V("lb1", 0, KT), ALU.max), lb_step)
            then(dve.tensor_tensor(lb[:, 1], V("lb0", 0, KT), lb[:, 0], ALU.subtract), lb_step)
            then(dve.tensor_tensor(lb[:, 2], V("lb1", 0, KT), lb[:, 0], ALU.subtract), lb_step)
            dve.wait_ge(silu_c_done, 1)

            def norm(n, gain, shift=None):
                c = NORM_COLS[n]
                w = c.stop - c.start
                dve.wait_ge(sqrt_done, n + 1)
                dve.reciprocal(rstd[:, 0:w], rstd[:, 0:w]).then_inc(rstd_done, 1)
                dve.wait_ge(rstd_done, n + 1)
                for k in range(KT):
                    ins = dve.scalar_tensor_tensor(u[:, k, 0:w], h[:, k, c], gain(k), rstd[:, 0:w], ALU.mult, ALU.mult)
                    ins.then_inc(u_done if shift is None else u_scaled, 1)
                if shift is not None:
                    for k in range(KT):
                        dve.wait_ge(u_scaled, KT * (n - 3) + k + 1)
                        dve.tensor_scalar(u[:, k, 0:w], u[:, k, 0:w], shift(k), None, ALU.add).then_inc(u_done, 1)

            def ada_add(n, kt, q):
                dve.wait_ge(ada_in[q], kt * 16 + 16)
                if isinstance(n, int) and n < ADA_Q:
                    dve.tensor_scalar(ada_acc[:, q, :], ada_ring[:, q, :], silu_c[:, 0:1], None, ALU.mult
                                      ).then_inc(ada_step, 1)
                else:
                    dve.wait_ge(ada_step, n - (ADA_Q - 1))
                    dve.scalar_tensor_tensor(ada_acc[:, q, :], ada_ring[:, q, :], silu_c[:, bass.ds(kt, 1)],
                                             ada_acc[:, q, :], ALU.mult, ALU.add).then_inc(ada_step, 1)

            def ffn(k):
                base = BASE["ffn2" if k else "ffn1"]
                w = SEQ if k else T

                def body(piece, slot):
                    f = piece - (base - FT * k)
                    dve.wait_ge(silu_done, f + 1)
                    dve.wait_ge(used, piece + 1)
                    dve.tensor_tensor(glu[:, bass.ds(piece - base, 1), 0:w].rearrange("p o t -> p (o t)"),
                                      act_g[:, slot, 0:w], ps[:, 2 * slot + 1, 0:w], ALU.mult).then_inc(glu_done, 1)

                if k:
                    each_piece(dve, base, FT, body)
                else:
                    def turn(i):
                        for slot in range(RING):
                            body(i * RING + slot, slot)
                            ada_add(i * RING + slot, i, slot)

                    turn(0)
                    with dve.Fori(1, FT // RING) as i:
                        turn(i)
                    for slot in range(FT % RING):
                        body(FT // RING * RING + slot, slot)
                        ada_add(FT // RING * RING + slot, FT // RING, slot)
                dve.wait_ge(down_mm, k + 1)
                c = slice(0, T) if k == 0 else xc
                for m in range(KT):
                    dve.scalar_tensor_tensor(h[:, m, c], ps[:, m, 0:w], 0.5, h[:, m, c], ALU.mult, ALU.add
                                             ).then_inc(h_done, 1)

            norm(0, lambda k: V("g_ffn1", k))
            ffn(0)
            norm(1, lambda k: V("g_mix", k))
            for n in range(FT, KT * ADA_Q):
                ada_add(n, n // ADA_Q, n % ADA_Q)

            dve.wait_ge(msqrt_done, 1)
            dve.reciprocal(m_rstd[:, 0:2, :], m_rstd[:, 0:2, :]).then_inc(mrec_done, 1)
            dve.wait_ge(mrec_done, 1)
            for k in range(2):
                dve.scalar_tensor_tensor(cqn[:, k, :], praw[:, k, xc], V("g_cq", k), m_rstd[:, 0, xc], ALU.mult, ALU.mult
                                         ).then_inc(lat_done, 1)
            dve.scalar_tensor_tensor(ckvn, praw[:, 2, :], V("g_ckv"), m_rstd[:, 1, :], ALU.mult, ALU.mult
                                     ).then_inc(lat_done, 1)
            fr = slice(FL_ROW, FL_ROW + HEADS)
            dve.wait_ge(proj_ev, 4)
            then(dve.tensor_scalar(logf[fr, 1, :], praw[fr, 3, :], V("b_f")[fr], None, ALU.add), z_done)
            then(dve.tensor_scalar(logf[fr, 0, :], logf[fr, 1, :], 0.0, None, ALU.min), z_done)
            then(dve.scalar_tensor_tensor(logf[fr, 1, :], logf[fr, 0, :], -2.0, logf[fr, 1, :], ALU.mult, ALU.add), z_done)
            dve.tensor_copy(km[PE_ROW:PE_ROW + ROPE, :, :],
                            praw[PE_ROW:PE_ROW + ROPE, 3:4, :].broadcast_to([ROPE, HEADS, T])).then_inc(kpe_done, 1)
            then(dve.memset(fqz[:, :, :], 0.0), lb_step)
            then(dve.memset(cumz, 0.0), lb_step)
            for b in range(2):
                dve.wait_ge(msqrt_done, b + 2)
                dve.reciprocal(m_rstd[:, :, :], m_rstd[:, :, :]).then_inc(mrec_done, 1)
                dve.wait_ge(mrec_done, b + 2)
                for j in range(4):
                    if b == 0:
                        for e in range(2):
                            r = slice(HD * e, HD * e + HD)
                            dve.scalar_tensor_tensor(fqz[r, 2 * j + e, :], praw[r, 4 + j, xc], V("g_fq")[r],
                                                     m_rstd[r, j, xc], ALU.mult, ALU.mult).then_inc(fox_done, 1)
                    else:
                        dve.scalar_tensor_tensor(fk[:, j, :], praw[:, 8 + j, :], V("g_fk"), m_rstd[:, j, :],
                                                 ALU.mult, ALU.mult).then_inc(fox_done, 1)
            dve.wait_ge(f_ln, 1)
            then(dve.tensor_tensor(logf[fr, 3, :], logf[fr, 0, :], logf[fr, 2, :], ALU.subtract), cum_done)
            then(dve.tensor_tensor_scan(cumz[fr, :], C("ones")[fr, 0:1].broadcast_to([HEADS, T]), logf[fr, 3, :], 0.0,
                                        ALU.mult, ALU.add), cum_done)
            dve.tensor_scalar(ncumz, cumz, -1.0, None, ALU.mult).then_inc(cum_done, 1)
            for b in range(4):
                g = 4 * (b % 2)
                w = SEQ if b < 2 else T
                x = (qm if b < 2 else km)[0:QK, g:g + 4, :]
                r = mrs[0:QK, :, 0:w]
                c = slice(T - w, T)
                dve.wait_ge(hsqrt, b + 1)
                dve.reciprocal(r, r).then_inc(hrec, 1)
                dve.wait_ge(hrec, 5 * b + 1)
                for i in range(4):
                    dve.scalar_tensor_tensor(x[:, i, :], x[:, i, :], V("g_q" if b < 2 else "g_k")[0:QK], r[:, i, :],
                                             ALU.mult, ALU.mult).then_inc(hrec, 1)
                dve.wait_ge(hrec, 5 * b + 5)
                dve.tensor_copy(lb[0:1, 5, 0:1], eps[0:1, :]).then_inc(hn_done, 1)
                dve.wait_ge(rot_mm, b + 1)
                dve.tensor_tensor(r, ps[0:QK, g:g + 4, 0:w], C("sin")[0:QK, None, c].broadcast_to([QK, 4, w]), ALU.mult
                                  ).then_inc(rope_step, 1)
                dve.tensor_tensor(x, x, C("cos")[0:QK, None, c].broadcast_to([QK, 4, w]), ALU.mult).then_inc(rope_step, 1)
                dve.wait_ge(rope_step, 3 * b + 2)
                dve.tensor_tensor(x, x, r, ALU.add).then_inc(rope_step, 1)

            def soft_max(n):
                hd, t = divmod(n, TT)
                keys_n = X0 + P * (t + 1)
                dve.wait_ge(s_mm, n + 1)
                dve.reduce_max(mx[:, n:n + 1], ps[:, n % 3, 0:keys_n], AX_X).then_inc(max_done, 1)
                dve.wait_ge(max_done, n + 1)
                dve.tensor_scalar(nmx[:, n:n + 1], mx[:, n:n + 1], -(MLA_SCALE if hd < HEADS else FOX_SCALE), None,
                                  ALU.mult).then_inc(nmax_done, 1)

            def scale_p(n):
                t = n % TT
                keys_n = X0 + P * (t + 1)
                dve.wait_ge(exp_done, n + 1)
                dve.reciprocal(rinv[:, n:n + 1], rsum[:, n:n + 1]).then_inc(rinv_done, 1)
                dve.wait_ge(rinv_done, n + 1)
                dve.tensor_scalar(probs[:, n % 4, 0:keys_n], probs[:, n % 4, 0:keys_n], rinv[:, n:n + 1], None, ALU.mult
                                  ).then_inc(p_done, 1)

            units = 2 * HEADS * TT
            soft_max(0)
            for n in range(units):
                if n + 1 < units:
                    soft_max(n + 1)
                scale_p(n)
            for m in range(KT):
                dve.wait_ge(wo_mm, m + 1)
                dve.tensor_tensor(h[:, m, xc], h[:, m, xc], ps[:, m, 0:SEQ], ALU.add).then_inc(h_done, 1)
            dve.wait_ge(ada_mm, 1)
            then(dve.tensor_tensor(ada[:, :], ps[:, 7, 256:304], V("ada_b", 0, 48), ALU.add), ada_done)
            then(dve.scalar_tensor_tensor(gain1[:, :], ada[:, 8:16], 1.0, V("norm1", 0, KT), ALU.add, ALU.mult), ada_done)
            then(dve.scalar_tensor_tensor(gain2[:, :], ada[:, 32:40], 1.0, V("norm2", 0, KT), ALU.add, ALU.mult), ada_done)
            norm(2, lambda k: V("g_ffn2", k))
            ffn(1)
            norm(3, lambda k: gain1[:, k:k + 1], lambda k: ada[:, k:k + 1])

            dve.wait_ge(lb_e, 2)
            then(dve.tensor_tensor(lb[:, 3], lb[:, 1], lb[:, 2], ALU.add), lb_step)
            then(dve.reciprocal(lb[:, 4], lb[:, 3]), lb_step)
            then(dve.tensor_tensor(lb[:, 0], lb[:, 1], lb[:, 4], ALU.mult), lb_step)
            then(dve.tensor_scalar(lb[:, 1], lb[:, 0], -1.0, 1.0, ALU.mult, ALU.add), lb_step)
            then(dve.memset(pad_glu[:, :, 0:PAD], 0.0), lb_step)
            dve.wait_ge(sig_done, 1)
            then(dve.tensor_tensor(pad_glu[:, :, PAD:PAD + SEQ], z[:, 0], z[:, 1], ALU.mult), dve2)
            cv = z[:, 0]
            for m in range(KT):
                dve.tensor_scalar(cv[:, m, :], pad_glu[:, m, 0:SEQ], V("conv_w", m), V("conv_b", m), ALU.mult, ALU.add
                                  ).then_inc(conv_step, 1)
            with dve.Fori(1, CONV_K) as tap:
                for m in range(KT):
                    dve.wait_ge(conv_step, tap * KT + (m + 1 - KT))
                    dve.scalar_tensor_tensor(cv[:, m, :], pad_glu[:, m, bass.ds(tap, SEQ)],
                                             cols[:, bass.ds(tap * KT + (COL["conv_w"] + m), 1)], cv[:, m, :],
                                             ALU.mult, ALU.add).then_inc(conv_step, 1)
            dve.wait_ge(conv_step, CONV_K * KT)
            dve.tensor_copy(lb[0:1, 5, 0:1], eps[0:1, :]).then_inc(dve2, 1)
            dve.wait_ge(ln_mm, 1)
            steps[dve2.name] = 2
            mean = ps[:, 0, None, 0:SEQ].broadcast_to([P, KT, SEQ])
            then(dve.tensor_tensor(cv, cv, mean, ALU.subtract), dve2)
            dve.wait_ge(ln_act, 2)
            then(dve.reciprocal(rstd[:, 0:SEQ], rstd[:, 0:SEQ]), dve2)
            then(dve.tensor_tensor(cv, cv, rstd[:, None, 0:SEQ].broadcast_to([P, KT, SEQ]), ALU.mult), dve2)
            pre, key, q = z[:, 2], z[:, 1], z[:, 3]
            dve.wait_ge(sig_done, 5)
            for m in range(KT):
                ins = dve.tensor_scalar(pre[:, m, :], pre[:, m, :], lb[:, 1, m:m + 1], lb[:, 0, m:m + 1], ALU.mult, ALU.add)
                ins.then_inc(lev_up, 1)
            dve.wait_ge(lev_up, KT)
            steps[lev_up.name] = KT
            then(dve.tensor_scalar(key, pre, -1.0, 1.0, ALU.mult, ALU.add), lev_up)
            then(dve.memset(suf[:, :, :], 1.0), lev_up)
            then(dve.memset(AT[:, :, :, :], 0.0), lev_up)

            def blocks(x, b, e):
                v = x.rearrange("p h t -> p (h t)").rearrange("p (n e b) -> p n e b", e=2, b=b)
                return v[:, :, e, :]

            def last(x, b, e, n):
                v = x.rearrange("p h t -> p (h t)").rearrange("p (n e b) -> p n e b", e=2, b=b)
                return v[:, :, e, b - 1:b].broadcast_to([P, n, b])

            def level_in(n, b):
                buf = n % 2
                if n >= 3:
                    dve.wait_ge(lev_mm, n - 2)
                if n <= 2:
                    dve.tensor_tensor(qt[buf], q, pre, ALU.mult).then_inc(lev_in, 1)
                    dve.tensor_tensor(kt_[:, buf], key, suf[:, :, :], ALU.mult).then_inc(lev_in, 1)
                else:
                    dve.tensor_tensor(blocks(qt[buf], b, 1), blocks(q, b, 1), blocks(pre, b, 1), ALU.mult).then_inc(lev_in, 1)
                    dve.tensor_tensor(blocks(kt_[:, buf], b, 0), blocks(key, b, 0), blocks(suf[:, :, :], b, 0), ALU.mult
                                      ).then_inc(lev_in, 1)
                if b < P:
                    dve.wait_ge(lev_in, 2 * n)
                    nb = KT * SEQ // (2 * b)
                    then(dve.tensor_tensor(blocks(suf[:, :, :], b, 0), blocks(suf[:, :, :], b, 0), last(pre, b, 1, nb),
                                           ALU.mult), lev_up)
                    then(dve.tensor_tensor(blocks(pre, b, 1), blocks(pre, b, 1), last(pre, b, 0, nb), ALU.mult), lev_up)

            def level_out(n):
                dve.wait_ge(lev_mm, n + 1)
                if n:
                    dve.wait_ge(lev_out, 2 * n)
                else:
                    dve.wait_ge(mask_in, 16)
                if n <= 7:
                    m = masks[:, n * P:(n + 1) * P]
                    src = ps[:, 4 * (n % 2):4 * (n % 2) + 4, :].rearrange("p b (h t) -> p (b h) t", t=P)
                    for half in range(2):
                        dve.copy_predicated(AT[:, :, half, :], m[:, None, :].broadcast_to([P, HEADS, P]),
                                            src[:, half::2, :]).then_inc(lev_out, 1)
                else:
                    src = ps[:, 0:2, :].rearrange("p b (h t) -> p (b h) t", t=P)
                    dve.tensor_copy(AT[:, :, 2, :], src).then_inc(lev_out, 1)

            levels = LEVELS + [P]
            for n in range(1, len(levels)):
                level_in(n, levels[n])
                level_out(n - 1)
            level_out(len(levels) - 1)
            on = kt_[:, 0]
            dve.wait_ge(on_act, 1)
            then(dve.reciprocal(on, on), lev_up)
            for m in range(KT):
                then_ = dve.scalar_tensor_tensor(o_h[:, m, :], o_h[:, m, :], V("hg_g", m), on[:, m, :], ALU.mult, ALU.mult)
                then_.then_inc(lev_up, 1)
            steps[lev_up.name] += KT
            dve.wait_ge(lev_up, steps[lev_up.name])
            dve.tensor_tensor(o_h, o_h, z[:, 4], ALU.mult).then_inc(dve2, 1)
            for m in range(KT):
                dve.wait_ge(dense_mm, m + 1)
                dve.tensor_tensor(z[:, 5, m, :], z[:, 5, m, :], ps[:, m, 0:SEQ], ALU.mult).then_inc(dense_ev, 1)
            for m in range(KT):
                dve.wait_ge(dense_mm, KT + m + 1)
                dve.tensor_tensor(z[:, 6, m, :], z[:, 6, m, :], ps[:, m, 0:SEQ], ALU.mult).then_inc(dense_ev, 1)
            dve.wait_ge(dense_ev, 2 * KT)
            dve.tensor_tensor(z[:, 5], z[:, 5], z[:, 6], ALU.add).then_inc(dve2, 1)
            for m in range(KT):
                dve.wait_ge(dense_mm, 2 * KT + m + 1)
                dve.scalar_tensor_tensor(h[:, m, xc], ps[:, m, 0:SEQ], ada[:, 16 + m:17 + m], h[:, m, xc], ALU.mult, ALU.add
                                         ).then_inc(h_done, 1)
            norm(4, lambda k: gain2[:, k:k + 1], lambda k: ada[:, 24 + k:25 + k])

            def top16(vals, idxs, src, scratch, n):
                then(dve.max(vals[:, 0:8], src), tk)
                then(dve.max_index(top_u[:, 0, :], vals[:, 0:8], src), tk)
                then(dve.match_replace(scratch, vals[:, 0:8], src, -3.0e38), tk)
                then(dve.max(vals[:, 8:16], scratch), tk)
                then(dve.max_index(top_u[:, 1, :], vals[:, 8:16], scratch), tk)
                then(dve.tensor_copy(idxs, top_u[:, 0:2, :].rearrange("p a b -> p (a b)")), tk)

            for t in range(TT):
                dve.wait_ge(sc_ev, 4 * (t + 1))
                for n in range(2 * HEADS):
                    top16(top[:, t, n, :], top_i[:, t, n, :], scores[:, t, n, :], work[:, 0:NKEYS], n)
                even = top[:, t].rearrange("p (h e) k -> p h e k", e=2)
                even_i = top_i[:, t].rearrange("p (h e) k -> p h e k", e=2)
                then(dve.tensor_tensor(cand.rearrange("p h (i j) -> p h i j", i=TOPK),
                                       even[:, :, 0, :, None].broadcast_to([P, HEADS, TOPK, TOPK]),
                                       even[:, :, 1, None, :].broadcast_to([P, HEADS, TOPK, TOPK]), ALU.add), tk)
                for n in range(HEADS):
                    then(dve.max(best[:, t, n, 0:8], cand[:, n, :]), tk)
                    then(dve.max_index(pos_u[:, n, 0:8], best[:, t, n, 0:8], cand[:, n, :]), tk)
                    then(dve.match_replace(work, best[:, t, n, 0:8], cand[:, n, :], -3.0e38), tk)
                    then(dve.max(best[:, t, n, 8:16], work), tk)
                    then(dve.max_index(pos_u[:, n, 8:16], best[:, t, n, 8:16], work), tk)
                dve.tensor_tensor(gate[:, t], best[:, t], best[:, t, :, 0:1].broadcast_to([P, HEADS, TOPK]), ALU.subtract
                                  ).then_inc(gate_e, 1)
                then(dve.tensor_scalar(hi_u[:, :, :], pos_u[:, :, :], 4, None, ALU.logical_shift_right), tk)
                then(dve.tensor_copy(pos_hi, hi_u[:, :, :]), tk)
                then(dve.tensor_scalar(hi_u[:, :, :], pos_u[:, :, :], TOPK - 1, None, ALU.bitwise_and), tk)
                then(dve.tensor_copy(pos_f, hi_u[:, :, :]), tk)
                iota = C("iota")[:, None, None, :].broadcast_to([P, HEADS, TOPK, TOPK])
                for e, where in ((0, pos_hi), (1, pos_f)):
                    then(dve.tensor_tensor(onehot, where[:, :, :, None].broadcast_to([P, HEADS, TOPK, TOPK]), iota,
                                           ALU.is_equal), tk)
                    then(dve.tensor_tensor(onehot, onehot,
                                           even_i[:, :, e, None, :].broadcast_to([P, HEADS, TOPK, TOPK]), ALU.mult), tk)
                    then(dve.reduce_sum(part_i[:, e], onehot, AX_X), tk)
                then(dve.scalar_tensor_tensor(part_i[:, 0], part_i[:, 0], float(NKEYS), part_i[:, 1], ALU.mult, ALU.add), tk)
                dve.tensor_copy(eidx[:, t, :], part_i[:, 0].rearrange("p h k -> p (h k)")).then_inc(idx_done, 1)
                dve.wait_ge(fin_act, t + 1)
                then(dve.reduce_sum(gate_s[:, t], gate[:, t], AX_X), tk)
                then(dve.reciprocal(gate_s[:, t], gate_s[:, t]), tk)
                dve.tensor_tensor(gate[:, t], gate[:, t], gate_s[:, t, :, None].broadcast_to([P, HEADS, TOPK]), ALU.mult
                                  ).then_inc(gate_e, 1)

            dve.wait_ge(tok_ev, 8)
            n0 = 0
            for t in range(TT):
                with dve.Fori(0, SLOTS // GR) as i:
                    for par in range(2):
                        n = i * 2 + (n0 + par)
                        turn = i + n0 // 2
                        for j in range(8):
                            r = par * 8 + j
                            dve.wait_ge(row_in[r], turn * 16 + 16)
                            dve.tensor_tensor_reduce(rows[r], rows[r], hf[:, t, :], 1.0, 0.0, ALU.mult, ALU.add,
                                                     dot8[:, par, j:j + 1]).then_inc(row_used, 1)
                        dve.wait_ge(row_used, n * 8 + 8)
                        dve.tensor_copy(dots[:, t, bass.ds(i * GR + par * 8, 8)], dot8[:, par, :]).then_inc(dot_out, 1)
                n0 += SLOTS // 8
            for t in range(TT):
                dve.memset(acc[:, t, :], 0.0).then_inc(w_done, 1)
            for t in range(TT):
                dve.wait_ge(gelu_done, t + 1)
                dve.wait_ge(gate_e, 2 * TT)
                dve.tensor_tensor(wts[:, t, :], dots[:, t, :], gate[:, t].rearrange("p h k -> p (h k)"), ALU.mult
                                  ).then_inc(w_done, 1)
            dve.wait_ge(w_done, 2 * TT)
            for t in range(TT):
                with dve.Fori(0, SLOTS // GR) as i:
                    for r in range(GR):
                        turn = i + n0 // 2
                        dve.wait_ge(row_in[r], turn * 16 + 16)
                        dve.wait_ge(row_used, i * GR + (n0 * 8 + r))
                        dve.scalar_tensor_tensor(acc[:, t, :], rows[r], wts[:, t, bass.ds(i * GR + r, 1)],
                                                 acc[:, t, :], ALU.mult, ALU.add).then_inc(row_used, 1)
                n0 += SLOTS // 8
                dve.wait_ge(row_used, n0 * 8)
                if t == 0:
                    dve.wait_ge(tok_ev, 10)
                    dve.wait_ge(final_in, 16)
                then(dve.tensor_tensor(acc[:, t, :], acc[:, t, :], y_gain, ALU.mult), fin_step)
                then(dve.tensor_tensor(acc[:, t, :], acc[:, t, :], h_tok[:, t, :], ALU.add), fin_step)
                then(dve.tensor_tensor_reduce(junk, acc[:, t, :], acc[:, t, :], 1.0, 0.0, ALU.mult, ALU.add,
                                              fin[:, 2 * t:2 * t + 1]), fin_step)
                dve.wait_ge(fin_act, TT + t + 1)
                then(dve.reciprocal(fin[:, 8 + t:9 + t], fin[:, 2 * t + 1:2 * t + 2]), fin_step)
                then(dve.tensor_scalar(acc[:, t, :], acc[:, t, :], fin[:, 8 + t:9 + t], None, ALU.mult), fin_step)
                then(dve.tensor_tensor(acc[:, t, :], acc[:, t, :], final_g[:, :], ALU.mult), fin_step)

        @block.tensor
        def _(pe):
            def arrived(piece, slot):
                turn = piece // RING if isinstance(piece, int) else None
                if turn is not None:
                    pe.wait_ge(landed[slot], 16 * turn + 16)
                return turn

            def each(base, n, body, peel=0):
                for at, turns in runs(base, n, peel):
                    if not turns:
                        pe.wait_ge(landed[at % RING], at // RING * 16 + 16)
                        body(at, at % RING).then_inc(used, 1)
                        continue
                    with pe.Fori(0, turns) as i:
                        for slot in range(RING):
                            pe.wait_ge(landed[slot], i * 16 + (at // RING * 16 + 16))
                            body(i * RING + (at + slot), slot).then_inc(used, 1)

            def blk(slot, b):
                return ring[:, slot, b * P:(b + 1) * P]

            def norm(n):
                w = NORM_COLS[n].stop - NORM_COLS[n].start
                pe.wait_ge(sq_done, n + 1)
                src = sq if n < 3 else sq2
                for k in range(KT):
                    mm = pe.matmul(ps[:, 7, 0:w], C("mean_d"), src[:, k, 0:w], start=(k == 0), stop=(k == KT - 1))
                mm.then_inc(ss_done, 1)

            def ffn(k):
                base = BASE["ffn2" if k else "ffn1"]
                w = SEQ if k else T
                pe.wait_ge(u_done, KT * (2 * k + 1))

                def up(piece, slot):
                    f = piece - (base - FT * k)
                    if not (k == 0 and isinstance(piece, int) and piece < RING):
                        pe.wait_ge(glu_done, f - (RING - 1))
                    for e in range(2):
                        for b in range(KT):
                            mm = pe.matmul(ps[:, 2 * slot + e, 0:w], blk(slot, e * KT + b), u[:, b, 0:w],
                                           start=(b == 0), stop=(b == KT - 1))
                        if e == 0:
                            mm.then_inc(gate_mm, 1)
                    return mm

                each(base, FT, up, peel=0 if k else RING)
                pe.wait_ge(glu_done, FT * (k + 1))

                def down(piece, slot):
                    f = (piece - (base + FT)) * 2
                    for e in range(2):
                        for m in range(KT):
                            first = isinstance(f, int) and f + e == 0
                            final = isinstance(f, int) and f + e == FT - 1
                            mm = pe.matmul(ps[:, m, 0:w], blk(slot, e * KT + m),
                                           glu[:, bass.ds(f + e, 1), 0:w].rearrange("p o t -> p (o t)"),
                                           start=first, stop=final)
                    return mm

                each(base + FT, FFN_P - FT - 1, down, peel=1)
                last = base + FFN_P - 1
                pe.wait_ge(landed[last % RING], last // RING * 16 + 16)
                down(last, last % RING).then_inc(down_mm, 1)
                pe.wait_ge(down_mm, k + 1)
                pe.sem_inc(used, 1)

            def dense(name, rhs, done):
                def body(piece, slot):
                    for e in range(2):
                        m = (piece - BASE[name]) * 2 + e
                        for b in range(KT):
                            mm = pe.matmul(ps[:, m, 0:SEQ], blk(slot, e * KT + b), rhs[:, b, 0:SEQ],
                                           start=(b == 0), stop=(b == KT - 1))
                        if e == 0:
                            mm.then_inc(done, 1)
                    return mm

                for piece in range(BASE[name], BASE[name] + 4):
                    pe.wait_ge(landed[piece % RING], piece // RING * 16 + 16)
                    body(piece, piece % RING).then_inc(done, 1)
                    pe.wait_ge(done, done_count(done, 2))
                    pe.sem_inc(used, 1)

            counts = {}

            def done_count(s, n):
                counts[s.name] = counts.get(s.name, 0) + n
                return counts[s.name]

            pe.wait_ge(con_in, 16)
            norm(0)
            ffn(0)
            norm(1)
            pe.wait_ge(u_done, 2 * KT)
            for p in range(6):
                piece = BASE["w_in"] + p
                slot = piece % RING
                pe.wait_ge(landed[slot], piece // RING * 16 + 16)
                for e in range(2):
                    i = 2 * p + e
                    if i >= 8:
                        pe.wait_ge(proj_ev, i - 7)
                    for b in range(KT):
                        mm = pe.matmul(ps[:, i % 8, 0:T], blk(slot, e * KT + b), u[:, b, :], start=(b == 0), stop=(b == KT - 1))
                    mm.then_inc(proj_mm, 1)
                pe.wait_ge(proj_mm, 2 * p + 2)
                pe.sem_inc(used, 1)
            pe.wait_ge(proj_ev, 8)
            for p in range(2):
                piece = BASE["w_in"] + 6 + p
                slot = piece % RING
                pe.wait_ge(landed[slot], piece // RING * 16 + 16)
                for b in range(4):
                    k = p * 4 + b
                    for t in range(3):
                        n = P if t < 2 else N_META
                        mm = pe.matmul(ps[0:n, 4 + t, :], u[:, k, t * P:t * P + n], ring[:, slot, b * 512:(b + 1) * 512],
                                       start=(k == 0), stop=(k == KT - 1))
                if p == 0:
                    mm.then_inc(used, 1)
                else:
                    mm.then_inc(fv_mm, 1)
                    pe.wait_ge(fv_mm, 1)
                    pe.sem_inc(used, 1)
            pe.wait_ge(proj_ev, 12)
            pe.wait_ge(msq_done, 1)
            for k in range(2):
                pe.matmul(ps[:, 0, 0:T], C("mean_256"), sq[:, k, :], start=(k == 0), stop=(k == 1))
            for b in range(1, 4):
                mm = pe.matmul(ps[:, b, 0:T], C("mean_128"), sq[:, 2, :], start=True, stop=True)
            mm.then_inc(mss_done, 1)
            pe.wait_ge(msq_done, 2)
            pe.wait_ge(fv_ev, 3)
            pe.wait_ge(msqrt_done, 1)
            for g in range(2):
                for j in range(4):
                    mm = pe.matmul(ps[:, 4 - 4 * g + j, 0:T], C("mean_64"), sq[:, 4 * g + j, :], start=True, stop=True)
                mm.then_inc(mss_done, 1)
            pe.wait_ge(small_in, 16 * 5)
            pe.wait_ge(lat_done, 3)
            pe.wait_ge(msqrt_done, 3)
            for b in range(4):
                if b >= 2:
                    pe.wait_ge(raw_ev, b - 1)
                for i in range(4):
                    hd = 4 * (b % 2) + i
                    if b < 2:
                        for k in range(2):
                            mm = pe.matmul(ps[0:QK, hd, 0:SEQ], wuq[:, k, hd * QK:(hd + 1) * QK], cqn[:, k, :],
                                           start=(k == 0), stop=(k == 1))
                    else:
                        mm = pe.matmul(ps[0:NOPE, hd, 0:T], wuk[:, hd * NOPE:(hd + 1) * NOPE], ckvn, start=True, stop=True)
                mm.then_inc(raw_mm, 1)
            pe.wait_ge(raw_ev, 3)
            for t in range(3):
                n = P if t < 2 else N_META
                mm = pe.matmul(ps[0:n, t, :], ckvn[:, t * P:t * P + n], wuv, start=True, stop=True)
            mm.then_inc(vm_mm, 1)
            pe.wait_ge(raw_ev, 4)
            pe.wait_ge(vm_ev, 3)

            def head_ss(b):
                g = 4 * (b % 2)
                w = SEQ if b < 2 else T
                pe.wait_ge(hsq_done, b + 1)
                if b >= 2:
                    pe.wait_ge(rope_step, 3 * (b - 2) + 1)
                for i in range(4):
                    mm = pe.matmul(ps[0:QK, g + i, 0:w], C("mean_96")[0:QK, 0:QK], msq[0:QK, i, 0:w], start=True, stop=True)
                mm.then_inc(hss_mm, 1)

            for b in range(4):
                head_ss(b)
                g = 4 * (b % 2)
                w = SEQ if b < 2 else T
                src = qm if b < 2 else km
                pe.wait_ge(hn_done, b + 1)
                for i in range(4):
                    mm = pe.matmul(ps[0:QK, g + i, 0:w], C("rot")[0:QK, 0:QK], src[0:QK, g + i, :], start=True, stop=True)
                mm.then_inc(rot_mm, 1)
            pe.wait_ge(rope_step, 12)
            pe.wait_ge(cum_done, 3)
            pe.wait_ge(fox_done, 12)
            units = 2 * HEADS * TT

            def scores_of(n):
                hd, t = divmod(n, TT)
                keys_n = X0 + P * (t + 1)
                q = slice(t * P, (t + 1) * P)
                dst = ps[:, n % 3, 0:keys_n]
                if n >= 3:
                    pe.wait_ge(exp_done, n - 2)
                if hd < HEADS:
                    pe.matmul(dst, qm[0:QK, hd, q], km[0:QK, hd, 0:keys_n], start=True, stop=False)
                else:
                    f = hd - HEADS
                    pe.matmul(dst, fqz[:, f, q], fk[:, f // 2, 0:keys_n], start=True, stop=False)
                    pe.matmul(dst, cumz[:, X0 + t * P:X0 + (t + 1) * P], sel[:, f, 0:keys_n], start=False, stop=False)
                    pe.matmul(dst, sel[:, f, 0:P], ncumz[:, 0:keys_n], start=False, stop=False)
                pe.matmul(ps[:, n % 3, keys_n - P:keys_n], ident, C("neg_mask"), start=False, stop=True).then_inc(s_mm, 1)

            def turn_probs(n):
                t = n % TT
                full = t + 1
                bank = 3 + n % 2
                pe.wait_ge(p_done, n + 1)
                if n >= 2:
                    pe.wait_ge(pT_ev, n - 1)
                for s in range(full):
                    pe.transpose(ps[:, bank, s * P:(s + 1) * P], probs[:, n % 4, s * P:(s + 1) * P], ident)
                pe.transpose(ps[0:N_META, bank, full * P:(full + 1) * P],
                             probs[:, n % 4, full * P:full * P + N_META], ident).then_inc(pT_mm, 1)

            def weigh(n):
                hd, t = divmod(n, TT)
                full = t + 1
                v = (vM if hd < HEADS else vF)
                pair = (hd % HEADS) // 2
                c = slice(pair * P, pair * P + P)
                pe.wait_ge(pT_ev, n + 1)
                if n >= 2:
                    pe.wait_ge(o_ev, n - 1)
                for s in range(full):
                    pe.matmul(ps[:, 5 + n % 2, 0:P], v[:, s, c], probsT[:, n % 2, s, :], start=(s == 0), stop=False)
                pe.matmul(ps[:, 5 + n % 2, 0:P], v[0:N_META, full, c], probsT[0:N_META, n % 2, full, :],
                          start=False, stop=True).then_inc(o_mm, 1)

            scores_of(0)
            scores_of(1)
            for n in range(units):
                if n + 2 < units:
                    scores_of(n + 2)
                turn_probs(n)
                if n:
                    weigh(n - 1)
            weigh(units - 1)
            pe.wait_ge(o_ev, units)
            dense("w_out", oT, wo_mm)
            pe.wait_ge(ada_step, KT * ADA_Q)
            flat = ada_acc.rearrange("p q w -> p (q w)")
            pe.wait_ge(h_done, 2 * KT)
            for m in range(48):
                mm = pe.matmul(ps[:, 7, 256 + m:257 + m], flat[:, m * P:(m + 1) * P], C("ones")[:, 0:1], start=True, stop=True)
            mm.then_inc(ada_mm, 1)
            pe.wait_ge(ada_done, 1)
            norm(2)
            ffn(1)
            norm(3)
            pe.wait_ge(u_done, 4 * KT)
            for p in range(4):
                piece = BASE["zi"] + p
                slot = piece % RING
                half = p // 2
                pe.wait_ge(landed[slot], piece // RING * 16 + 16)
                for b in range(4):
                    k = (p % 2) * 4 + b
                    for t in range(TT):
                        mm = pe.matmul(ps[:, t * 2 + half, :], u[:, k, t * P:(t + 1) * P], ring[:, slot, b * 512:(b + 1) * 512],
                                       start=(k == 0), stop=(k == KT - 1))
                if p < 3:
                    mm.then_inc(used, 1)
                else:
                    mm.then_inc(zi_mm, 1)
                    pe.wait_ge(zi_mm, 1)
                    pe.sem_inc(used, 1)
            pe.wait_ge(zi_ev, 4)

            def z_seg(piece, slot, pair, n, first):
                for e in range(2):
                    m = 2 * pair + e
                    if not first:
                        pe.wait_ge(z_ev, n * KT + (m + 1 - KT))
                    for b in range(KT):
                        mm = pe.matmul(ps[:, m, 0:SEQ], blk(slot, e * KT + b), u[:, b, 0:SEQ], start=(b == 0), stop=(b == KT - 1))
                    mm.then_inc(z_mm, 1)
                return m

            zb = BASE["z"]
            def z_turn(n, first):
                for pair in range(4):
                    slot = (zb + pair) % RING
                    turn0 = (zb + pair) // RING
                    pe.wait_ge(landed[slot], n * 16 + (turn0 * 16 + 16))
                    z_seg(None, slot, pair, n, first)
                    pe.wait_ge(z_mm, n * KT + (2 * pair + 2))
                    pe.sem_inc(used, 1)

            z_turn(0, True)
            with pe.Fori(1, 7) as n:
                z_turn(n, False)
            pe.wait_ge(z_ev, 7 * KT)
            pe.wait_ge(dve2, 2)
            for m in range(KT):
                mm = pe.matmul(ps[:, 0, 0:SEQ], C("mean_d"), z[:, 0, m, :], start=(m == 0), stop=(m == KT - 1))
            mm.then_inc(ln_mm, 1)
            pe.wait_ge(ln_act, 1)
            for m in range(KT):
                mm = pe.matmul(ps[:, 1, 0:SEQ], C("mean_d"), sq2[:, m, :], start=(m == 0), stop=(m == KT - 1))
            mm.then_inc(ln_mm, 1)
            pe.wait_ge(lev_up, KT + 3)
            pe.wait_ge(ln_act, 2)
            levels = LEVELS + [P]
            for n, b in enumerate(levels):
                if n:
                    pe.wait_ge(lev_in, 2 * n)
                kk, qq = (z[:, 1], z[:, 3]) if n == 0 else (kt_[:, n % 2], qt[n % 2])
                if n >= 2:
                    pe.wait_ge(lev_out, 2 * (n - 1))
                for hd in range(HEADS):
                    if b < P:
                        for half in range(2):
                            c = slice(half * P, half * P + P)
                            at = hd * 2 + half
                            mm = pe.matmul(ps[:, 4 * (n % 2) + at // 4, at % 4 * P:at % 4 * P + P], kk[:, hd, c], qq[:, hd, c],
                                           start=True, stop=True)
                    else:
                        mm = pe.matmul(ps[:, hd // 4, hd % 4 * P:hd % 4 * P + P], kk[:, hd, 0:P], qq[:, hd, P:2 * P],
                                       start=True, stop=True)
                mm.then_inc(lev_mm, 1)
            pe.wait_ge(mask_in, 16)
            pe.wait_ge(lev_out, 2 * (len(levels) - 1) + 1)
            for hd in range(HEADS):
                c = slice(hd * P, hd * P + P)
                at = hd % 2 * SEQ
                pe.matmul(ps[:, hd // 2, at:at + P], zi[:, 0, c], AT[:, hd, 0, :], start=True, stop=True)
                pe.matmul(ps[:, hd // 2, at + P:at + 2 * P], zi[:, 0, c], AT[:, hd, 2, :], start=True, stop=False)
                mm = pe.matmul(ps[:, hd // 2, at + P:at + 2 * P], zi[:, 1, c], AT[:, hd, 1, :], start=False, stop=True)
            mm.then_inc(oh_mm, 1)
            pe.wait_ge(oh_ev, 2)
            s2 = sq2.rearrange("p h t -> p (h t)")
            for b in range(4):
                mm = pe.matmul(ps[:, 4 + b, :], C("mean_128"), s2[:, b * 512:(b + 1) * 512], start=True, stop=True)
            mm.then_inc(on_mm, 1)
            pe.wait_ge(on_act, 1)
            pe.wait_ge(dve2, 6)
            dense("w_a", o_h, dense_mm)
            pe.wait_ge(dense_ev, KT)
            pe.wait_ge(ln_act, 2 + KT)
            dense("w_b", z[:, 0], dense_mm)
            pe.wait_ge(dve2, 7)
            dense("w_out_2", z[:, 5], dense_mm)
            norm(4)
            pe.wait_ge(u_done, 5 * KT)

            def q_tiles(piece, slot):
                pair = (piece - BASE["wq"])
                for e in range(2):
                    if not isinstance(piece, int) or piece - BASE["wq"] >= RING:
                        pe.wait_ge(q_ev, pair * 2 + (e + 1 - 8))
                    for b in range(KT):
                        mm = pe.matmul(ps[:, 2 * slot + e, 0:SEQ], blk(slot, e * KT + b), u[:, b, 0:SEQ],
                                       start=(b == 0), stop=(b == KT - 1))
                    mm.then_inc(q_mm, 1)
                return mm

            for p in range(8):
                piece = BASE["wq"] + p
                pe.wait_ge(landed[piece % RING], piece // RING * 16 + 16)
                q_tiles(piece, piece % RING)
                if p < 7:
                    pe.wait_ge(q_mm, 2 * p + 2)
                    pe.sem_inc(used, 1)
            pe.wait_ge(q_ev, 16)
            for n in range(8):
                t, g = divmod(n, 4)
                for i in range(4):
                    hp = g * 4 + i
                    mm = pe.matmul(ps[:, n, i * NKEYS:(i + 1) * NKEYS], qT[:, hp, t * P:(t + 1) * P], keys[:, hp, :],
                                   start=True, stop=True)
                mm.then_inc(sc_mm, 1)
            for n in range(8):
                src, t, half = n // 4, n // 2 % 2, n % 2
                pe.wait_ge(sc_ev, n + 1)
                for i in range(4):
                    k = half * 4 + i
                    x = u[:, k, t * P:(t + 1) * P] if src == 0 else h[:, k, X0 + t * P:X0 + (t + 1) * P]
                    mm = pe.transpose(ps[:, n, i * P:(i + 1) * P], x, ident)
                mm.then_inc(tok_mm, 1)
            pe.wait_ge(tok_ev, 2)
            for k in range(KT):
                mm = pe.matmul(ps[:, k // 4, k % 4 * P:k % 4 * P + P], ada[:, 40 + k:41 + k].broadcast_to([P, P]), ident,
                               start=True, stop=True)
            mm.then_inc(gain_mm, 1)


def _blocks(w):
    k, m = w.shape
    return w.reshape(k // P, P, m // P, P).transpose(0, 2, 1, 3)


def _pieces(blocks):
    n = blocks.shape[0]
    return blocks.reshape(n // BLOCKS, BLOCKS, P, P).transpose(0, 2, 1, 3).reshape(n // BLOCKS, P, PIECE)


def _by_output(w):
    b = _blocks(w)
    return _pieces(b.transpose(1, 0, 2, 3).reshape(-1, P, P))


def _by_input(w):
    return _pieces(_blocks(w).reshape(-1, P, P))


def _wide(w):
    k, m = w.shape
    b = w.reshape(k // P, P, m // 512, 4, P).transpose(2, 0, 3, 1, 4)
    return _pieces(b.reshape(-1, P, P))


def layout(x):
    f = {k: np.asarray(v) for k, v in x.items()}

    def ffn(n):
        g, up, dn = f[f"w{n}_gate"][0], f[f"w{n}_up"][0], f[f"w{n}_down"][0]
        gu = np.stack([_blocks(g).transpose(1, 0, 2, 3), _blocks(up).transpose(1, 0, 2, 3)], 1)
        return np.concatenate([_pieces(gu.reshape(-1, P, P)), _by_input(dn)])

    w_in = f["w_in"][0]
    misc = np.zeros((D, P), np.float32)
    misc[:, PE_ROW:PE_ROW + ROPE] = w_in[:, 384:416]
    misc[:, FL_ROW:FL_ROW + HEADS] = w_in[:, 1952:1960]
    w_proj = np.concatenate([w_in[:, 0:384], misc, w_in[:, 416:416 + 1024]], 1)
    zs = np.split(f["w_in_2"][0], 8, axis=1)
    zq, zf, zi, zg, zca, zcb, zga, zgb = zs
    stream = np.concatenate(
        [ffn(1), _by_output(w_proj), _wide(w_in[:, 1440:1952]), _by_output(f["w_out"][0]), ffn(2), _wide(zi)]
        + [_by_output(w) for w in (zca, zcb, zf, zq, zg, zga, zgb)]
        + [_by_output(f[n][0]) for n in ("w_a_2", "w_b_2", "w_out_2", "peer_wq_2")])
    assert stream.shape == (N_PIECES, P, PIECE)
    ada = f["ada_w_2"][0].reshape(KT, P, ADA_Q, ADA_W).transpose(0, 2, 1, 3).reshape(KT * ADA_Q, P, ADA_W)
    cols = np.zeros((P, N_COLS), np.float32)

    def put(name, v):
        v = v.reshape(-1, P).T
        cols[:, COL[name]:COL[name] + v.shape[1]] = v

    for name, key in (("g_ffn1", "g_ffn1"), ("g_mix", "g_mix"), ("g_ffn2", "g_ffn2"), ("norm1", "norm1_g_2"),
                      ("hg_g", "hg_norm_g_2"), ("conv_b", "conv_b_2"), ("ln_g", "conv_ln_g_2"),
                      ("ln_b", "conv_ln_b_2"), ("norm2", "norm2_g_2"), ("c", "c_2"), ("ada_b", "ada_b_2"),
                      ("g_cq", "g_cq"), ("g_ckv", "g_ckv"), ("conv_w", "conv_w_2")):
        put(name, f[key])
    put("lb0", f["lb_logits_2"][0])
    put("lb1", f["lb_logits_2"][1])
    cols[0:QK, COL["g_q"]] = f["g_q_mla"][0]
    cols[0:QK, COL["g_k"]] = f["g_k_mla"][0]
    for e in range(2):
        cols[HD * e:HD * e + HD, COL["g_fq"]] = f["g_q_fox"][0]
        cols[HD * e:HD * e + HD, COL["g_fk"]] = f["g_k_fox"][0]
    cols[FL_ROW:FL_ROW + HEADS, COL["b_f"]] = f["b_forget"][0]
    wukv = f["w_ukv"][0].reshape(P, HEADS, NOPE + HD)
    con, sel, masks = constants()
    tokens = np.concatenate([f["meta_tokens"], f["x"][0]], 0)
    return {
        "x_t": tokens.T.reshape(KT, P, T).transpose(1, 0, 2),
        "stream": stream, "ada": ada, "cols": cols, "con": con, "sel": sel, "masks": masks,
        "wuq": f["w_uq"][0].reshape(2, P, HEADS * QK).transpose(1, 0, 2),
        "wuk": wukv[:, :, :NOPE].reshape(P, HEADS * NOPE),
        "wuv": wukv[:, :, NOPE:].reshape(P, HEADS * HD),
        "keys": f["peer_keys_2"][0].reshape(2 * HEADS, NKEYS, P).transpose(2, 0, 1),
        "peer_u": f["peer_u_2"][0], "peer_v": f["peer_v_2"][0], "final_g": f["final_g_2"],
    }


def kernel(**inputs):
    import concourse.bacc as bacc
    from concourse.bass_utils import run_bass_kernel_spmd

    nc = bacc.Bacc("TRN2", target_bir_lowering=False, num_devices=1)
    arrays = {f"in_{k}": np.ascontiguousarray(v) for k, v in layout(inputs).items()}
    args = {k[3:]: nc.dram_tensor(k, v.shape, mybir.dt.from_np(v.dtype), kind="ExternalInput").ap()
            for k, v in arrays.items()}
    out = nc.dram_tensor("out", (1, SEQ, D), F32, kind="ExternalOutput").ap()
    program(nc, args, out)
    r = run_bass_kernel_spmd(nc, [arrays], core_ids=[0])
    return r.results[0]["out"]
```

```python
from contextlib import ExitStack

import numpy as np

import concourse.bass as bass
from concourse import mybir

F32 = mybir.dt.float32
U32 = mybir.dt.uint32
I32 = mybir.dt.int32
ACT = mybir.ActivationFunctionType
ALU = mybir.AluOpType
AX_X = mybir.AxisListType.X

P = 128
D = 1024
KT = D // P
SEQ = 256
N_META = 16
T = N_META + SEQ
X0 = N_META
TT = SEQ // P
D_FF = 2816
FT = D_FF // P
EPS = 1e-6
HEADS = 8
QK = 96
NOPE = 64
ROPE = 32
HD = 64
PE_ROW = 64
FL_ROW = 96
CONV_K = 31
PAD = CONV_K - 1
TOPK = 16
NKEYS = 128
SLOTS = HEADS * TOPK
RING = 4
BLOCKS = 16
PIECE = BLOCKS * P
ADA_Q = 4
ADA_W = 6 * D // ADA_Q
GR = 16
CHOOSE_STEPS = 43
FOX_SCALE = HD ** -0.5
MLA_SCALE = QK ** -0.5
NEG = -1e30

FFN_P = FT + FT * KT // BLOCKS
PARTS = [("ffn1", FFN_P), ("w_in", 8), ("w_out", 4), ("ffn2", FFN_P), ("z", 16), ("zi", 4), ("z_gate", 12),
         ("w_b", 4), ("w_a", 4), ("w_out_2", 4), ("wq", 8)]
BASE = {}
_at = 0
for _name, _n in PARTS:
    BASE[_name] = _at
    _at += _n
N_PIECES = _at

VECS = [("g_ffn1", 8), ("g_mix", 8), ("g_ffn2", 8), ("norm1", 8), ("lb0", 8), ("lb1", 8), ("hg_g", 8),
        ("conv_b", 8), ("ln_g", 8), ("ln_b", 8), ("norm2", 8), ("c", 8), ("ada_b", 48), ("g_cq", 2),
        ("g_ckv", 1), ("g_q", 1), ("g_k", 1), ("g_fq", 1), ("g_fk", 1), ("b_f", 1), ("conv_w", 8 * CONV_K)]
COL = {}
_at = 0
for _name, _n in VECS:
    COL[_name] = _at
    _at += _n
N_COLS = _at

CONSTS = [("ident", P), ("mean_d", P), ("mean_256", P), ("mean_128", P), ("mean_64", P), ("mean_96", P),
          ("ones", P), ("rot", P), ("cos", T), ("sin", T), ("neg_mask", P), ("iota", TOPK)]
CON = {}
_at = 0
for _name, _n in CONSTS:
    CON[_name] = (_at, _n)
    _at += _n
N_CONSTS = _at
LEVELS = [1, 2, 4, 8, 16, 32, 64, P]


def constants():
    c = np.zeros((P, N_CONSTS), np.float32)

    def put(name, a):
        at = CON[name][0]
        c[:a.shape[0], at:at + a.shape[1]] = a

    put("ident", np.eye(P, dtype=np.float32))
    for name, n in (("mean_d", D), ("mean_256", 256), ("mean_128", 128)):
        put(name, np.full((P, P), 1.0 / n, np.float32))
    put("mean_96", np.full((QK, QK), 1.0 / QK, np.float32))
    put("mean_64", np.kron(np.eye(2), np.full((HD, HD), 1.0 / HD)).astype(np.float32))
    put("ones", np.ones((P, P), np.float32))
    half = ROPE // 2
    rot = np.zeros((QK, QK), np.float32)
    for i in range(half):
        rot[NOPE + half + i, NOPE + i] = -1.0
        rot[NOPE + i, NOPE + half + i] = 1.0
    put("rot", rot)
    freq = (1.0 / (np.float32(10000.0) ** (np.arange(half, dtype=np.float32) / np.float32(half)))).astype(np.float32)
    ang = (np.arange(T, dtype=np.float32)[None, :] * freq[:, None]).astype(np.float32).astype(np.float64)
    cos = np.ones((QK, T), np.float32)
    sin = np.zeros((QK, T), np.float32)
    for at in (NOPE, NOPE + half):
        cos[at:at + half] = np.cos(ang)
        sin[at:at + half] = np.sin(ang)
    put("cos", cos)
    put("sin", sin)
    put("neg_mask", np.where(np.arange(P)[None, :] > np.arange(P)[:, None], NEG, 0.0).astype(np.float32))
    sel = np.zeros((P, HEADS, T), np.float32)
    for h in range(HEADS):
        sel[FL_ROW + h, h] = 1.0 / FOX_SCALE
    put("iota", np.broadcast_to(np.arange(TOPK, dtype=np.float32), (P, TOPK)))
    masks = np.zeros((P, len(LEVELS) - 1, 2, HD), np.uint32)
    s = np.arange(P)[:, None]
    for n, b in enumerate(LEVELS[:-1]):
        t = np.arange(P).reshape(-1, 2, b)[:, 1].reshape(1, HD)
        masks[:, n] = (s // b == t // b - 1)[:, None, :]
    return c, sel, masks.reshape(P, -1)


def runs(base, n, peel=0):
    at, out = base, []
    while at < base + n:
        left = base + n - at
        if at % RING == 0 and left >= 2 * RING and at - base >= peel:
            out.append((at, left // RING))
            at += left // RING * RING
        else:
            out.append((at, 0))
            at += 1
    return out


def each_piece(eng, base, n, body, peel=0):
    for at, turns in runs(base, n, peel):
        if not turns:
            body(at, at % RING)
            continue
        with eng.Fori(0, turns) as i:
            for slot in range(RING):
                body(i * RING + (at + slot), slot)


def each_turn(eng, n, body):
    with eng.Fori(0, n) as i:
        body(i)


def program(nc, a, out):
    ctx = ExitStack()
    with ctx:
        def sb(name, shape, dt=F32):
            return ctx.enter_context(nc.sbuf_tensor(name, shape, dt))

        def sem(name):
            return ctx.enter_context(nc.semaphore(name))

        ps = ctx.enter_context(nc.psum_tensor("ps", [P, 8, 512], F32))
        ring = sb("ring", [P, RING, PIECE])
        h = sb("h", [P, KT, T])
        u_all = sb("u", [P, KT * T])
        u = u_all[:, :].rearrange("p (k t) -> p k t", t=T)
        cols = sb("cols", [P, N_COLS])
        con = sb("con", [P, N_CONSTS])
        masks = sb("masks", [P, (len(LEVELS) - 1) * P], U32)
        keys = sb("keys", [P, 2 * HEADS, NKEYS])
        rstd = sb("rstd", [P, T])
        silu_c = sb("silu_c", [P, KT])
        ada = sb("ada", [P, 48])
        lb = sb("lb", [P, 6, KT])
        gain1 = sb("gain1", [P, KT])
        gain2 = sb("gain2", [P, KT])
        eps = sb("eps", [P, 1])
        ARENA = 32256
        arena = sb("arena", [P, ARENA])
        spot = [0]

        def place(at=None):
            if at is not None:
                spot[0] = at

        def view(*shape):
            n = int(np.prod(shape))
            assert spot[0] + n <= ARENA, (spot[0], n)
            v = arena[:, spot[0]:spot[0] + n]
            spot[0] += n
            names = "abcd"[:len(shape)]
            if len(shape) == 1:
                return v
            return v.rearrange(f"p ({' '.join(names)}) -> p {' '.join(names)}",
                               **dict(zip(names, shape)))

        def C(name):
            at, n = CON[name]
            return con[:, at:at + n]

        def V(name, k=0, n=1):
            return cols[:, COL[name] + k:COL[name] + k + n]

        ident = C("ident")

        place(0)
        glu = view(FT, T)
        sq = view(KT, T)
        act_g = view(RING, T)
        ada_ring = view(ADA_Q, ADA_W)
        ada_acc = view(ADA_Q, ADA_W)
        wuq = view(2, HEADS * QK)
        wuk = view(HEADS * NOPE)
        wuv = view(HEADS * HD)
        w_end = spot[0]
        place(0)
        praw = view(12, T)
        fqz = view(HEADS, SEQ)
        fk_tiles = view(2, T)
        lat_sq = act_g
        place(FT * T + KT * T + RING * T)
        lat_rms = view(2, T)
        cqn = view(2, SEQ)
        ckvn = view(T)
        cumz = view(T)
        ncumz = view(T)
        logf = view(4, T)
        vM = view(3, HEADS * HD)
        vF = view(3, HEADS * HD)
        assert spot[0] <= FT * T + KT * T + RING * T + ADA_Q * ADA_W, spot[0]
        place(w_end)
        qm = view(HEADS, SEQ)
        km = view(HEADS, T)
        turned = view(2, T)
        pe_sq = view(T)
        frms = view(40)
        mrms = view(40)
        qscale = view(16)
        mx = view(64)
        nmx = view(64)
        rsum = view(64)
        rinv = view(64)
        probs = act_g
        qsq = sq[:, :, 0:SEQ]
        ksq = praw[:, 0:HEADS, :]
        probsT = sq[:, 2:8, 0:P].rearrange("p (a b) t -> p a b t", a=2)
        sel = view(HEADS, T)
        more_fk_tiles = view(2, T)
        fk = [fk_tiles[:, 0, :], fk_tiles[:, 1, :], more_fk_tiles[:, 0, :], more_fk_tiles[:, 1, :]]
        oT = glu[:, 0:KT, 0:SEQ]

        place(0)
        z = view(7, KT, SEQ)
        pad_glu = view(KT, PAD + SEQ)
        zi = view(TT, D)
        suf = view(KT, SEQ)
        pre = z[:, 2]
        key = z[:, 1]
        q_odd = view(2, KT * P)
        k_even = view(2, KT, SEQ)
        qk = k_even[:, 1]
        AT = view(HEADS, 3, P)
        sq2 = view(KT, SEQ)
        o_rms = view(2 * HEADS)
        o_h = suf
        place(0)
        rows = view(GR, D)
        hf = view(TT, D)
        h_tok = view(TT, D)
        acc = view(TT, D)
        y_gain = view(D)
        final_g = view(D)
        qh = y_gain.rearrange("p (a e t) -> p a e t", a=2, e=2)
        scores = view(HEADS, TT, 2, NKEYS)
        left = view(TT, 2, NKEYS)
        left2 = left.rearrange("p t e n -> p t (e n)")
        cand = view(TT, TOPK * TOPK)
        onehot = cand.rearrange("p t (i j) -> p t i j", i=TOPK)
        top = view(TT, 2, TOPK)
        top_i = view(TT, 2, TOPK)
        pos = view(2, TT, TOPK)
        part_i = view(2, TT, TOPK)
        own_scores = view(TT, 2, NKEYS)
        own_best = view(TT, TOPK)
        own_gate = view(TT, TOPK)
        gate_s = view(TT)
        gate = view(TT, TOPK)
        dots = view(TT, TOPK)
        wts = view(TT, TOPK)
        fin = view(16)
        top_u = sb("top_u", [P, TT, 2, TOPK], U32)
        pos_u = sb("pos_u", [P, TT, TOPK], U32)
        part_u = sb("part_u", [P, 2, TT, TOPK], U32)
        eidx = sb("eidx", [P, HEADS * TT * TOPK], U32)
        stage = sb("stage", [P, 2, 8], U32)

        landed = [sem(f"weights_landed{i}") for i in range(RING)]
        used = sem("weights_used")
        x_in = sem("x_in")
        cols_in = sem("cols_in")
        con_in = sem("con_in")
        mask_in = sem("mask_in")
        small_in = sem("small_in")
        final_in = sem("final_in")
        ada_in = [sem(f"ada_in{i}") for i in range(ADA_Q)]
        ada_step = sem("ada_step")
        ada_mm = sem("ada_mm")
        ada_done = sem("ada_done")
        set_up = sem("set_up")
        lb_e = sem("lb_e")
        lb_step = sem("lb_step")
        silu_c_done = sem("silu_c_done")
        sq_done = sem("sq_done")
        ss_done = sem("ss_done")
        sqrt_done = sem("sqrt_done")
        rstd_done = sem("rstd_done")
        u_scaled = sem("u_scaled")
        u_done = sem("u_done")
        gate_mm = sem("gate_mm")
        silu_done = sem("silu_done")
        glu_done = sem("glu_done")
        down_mm = sem("down_mm")
        h_done = sem("h_done")
        proj_mm = sem("proj_mm")
        proj_ev = sem("proj_ev")
        fv_mm = sem("fv_mm")
        fv_ev = sem("fv_ev")
        lat_mm = sem("lat_mm")
        lat_sqrt = sem("lat_sqrt")
        mrec_done = sem("mrec_done")
        mstep = sem("mstep")
        fstat_mm = sem("fstat_mm")
        fstat_sqrt = sem("fstat_sqrt")
        frec = sem("frec")
        fq_mm = sem("fq_mm")
        fk_mm = sem("fk_mm")
        mstat_mm = sem("mstat_mm")
        mstat_sqrt = sem("mstat_sqrt")
        mrec2 = sem("mrec2")
        q_raw_mm = sem("q_raw_mm")
        q_raw_ev = sem("q_raw_ev")
        k_raw_mm = sem("k_raw_mm")
        k_raw_ev = sem("k_raw_ev")
        qrot_mm = sem("qrot_mm")
        krot_mm = sem("krot_mm")
        kn_mm = sem("kn_mm")
        kn_done = sem("kn_done")
        lat_done = sem("lat_done")
        fox_done = sem("fox_done")
        z_done = sem("z_done")
        f_exp = sem("f_exp")
        f_ln = sem("f_ln")
        cum_done = sem("cum_done")
        kpe_done = sem("kpe_done")
        rope_step = sem("rope_step")
        vm_mm = sem("vm_mm")
        vm_ev = sem("vm_ev")
        s_mm = sem("s_mm")
        max_done = sem("max_done")
        nmax_done = sem("nmax_done")
        exp_done = sem("exp_done")
        rinv_done = sem("rinv_done")
        p_done = sem("p_done")
        pT_mm = sem("pT_mm")
        pT_ev = sem("pT_ev")
        o_mm = sem("o_mm")
        o_ev = sem("o_ev")
        wo_mm = sem("wo_mm")
        zi_mm = sem("zi_mm")
        zi_ev = sem("zi_ev")
        z_mm = sem("z_mm")
        z_ev = sem("z_ev")
        sig_done = sem("sig_done")
        lb_done = sem("lb_done")
        f_done = sem("f_done")
        suf_set = sem("suf_set")
        qk_done = sem("qk_done")
        diag_mm = sem("diag_mm")
        pad_done = sem("pad_done")
        cv_step = sem("cv_step")
        on_rec = sem("on_rec")
        o_step = sem("o_step")
        o_done = sem("o_done")
        merged = sem("merged")
        conv_step = sem("conv_step")
        ln_mm = sem("ln_mm")
        ln_act = sem("ln_act")
        lev_mm = sem("lev_mm")
        lev_in = sem("lev_in")
        lev_out = sem("lev_out")
        lev_up = sem("lev_up")
        oh_mm = sem("oh_mm")
        oh_ev = sem("oh_ev")
        on_mm = sem("on_mm")
        on_act = sem("on_act")
        dense_mm = sem("dense_mm")
        dense_ev = sem("dense_ev")
        q_mm = sem("q_mm")
        q_ev = sem("q_ev")
        tok_mm = sem("tok_mm")
        tok_ev = sem("tok_ev")
        sc_mm = sem("sc_mm")
        sc_ev = sem("sc_ev")
        tk = sem("topk_step")
        choose_passed = sem("choose_passed")
        idx_done = sem("idx_done")
        gate_sub = sem("gate_sub")
        gate_e = sem("gate_e")
        gate_done = sem("gate_done")
        rows_free = sem("rows_free")
        staged = sem("staged")
        idx_staged = sem("idx_staged")
        row_in = [sem(f"row_in{i}") for i in range(GR)]
        row_used = sem("row_used")
        gelu_done = sem("gelu_done")
        w_done = sem("w_done")
        fin_step = sem("fin_step")
        fin_act = sem("fin_act")
        gain_mm = sem("gain_mm")
        out_done = sem("out_done")
        assert N_PIECES % RING == 2

        block = ctx.enter_context(nc.Block())
        xc = slice(X0, T)
        PROJ_BANKS = 6
        HEAD_BANKS = [3, 4, 5, 7]
        FK_BANKS = [2, 0, 1, 2]
        NORM_BANKS = [0, 1, 2, 6]
        GATES = [ACT.Silu, ACT.Sigmoid, ACT.Sigmoid]
        Z_BANKS = [4, 5, 6, 7]
        LEVEL_BANKS = [2, 0]

        def q_scale(hd, t):
            return qscale[:, t * HEADS + hd:t * HEADS + hd + 1] if hd < HEADS else FOX_SCALE

        NORM_COLS = [slice(0, T), slice(0, T), xc, xc, xc]

        @block.sync
        def _(sp):
            sp.dma_start(h[:, :, :], a["x_t"]).then_inc(x_in, 16)

            def load(piece, slot):
                sp.wait_ge(used, piece - (RING - 1))
                src = a["stream"][piece] if isinstance(piece, int) else \
                    a["stream"][bass.ds(piece, 1)].rearrange("o p m -> p (o m)")
                sp.dma_start(ring[:, slot, :], src).then_inc(landed[slot], 16)

            for n in range(RING):
                sp.dma_start(ring[:, n, :], a["stream"][n]).then_inc(landed[n], 16)
            each_piece(sp, RING, N_PIECES - RING, load)
            sp.wait_ge(fin_step, 2 * 6)
            for t in range(TT):
                sp.dma_start(out[0, t * P:(t + 1) * P, :], acc[:, t, :]).then_inc(out_done, 16)
            sp.wait_ge(out_done, 16 * TT)

        @block.gpsimd
        def _(pool):
            pool.memset(eps[:, :], EPS).then_inc(set_up, 1)
            for n in range(KT * ADA_Q):
                kt, q = divmod(n, ADA_Q)
                if kt:
                    pool.wait_ge(ada_step, n - ADA_Q + 1)
                pool.dma_start(ada_ring[:, q, :], a["ada"][n]).then_inc(ada_in[q], 16)

            pool.wait_ge(h_done, 3 * KT)
            pool.memset(suf[:, :, :], 1.0).then_inc(suf_set, 1)
            pool.wait_ge(z_ev, 4 * KT)
            pool.wait_ge(f_done, KT + 1)
            pool.tensor_tensor(qk, z[:, 3], key, ALU.mult).then_inc(qk_done, 1)

            def gather(table, n, slot0):
                par = slot0[1]
                if not isinstance(n, int) or n >= 2:
                    pool.wait_ge(row_used, n * 8 - GR + 8)
                    pool.sem_inc(rows_free, 1)
                pool.tensor_copy(stage[:, par, :], eidx[:, bass.ds(slot0[0], 8)]).then_inc(staged, 1)
                pool.wait_ge(staged, n + 1)
                pool.sem_inc(idx_staged, 1)
                for j in range(8):
                    r = par * 8 + j
                    pool.indirect_dma_start(rows[:, r, :], None, table,
                                            bass.IndirectOffsetOnAxis(ap=stage[:, par, j:j + 1], axis=0)
                                            ).then_inc(row_in[r], 16)

            def gather_head(hd):
                pool.wait_ge(idx_done, hd + 1)
                for g in range(4 * TT):
                    table = a["peer_u"] if g < 2 * TT else a["peer_v"]
                    gather(table, hd * (4 * TT) + g, (hd * (TT * TOPK) + g % (2 * TT) * 8, g % 2))

            gather_head(0)
            with pool.Fori(1, HEADS) as hd:
                gather_head(hd)

        @block.scalar
        def _(act):
            act.dma_start(cols[:, :], a["cols"]).then_inc(cols_in, 16)
            act.dma_start(con[:, :], a["con"]).then_inc(con_in, 16)
            act.dma_start(wuq[:, :, :], a["wuq"]).then_inc(small_in, 16)
            act.dma_start(wuk, a["wuk"]).then_inc(small_in, 16)
            act.dma_start(wuv, a["wuv"]).then_inc(small_in, 16)
            act.dma_start(masks[:, :], a["masks"]).then_inc(mask_in, 16)
            act.dma_start(keys[:, :, :], a["keys"]).then_inc(small_in, 16)
            act.dma_start(sel, a["sel"]).then_inc(small_in, 16)
            act.wait_ge(cols_in, 16)
            act.activation(silu_c[:, :], V("c", 0, KT), ACT.Silu).then_inc(silu_c_done, 1)
            act.wait_ge(lb_step, 3)
            for r in (1, 2):
                act.activation(lb[:, r], lb[:, r], ACT.Exp).then_inc(lb_e, 1)

            def norm(n):
                c = NORM_COLS[n]
                w = c.stop - c.start
                if n == 0:
                    act.wait_ge(x_in, 16)
                    act.wait_ge(set_up, 1)
                dst = sq if n < 3 else sq2
                for k in range(KT):
                    if n:
                        act.wait_ge(h_done, KT * (n - 1) + k + 1)
                    act.activation(dst[:, k, 0:w], h[:, k, c], ACT.Square).then_inc(sq_done, 1)
                act.wait_ge(ss_done, n + 1)
                act.activation(rstd[:, 0:w], ps[:, 0, 0:w], ACT.Sqrt, bias=eps[:, :]).then_inc(sqrt_done, 1)

            def ffn(k):
                base = BASE["ffn2" if k else "ffn1"]
                w = SEQ if k else T

                def body(piece, slot):
                    f = piece - (base - FT * k)
                    act.wait_ge(gate_mm, f + 1)
                    act.activation(act_g[:, slot, 0:w], ps[:, 2 * slot, 0:w], ACT.Silu).then_inc(silu_done, 1)

                each_piece(act, base, FT, body, peel=0 if k else RING)

            def attn_evac(act, n):
                hd, t = divmod(n, TT)
                half = HD * (hd % 2)
                act.wait_ge(pT_mm, n + 1)
                if n >= 2:
                    act.wait_ge(o_mm, n - 1)
                full = t + 1
                bank = 3 + n % 2
                act.activation(probsT[:, n % 2, 0:full, :],
                               ps[:, bank, 0:full * P].rearrange("p (a b) -> p a b", b=P), ACT.Copy)
                act.activation(probsT[0:N_META, n % 2, full, :], ps[0:N_META, bank, full * P:full * P + P], ACT.Copy
                               ).then_inc(pT_ev, 1)
                act.wait_ge(o_mm, n + 1)
                act.activation(oT[half:half + HD, hd // 2, t * P:(t + 1) * P],
                               ps[half:half + HD, 5 + n % 2, 0:P], ACT.Copy).then_inc(o_ev, 1)

            norm(0)
            ffn(0)
            norm(1)
            for i in range(12):
                act.wait_ge(proj_mm, i + 1)
                src = ps[:, i % PROJ_BANKS, 0:T]
                copy = act.activation(praw[:, i, :], src, ACT.Copy)
                if i == 3:
                    copy.then_inc(proj_ev, 1)
                else:
                    act.activation(lat_sq[:, i, :] if i < 3 else sq[:, i - 4, :], src, ACT.Square).then_inc(proj_ev, 1)
                if i == 8:
                    act.wait_ge(ada_step, KT * ADA_Q)
                    act.wait_ge(lat_mm, 1)
                    act.activation(lat_rms[:, 0, :], ps[:, 6, 0:T], ACT.Sqrt, bias=eps[:, :]).then_inc(lat_sqrt, 1)
                    act.activation(lat_rms[:, 1, :], ps[:, 7, 0:T], ACT.Sqrt, bias=eps[:, :]).then_inc(lat_sqrt, 1)
            act.wait_ge(fv_mm, 1)
            for t in range(3):
                n = P if t < 2 else N_META
                act.activation(vF[0:n, t, :], ps[0:n, t, :], ACT.Copy).then_inc(fv_ev, 1)
            act.wait_ge(fstat_mm, 1)
            act.activation(frms[:, 0:32], ps[:, 6, 0:32], ACT.Sqrt, bias=eps[:, :]).then_inc(fstat_sqrt, 1)
            act.activation(frms[0:N_META, 32:40], ps[0:N_META, 6, 32:40], ACT.Sqrt, bias=eps[0:N_META, :]
                           ).then_inc(fstat_sqrt, 1)
            for b in range(4):
                act.wait_ge(q_raw_mm, b + 1)
                src = ps[0:QK, HEAD_BANKS[b], :].rearrange("p (a t) -> p a t", a=2)
                act.activation(qm[0:QK, 2 * b:2 * b + 2, :], src, ACT.Copy, scale=V("g_q")[0:QK])
                act.activation(qsq[0:QK, 2 * b:2 * b + 2, :], src, ACT.Square).then_inc(q_raw_ev, 1)
            fr = slice(FL_ROW, FL_ROW + HEADS)
            act.wait_ge(z_done, 3)
            act.activation(logf[fr, 1, :], logf[fr, 1, :], ACT.Exp, scale=-1.0).then_inc(f_exp, 1)
            act.wait_ge(f_exp, 1)
            act.activation(logf[fr, 2, :], logf[fr, 1, :], ACT.Ln, bias=1.0).then_inc(f_ln, 1)
            for hd in range(HEADS):
                act.wait_ge(k_raw_mm, hd + 1)
                if hd == 0:
                    act.wait_ge(fox_done, 12)
                    act.wait_ge(kpe_done, 2)
                src = ps[0:NOPE, HEAD_BANKS[hd % 4], 0:T]
                act.activation(km[0:NOPE, hd, :], src, ACT.Copy, scale=V("g_k")[0:NOPE])
                act.activation(ksq[0:NOPE, hd, :], src, ACT.Square).then_inc(k_raw_ev, 1)
            act.wait_ge(vm_mm, 1)
            for t in range(3):
                n = P if t < 2 else N_META
                act.activation(vM[0:n, t, :], ps[0:n, t, :], ACT.Copy).then_inc(vm_ev, 1)
            act.wait_ge(mstat_mm, 1)
            act.activation(mrms[:, 0:32], ps[:, 6, 0:32], ACT.Sqrt, bias=eps[:, :]).then_inc(mstat_sqrt, 1)
            act.activation(mrms[0:N_META, 32:40], ps[0:N_META, 6, 32:40], ACT.Sqrt, bias=eps[0:N_META, :]
                           ).then_inc(mstat_sqrt, 1)
            for n in range(2 * HEADS * TT):
                hd, t = divmod(n, TT)
                keys_n = X0 + P * (t + 1)
                act.wait_ge(nmax_done, n + 1)
                if n >= 4:
                    act.wait_ge(pT_mm, n - 3)
                act.activation(probs[:, n % 4, 0:keys_n], ps[:, n % 3, 0:keys_n], ACT.Exp,
                               bias=nmx[:, n:n + 1], scale=q_scale(hd, t),
                               accum_out=rsum[:, n:n + 1]).then_inc(exp_done, 1)
                if n >= 2:
                    attn_evac(act, n - 2)
            attn_evac(act, 2 * HEADS * TT - 2)
            attn_evac(act, 2 * HEADS * TT - 1)
            norm(2)
            ffn(1)
            norm(3)

            def z_copy(seg):
                for m in range(KT):
                    act.wait_ge(z_mm, seg * KT + (m + 1))
                    act.activation(z[:, bass.ds(seg, 1), m, :].rearrange("p o t -> p (o t)"),
                                   ps[:, Z_BANKS[m % 4], 0:SEQ], ACT.Copy).then_inc(z_ev, 1)

            def gate_copy(i, fn):
                act.wait_ge(z_mm, 4 * KT + i + 1)
                act.activation(z[:, 4 + i // KT, i % KT, :], ps[:, Z_BANKS[i % 4], 0:SEQ], fn).then_inc(z_ev, 1)

            for pair in range(2):
                with act.Fori(2 * pair, 2 * pair + 2) as seg:
                    z_copy(seg)
                seg = 1 + pair
                act.wait_ge(z_ev, (seg + 1 if seg == 1 else 2 * pair + 2) * KT)
                act.activation(z[:, seg], z[:, seg], ACT.Sigmoid).then_inc(sig_done, 1)
            act.wait_ge(lb_done, 1)
            act.wait_ge(sig_done, 2)
            for m in range(KT):
                act.activation(pre[:, m, :], pre[:, m, :], ACT.Identity, scale=lb[:, 1, m:m + 1], bias=lb[:, 0, m:m + 1]
                               ).then_inc(f_done, 1)
            act.wait_ge(f_done, KT)
            act.wait_ge(pad_done, 1)
            act.activation(key, pre, ACT.Identity, scale=-1.0, bias=1.0).then_inc(f_done, 1)
            act.wait_ge(zi_mm, 1)
            for t in range(TT):
                for half in range(2):
                    act.activation(zi[:, t, half * 512:(half + 1) * 512], ps[:, t * 2 + half, :], ACT.Copy
                                   ).then_inc(zi_ev, 1)
            for i in range(4):
                gate_copy(i, GATES[0])
            act.wait_ge(cv_step, 1)
            act.activation(sq2[:, :, :], z[:, 0], ACT.Square).then_inc(ln_act, 1)
            for i in range(4, 6):
                gate_copy(i, GATES[0])
            act.wait_ge(ln_mm, 2)
            act.activation(rstd[:, 0:SEQ], ps[:, 0, 0:SEQ], ACT.Sqrt, bias=eps[:, :]).then_inc(ln_act, 1)
            for i in range(6, 10):
                gate_copy(i, GATES[i // KT])
            act.wait_ge(cv_step, 3)
            for m in range(KT):
                act.activation(z[:, 0, m, :], z[:, 0, m, :], ACT.Silu, scale=V("ln_g", m), bias=V("ln_b", m)
                               ).then_inc(ln_act, 1)
            for i in range(10, 20):
                gate_copy(i, GATES[i // KT])
            for b in range(4):
                act.wait_ge(oh_mm, b + 1)
                flat = slice(2 * b, 2 * b + 2)
                act.activation(o_h[:, flat, :].rearrange("p h t -> p (h t)"), ps[:, b, :], ACT.Copy).then_inc(oh_ev, 1)
                act.activation(sq2[:, flat, :].rearrange("p h t -> p (h t)"), ps[:, b, :], ACT.Square).then_inc(oh_ev, 1)
            for i in range(20, 24):
                gate_copy(i, GATES[i // KT])
            act.wait_ge(on_mm, 1)
            act.activation(o_rms, ps[:, 0, 0:2 * HEADS], ACT.Sqrt, bias=eps[:, :]).then_inc(on_act, 1)
            norm(4)
            act.dma_start(final_g, a["final_g"].rearrange("(o d) -> o d", o=1).broadcast_to([P, D])
                          ).then_inc(final_in, 16)

            def tok_copy(n):
                act.wait_ge(tok_mm, n + 1)
                act.activation((hf, h_tok)[n // 4][:, n // 2 % 2, n % 2 * 512:n % 2 * 512 + 512], ps[:, 6 + n % 2, :], ACT.Copy
                               ).then_inc(tok_ev, 1)

            for hd in range(HEADS):
                for e in range(2):
                    act.wait_ge(q_mm, hd * 2 + e + 1)
                    if hd >= 2:
                        act.wait_ge(sc_mm, hd - 1)
                    act.activation(qh[:, hd % 2, e, :], ps[:, hd % 2 * 2 + e, 0:SEQ], ACT.Copy).then_inc(q_ev, 1)
                if hd == 0:
                    tok_copy(0)
                    tok_copy(1)
                act.wait_ge(sc_mm, hd + 1)
                act.activation(scores[:, hd].rearrange("p t e n -> p (t e n)"), ps[:, 4 + hd % 2, :], ACT.Copy
                               ).then_inc(sc_ev, 1)
                if hd == 0:
                    tok_copy(2)
                    tok_copy(3)
            for n in range(4, 8):
                tok_copy(n)
            act.wait_ge(gain_mm, 1)
            for half in range(2):
                act.activation(y_gain[:, half * 512:half * 512 + 512], ps[:, half, :], ACT.Copy).then_inc(tok_ev, 1)
            def weights(hd):
                act.wait_ge(gate_sub, hd + 1)
                act.activation(own_gate, own_gate, ACT.Exp).then_inc(gate_e, 1)
                act.wait_ge(row_used, hd * (2 * TT * GR) + TT * GR)
                act.activation(dots, dots, ACT.Gelu).then_inc(gelu_done, 1)

            each_turn(act, HEADS, weights)
            for t in range(TT):
                act.wait_ge(fin_step, 6 * t + 3)
                act.activation(fin[:, 2 * t + 1:2 * t + 2], fin[:, 2 * t:2 * t + 1], ACT.Sqrt, bias=eps[:, :],
                               scale=1.0 / D).then_inc(fin_act, 1)

        @block.vector
        def _(dve):
            steps = {}

            def then(ins, s):
                steps[s.name] = steps.get(s.name, 0) + 1
                ins.then_inc(s, 1)
                dve.wait_ge(s, steps[s.name])

            dve.wait_ge(cols_in, 16)
            then(dve.tensor_tensor(lb[:, 0], V("lb0", 0, KT), V("lb1", 0, KT), ALU.max), lb_step)
            then(dve.tensor_tensor(lb[:, 1], V("lb0", 0, KT), lb[:, 0], ALU.subtract), lb_step)
            then(dve.tensor_tensor(lb[:, 2], V("lb1", 0, KT), lb[:, 0], ALU.subtract), lb_step)
            dve.wait_ge(silu_c_done, 1)

            def norm(n, gain, shift=None):
                c = NORM_COLS[n]
                w = c.stop - c.start
                dve.wait_ge(sqrt_done, n + 1)
                dve.reciprocal(rstd[:, 0:w], rstd[:, 0:w]).then_inc(rstd_done, 1)
                dve.wait_ge(rstd_done, n + 1)
                for k in range(KT):
                    ins = dve.scalar_tensor_tensor(u[:, k, 0:w], h[:, k, c], gain(k), rstd[:, 0:w], ALU.mult, ALU.mult)
                    ins.then_inc(u_done if shift is None else u_scaled, 1)
                if shift is not None:
                    for k in range(KT):
                        dve.wait_ge(u_scaled, KT * (n - 3) + k + 1)
                        dve.tensor_scalar(u[:, k, 0:w], u[:, k, 0:w], shift(k), None, ALU.add).then_inc(u_done, 1)

            def ada_add(n, kt, q):
                dve.wait_ge(ada_in[q], kt * 16 + 16)
                if isinstance(n, int) and n < ADA_Q:
                    dve.tensor_scalar(ada_acc[:, q, :], ada_ring[:, q, :], silu_c[:, 0:1], None, ALU.mult
                                      ).then_inc(ada_step, 1)
                else:
                    dve.wait_ge(ada_step, n - (ADA_Q - 1))
                    dve.scalar_tensor_tensor(ada_acc[:, q, :], ada_ring[:, q, :], silu_c[:, bass.ds(kt, 1)],
                                             ada_acc[:, q, :], ALU.mult, ALU.add).then_inc(ada_step, 1)

            def ffn(k):
                base = BASE["ffn2" if k else "ffn1"]
                w = SEQ if k else T

                def body(piece, slot):
                    f = piece - (base - FT * k)
                    dve.wait_ge(silu_done, f + 1)
                    dve.wait_ge(used, piece + 1)
                    dve.tensor_tensor(glu[:, bass.ds(piece - base, 1), 0:w].rearrange("p o t -> p (o t)"),
                                      act_g[:, slot, 0:w], ps[:, 2 * slot + 1, 0:w], ALU.mult).then_inc(glu_done, 1)

                if k:
                    each_piece(dve, base, FT, body)
                else:
                    def turn(i):
                        for slot in range(RING):
                            body(i * RING + slot, slot)
                            ada_add(i * RING + slot, i, slot)

                    turn(0)
                    with dve.Fori(1, FT // RING) as i:
                        turn(i)
                    for slot in range(FT % RING):
                        body(FT // RING * RING + slot, slot)
                        ada_add(FT // RING * RING + slot, FT // RING, slot)
                dve.wait_ge(down_mm, k + 1)
                c = slice(0, T) if k == 0 else xc
                for m in range(KT):
                    dve.scalar_tensor_tensor(h[:, m, c], ps[:, m, 0:w], 0.5, h[:, m, c], ALU.mult, ALU.add
                                             ).then_inc(h_done, 1)

            norm(0, lambda k: V("g_ffn1", k))
            ffn(0)
            norm(1, lambda k: V("g_mix", k))
            for n in range(FT, KT * ADA_Q):
                ada_add(n, n // ADA_Q, n % ADA_Q)

            dve.wait_ge(lat_sqrt, 2)
            dve.reciprocal(lat_rms[:, :, :], lat_rms[:, :, :]).then_inc(mrec_done, 1)
            dve.wait_ge(mrec_done, 1)
            for k in range(2):
                dve.scalar_tensor_tensor(cqn[:, k, :], praw[:, k, xc], V("g_cq", k), lat_rms[:, 0, xc], ALU.mult, ALU.mult
                                         ).then_inc(lat_done, 1)
            dve.scalar_tensor_tensor(ckvn, praw[:, 2, :], V("g_ckv"), lat_rms[:, 1, :], ALU.mult, ALU.mult
                                     ).then_inc(lat_done, 1)
            fr = slice(FL_ROW, FL_ROW + HEADS)
            then(dve.tensor_scalar(logf[fr, 1, :], praw[fr, 3, :], V("b_f")[fr], None, ALU.add), z_done)
            then(dve.tensor_scalar(logf[fr, 0, :], logf[fr, 1, :], 0.0, None, ALU.min), z_done)
            then(dve.scalar_tensor_tensor(logf[fr, 1, :], logf[fr, 0, :], -2.0, logf[fr, 1, :], ALU.mult, ALU.add), z_done)
            pr = slice(PE_ROW, PE_ROW + ROPE)
            pe_all = praw[pr, 3:4, :].broadcast_to([ROPE, HEADS, T])
            dve.tensor_scalar(km[pr, :, :], pe_all, V("g_k")[pr], None, ALU.mult).then_inc(kpe_done, 1)
            then(dve.tensor_tensor(pe_sq[pr, :], praw[pr, 3, :], praw[pr, 3, :], ALU.mult), lb_step)
            then(dve.memset(fqz[:, :, :], 0.0), lb_step)
            then(dve.memset(cumz, 0.0), lb_step)
            dve.wait_ge(fstat_sqrt, 2)
            then(dve.reciprocal(frms[:, 0:32], frms[:, 0:32]), mstep)
            dve.reciprocal(frms[0:N_META, 32:40], frms[0:N_META, 32:40]).then_inc(frec, 1)
            for j in range(4):
                dve.wait_ge(fq_mm, j // 2 + 1)
                for e in range(2):
                    r = slice(HD * e, HD * e + HD)
                    dve.scalar_tensor_tensor(fqz[r, 2 * j + e, :], praw[r, 4 + j, xc], V("g_fq")[r],
                                             ps[r, j // 2, j % 2 * SEQ:j % 2 * SEQ + SEQ], ALU.mult, ALU.mult
                                             ).then_inc(fox_done, 1)
            for j in range(4):
                dve.wait_ge(fk_mm, j + 1)
                dve.scalar_tensor_tensor(fk[j], praw[:, 8 + j, :], V("g_fk"), ps[:, FK_BANKS[j], 0:T],
                                         ALU.mult, ALU.mult).then_inc(fox_done, 1)
            dve.wait_ge(f_ln, 1)
            then(dve.tensor_tensor(logf[fr, 3, :], logf[fr, 0, :], logf[fr, 2, :], ALU.subtract), cum_done)
            then(dve.tensor_tensor_scan(cumz[fr, :], C("ones")[fr, 0:1].broadcast_to([HEADS, T]), logf[fr, 3, :], 0.0,
                                        ALU.mult, ALU.add), cum_done)
            dve.tensor_scalar(ncumz, cumz, -1.0, None, ALU.mult).then_inc(cum_done, 1)
            dve.wait_ge(fox_done, 12)
            dve.wait_ge(kpe_done, 1)
            dve.tensor_copy(ksq[pr, :, :], pe_sq[pr, None, :].broadcast_to([ROPE, HEADS, T])).then_inc(kpe_done, 1)

            def rope(x, rotated, c, n):
                shape = list(x.shape)
                cos = C("cos")[0:QK, None, c].broadcast_to(shape)
                sin = C("sin")[0:QK, None, c].broadcast_to(shape)
                tmp = turned[0:QK, 0:shape[1], 0:shape[2]]
                if n:
                    dve.wait_ge(rope_step, 3 * n)
                dve.tensor_tensor(tmp, rotated, sin, ALU.mult).then_inc(rope_step, 1)
                dve.tensor_tensor(x, x, cos, ALU.mult).then_inc(rope_step, 1)
                dve.wait_ge(rope_step, 3 * n + 2)
                dve.tensor_tensor(x, x, tmp, ALU.add).then_inc(rope_step, 1)

            dve.wait_ge(mstat_sqrt, 2)
            then(dve.reciprocal(mrms[:, 0:32], mrms[:, 0:32]), mstep)
            then(dve.reciprocal(mrms[0:N_META, 32:40], mrms[0:N_META, 32:40]), mstep)
            dve.tensor_scalar(qscale, mrms[:, 0:16], MLA_SCALE, None, ALU.mult).then_inc(mrec2, 1)
            for b in range(4):
                dve.wait_ge(qrot_mm, b + 1)
                rope(qm[0:QK, 2 * b:2 * b + 2, :], ps[0:QK, HEAD_BANKS[b], :].rearrange("p (a t) -> p a t", a=2),
                     slice(X0, T), b)
            for hd in range(HEADS):
                dve.wait_ge(kn_mm, hd + 1)
                dve.tensor_tensor(km[0:QK, hd, :], km[0:QK, hd, :], ps[0:QK, NORM_BANKS[hd % 4], 0:T], ALU.mult
                                  ).then_inc(kn_done, 1)
                if hd:
                    dve.wait_ge(krot_mm, hd)
                    rope(km[0:QK, hd - 1:hd, :], ps[0:QK, None, HEAD_BANKS[(hd - 1) % 4], 0:T], slice(0, T), 4 + hd - 1)
            dve.wait_ge(krot_mm, HEADS)
            rope(km[0:QK, HEADS - 1:HEADS, :], ps[0:QK, None, HEAD_BANKS[(HEADS - 1) % 4], 0:T], slice(0, T), 4 + HEADS - 1)

            def soft_max(n):
                hd, t = divmod(n, TT)
                keys_n = X0 + P * (t + 1)
                dve.wait_ge(s_mm, n + 1)
                dve.reduce_max(mx[:, n:n + 1], ps[:, n % 3, 0:keys_n], AX_X).then_inc(max_done, 1)
                dve.wait_ge(max_done, n + 1)
                dve.tensor_scalar(nmx[:, n:n + 1], mx[:, n:n + 1], q_scale(hd, t), -1.0, ALU.mult, ALU.mult
                                  ).then_inc(nmax_done, 1)

            def scale_p(n):
                t = n % TT
                keys_n = X0 + P * (t + 1)
                dve.wait_ge(exp_done, n + 1)
                dve.reciprocal(rinv[:, n:n + 1], rsum[:, n:n + 1]).then_inc(rinv_done, 1)
                dve.wait_ge(rinv_done, n + 1)
                dve.tensor_scalar(probs[:, n % 4, 0:keys_n], probs[:, n % 4, 0:keys_n], rinv[:, n:n + 1], None, ALU.mult
                                  ).then_inc(p_done, 1)

            units = 2 * HEADS * TT
            soft_max(0)
            for n in range(units):
                if n + 1 < units:
                    soft_max(n + 1)
                scale_p(n)
            for m in range(KT):
                dve.wait_ge(wo_mm, m + 1)
                dve.tensor_tensor(h[:, m, xc], h[:, m, xc], ps[:, m, 0:SEQ], ALU.add).then_inc(h_done, 1)
            norm(2, lambda k: V("g_ffn2", k))
            dve.wait_ge(ada_mm, 1)
            then(dve.tensor_tensor(ada[:, :], ps[:, 7, 256:304], V("ada_b", 0, 48), ALU.add), ada_done)
            then(dve.scalar_tensor_tensor(gain1[:, :], ada[:, 8:16], 1.0, V("norm1", 0, KT), ALU.add, ALU.mult), ada_done)
            then(dve.scalar_tensor_tensor(gain2[:, :], ada[:, 32:40], 1.0, V("norm2", 0, KT), ALU.add, ALU.mult), ada_done)
            ffn(1)
            norm(3, lambda k: gain1[:, k:k + 1], lambda k: ada[:, k:k + 1])

            dve.wait_ge(lb_e, 2)
            then(dve.tensor_tensor(lb[:, 3], lb[:, 1], lb[:, 2], ALU.add), lb_step)
            then(dve.reciprocal(lb[:, 4], lb[:, 3]), lb_step)
            then(dve.tensor_tensor(lb[:, 0], lb[:, 1], lb[:, 4], ALU.mult), lb_step)
            dve.tensor_scalar(lb[:, 1], lb[:, 0], -1.0, 1.0, ALU.mult, ALU.add).then_inc(lb_done, 1)
            then(dve.memset(pad_glu[:, :, 0:PAD], 0.0), lb_step)
            dve.wait_ge(sig_done, 1)
            dve.tensor_tensor(pad_glu[:, :, PAD:PAD + SEQ], z[:, 0], z[:, 1], ALU.mult).then_inc(pad_done, 1)
            dve.wait_ge(pad_done, 1)
            cv = z[:, 0]
            for m in range(KT):
                dve.tensor_scalar(cv[:, m, :], pad_glu[:, m, 0:SEQ], V("conv_w", m), V("conv_b", m), ALU.mult, ALU.add
                                  ).then_inc(conv_step, 1)
            with dve.Fori(1, CONV_K) as tap:
                for m in range(KT):
                    dve.wait_ge(conv_step, tap * KT + (m + 1 - KT))
                    dve.scalar_tensor_tensor(cv[:, m, :], pad_glu[:, m, bass.ds(tap, SEQ)],
                                             cols[:, bass.ds(tap * KT + (COL["conv_w"] + m), 1)], cv[:, m, :],
                                             ALU.mult, ALU.add).then_inc(conv_step, 1)

            def blocks(x, b, e):
                v = x.rearrange("p h t -> p (h t)").rearrange("p (n e b) -> p n e b", e=2, b=b)
                return v[:, :, e, :]

            def last(x, b, e):
                v = x.rearrange("p h t -> p (h t)").rearrange("p (n e b) -> p n e b", e=2, b=b)
                return v[:, :, e, b - 1:b].broadcast_to([P, KT * SEQ // (2 * b), b])

            q = z[:, 3]

            def level_in(n):
                b = LEVELS[n]
                buf = n % 2
                if n >= 2:
                    dve.wait_ge(lev_mm, n - 1)
                dve.tensor_tensor(q_odd[:, buf].rearrange("p (n b) -> p n b", b=b), blocks(q, b, 1), blocks(pre, b, 1), ALU.mult
                                  ).then_inc(lev_in, 1)
                if n in (1, 2):
                    if n == 2:
                        dve.wait_ge(diag_mm, 1)
                    dve.tensor_tensor(k_even[:, buf], key, suf[:, :, :], ALU.mult).then_inc(lev_in, 1)
                elif n:
                    dve.tensor_tensor(blocks(k_even[:, buf], b, 0), blocks(key, b, 0), blocks(suf[:, :, :], b, 0), ALU.mult
                                      ).then_inc(lev_in, 1)
                if b < P:
                    dve.wait_ge(lev_in, 2 * n + 1 if n else 1)
                    then(dve.tensor_tensor(blocks(suf[:, :, :], b, 0), blocks(suf[:, :, :], b, 0), last(pre, b, 1),
                                           ALU.mult), lev_up)
                    then(dve.tensor_tensor(blocks(pre, b, 1), blocks(pre, b, 1), last(pre, b, 0), ALU.mult), lev_up)

            def level_out(n):
                b = LEVELS[n]
                dve.wait_ge(lev_mm, n + 1)
                dve.wait_ge(lev_out, n + 1)
                src = ps[:, LEVEL_BANKS[n % 2]:LEVEL_BANKS[n % 2] + 2, :].rearrange("p k t -> p (k t)")
                if b < P:
                    m = masks[:, n * P:(n + 1) * P].rearrange("p (n b) -> p n b", b=b)
                    per = P // b
                    dst = AT[:, :, 0:2, :].rearrange("p h c t -> p h (c t)").rearrange("p h (n e b) -> p h n e b", e=2, b=b)
                    dve.copy_predicated(dst[:, :, :, 1, :], m[:, None, :, :].broadcast_to([P, HEADS, per, b]),
                                        src.rearrange("p (h n b) -> p h n b", h=HEADS, b=b)).then_inc(lev_out, 1)
                else:
                    dve.tensor_copy(AT[:, :, 2, :], src.rearrange("p (h t) -> p h t", t=P)).then_inc(lev_out, 1)

            dve.wait_ge(f_done, KT + 1)
            dve.wait_ge(suf_set, 1)
            level_in(0)
            dve.wait_ge(ln_mm, 1)
            mean = ps[:, 0, None, 0:SEQ].broadcast_to([P, KT, SEQ])
            dve.tensor_tensor(cv, cv, mean, ALU.subtract).then_inc(cv_step, 1)
            dve.wait_ge(diag_mm, 1)
            dve.tensor_tensor(AT[:, :, 0:2, :].rearrange("p h c t -> p h (c t)").rearrange("p h (c t) -> p h c t", c=2),
                              ident[:, None, None, :].broadcast_to([P, HEADS, TT, P]),
                              ps[:, 1, 0:2 * HEADS].rearrange("p (h c) -> p h c", c=2)[:, :, :, None].broadcast_to([P, HEADS, TT, P]),
                              ALU.mult).then_inc(lev_out, 1)
            dve.wait_ge(mask_in, 16)
            level_in(1)
            level_out(0)
            dve.wait_ge(ln_act, 2)
            dve.reciprocal(rstd[:, 0:SEQ], rstd[:, 0:SEQ]).then_inc(cv_step, 1)
            level_in(2)
            level_out(1)
            dve.wait_ge(cv_step, 2)
            dve.tensor_tensor(cv, cv, rstd[:, None, 0:SEQ].broadcast_to([P, KT, SEQ]), ALU.mult).then_inc(cv_step, 1)
            for n in range(3, len(LEVELS)):
                level_in(n)
                level_out(n - 1)
            level_out(len(LEVELS) - 1)
            dve.wait_ge(on_act, 1)
            dve.reciprocal(o_rms, o_rms).then_inc(on_rec, 1)
            for m in range(KT):
                dve.wait_ge(on_mm, 2 + m // 2)
                dve.scalar_tensor_tensor(o_h[:, m, :], o_h[:, m, :], V("hg_g", m), ps[:, m // 2, m % 2 * SEQ:m % 2 * SEQ + SEQ],
                                         ALU.mult, ALU.mult).then_inc(o_step, 1)
            for m in range(KT):
                dve.wait_ge(o_step, m + 1)
                dve.wait_ge(z_ev, 5 * KT)
                dve.tensor_tensor(o_h[:, m, :], o_h[:, m, :], z[:, 4, m, :], ALU.mult).then_inc(o_done, 1)
            for m in range(KT):
                dve.wait_ge(dense_mm, m + 1)
                dve.tensor_tensor(z[:, 6, m, :], z[:, 6, m, :], ps[:, Z_BANKS[m % 4], 0:SEQ], ALU.mult).then_inc(dense_ev, 1)
            for m in range(KT):
                dve.wait_ge(dense_mm, KT + m + 1)
                dve.tensor_tensor(z[:, 5, m, :], z[:, 5, m, :], ps[:, Z_BANKS[m % 4], 0:SEQ], ALU.mult).then_inc(dense_ev, 1)
                dve.wait_ge(dense_ev, KT + m + 1)
                dve.tensor_tensor(z[:, 5, m, :], z[:, 5, m, :], z[:, 6, m, :], ALU.add).then_inc(merged, 1)
            for m in range(KT):
                dve.wait_ge(dense_mm, 2 * KT + m + 1)
                dve.scalar_tensor_tensor(h[:, m, xc], ps[:, Z_BANKS[m % 4], 0:SEQ], ada[:, 16 + m:17 + m], h[:, m, xc], ALU.mult, ALU.add
                                         ).then_inc(h_done, 1)
            norm(4, lambda k: gain2[:, k:k + 1], lambda k: ada[:, 24 + k:25 + k])

            tile_shape = [P, TT, TOPK, TOPK]
            count = [0]

            def step(ins):
                ins.then_inc(tk, 1)
                count[0] += 1
                return count[0]

            def passed(hd, n):
                dve.wait_ge(tk, hd * CHOOSE_STEPS + n)
                dve.sem_inc(choose_passed, 1)

            def eight(hd, chains, at):
                for v, _, src in chains:
                    n = step(dve.max(v[:, at:at + 8], src))
                passed(hd, n)
                for v, where, src in chains:
                    step(dve.max_index(where[:, at:at + 8], v[:, at:at + 8], src))

            def without(chains, rests):
                for (v, _, src), rest in zip(chains, rests):
                    n = step(dve.match_replace(rest, v[:, 0:8], src, -3.0e38))
                return n

            halves = [(t, e) for t in range(TT) for e in range(2)]

            def choose_halves(hd):
                count[0] = 0
                dve.wait_ge(sc_ev, hd + 1)
                if not isinstance(hd, int) or hd:
                    dve.sem_inc(choose_passed, 1)
                    dve.wait_ge(tk, hd * CHOOSE_STEPS)
                    dve.sem_inc(choose_passed, 1)
                passed(hd, step(dve.tensor_copy(own_scores, scores[:, bass.ds(hd, 1)].rearrange("p o t e n -> p (o t) e n"))))
                chains = [(top[:, t, e], top_u[:, t, e], own_scores[:, t, e]) for t, e in halves]
                eight(hd, chains, 0)
                without(chains, [left[:, t, e] for t, e in halves])

            def choose_rest(hd):
                passed(hd, count[0])
                eight(hd, [(top[:, t, e], top_u[:, t, e], left[:, t, e]) for t, e in halves], TOPK // 2)
                step(dve.tensor_tensor(cand.rearrange("p t (i j) -> p t i j", i=TOPK),
                                       top[:, :, 0, :, None].broadcast_to(tile_shape),
                                       top[:, :, 1, None, :].broadcast_to(tile_shape), ALU.add))

            def choose_sums(hd):
                passed(hd, count[0])
                step(dve.tensor_copy(top_i, top_u[:, :, :, :]))
                chains = [(own_best[:, t], pos_u[:, t], cand[:, t]) for t in range(TT)]
                eight(hd, chains, 0)
                passed(hd, without(chains, [left2[:, t] for t in range(TT)]))
                eight(hd, [(own_best[:, t], pos_u[:, t], left2[:, t]) for t in range(TT)], TOPK // 2)
                dve.tensor_tensor(own_gate, own_best, own_best[:, :, 0:1].broadcast_to([P, TT, TOPK]), ALU.subtract
                                  ).then_inc(gate_sub, 1)

            def choose_index(hd):
                passed(hd, count[0])
                step(dve.tensor_scalar(part_u[:, 0], pos_u[:, :, :], 4, None, ALU.logical_shift_right))
                passed(hd, step(dve.tensor_scalar(part_u[:, 1], pos_u[:, :, :], TOPK - 1, None, ALU.bitwise_and)))
                passed(hd, step(dve.tensor_copy(pos, part_u[:, :, :, :])))
                iota = C("iota")[:, None, None, :].broadcast_to(tile_shape)
                for e in range(2):
                    passed(hd, step(dve.tensor_tensor(onehot, pos[:, e, :, :, None].broadcast_to(tile_shape), iota, ALU.is_equal)))
                    passed(hd, step(dve.tensor_tensor(onehot, onehot, top_i[:, :, e, None, :].broadcast_to(tile_shape), ALU.mult)))
                    passed(hd, step(dve.reduce_sum(part_i[:, e], onehot, AX_X)))
                passed(hd, step(dve.scalar_tensor_tensor(part_i[:, 0], part_i[:, 0], float(NKEYS), part_i[:, 1], ALU.mult, ALU.add)))
                dve.tensor_copy(eidx[:, bass.ds(hd * (TT * TOPK), TT * TOPK)],
                                part_i[:, 0].rearrange("p t k -> p (t k)")).then_inc(idx_done, 1)
                assert count[0] == CHOOSE_STEPS, count

            def dot(hd, t, par):
                turn = hd * (2 * TT) + t
                for r in range(par * 8, par * 8 + 8):
                    dve.wait_ge(row_in[r], turn * 16 + 16)
                    dve.tensor_tensor_reduce(rows[:, r, :], rows[:, r, :], hf[:, t, :], 1.0, 0.0, ALU.mult, ALU.add,
                                             dots[:, t, r:r + 1]).then_inc(row_used, 1)

            def weigh(hd, t, par):
                turn = hd * (2 * TT) + (TT + t)
                for r in range(par * 8, par * 8 + 8):
                    dve.wait_ge(row_in[r], turn * 16 + 16)
                    dve.wait_ge(row_used, turn * GR + r)
                    dve.scalar_tensor_tensor(acc[:, t, :], rows[:, r, :], wts[:, t, r:r + 1], acc[:, t, :], ALU.mult, ALU.add
                                             ).then_inc(row_used, 1)

            def head(hd, more):
                dot(hd, 0, 0)
                if more:
                    choose_halves(hd + 1)
                dot(hd, 0, 1)
                if more:
                    choose_rest(hd + 1)
                dot(hd, 1, 0)
                dve.wait_ge(gate_e, hd * 3 + 1)
                dve.reduce_sum(gate_s, own_gate, AX_X).then_inc(gate_e, 1)
                dve.wait_ge(gate_e, hd * 3 + 2)
                dve.reciprocal(gate_s, gate_s).then_inc(gate_e, 1)
                dve.wait_ge(gate_e, hd * 3 + 3)
                dve.tensor_tensor(gate, own_gate, gate_s[:, :, None].broadcast_to([P, TT, TOPK]), ALU.mult).then_inc(gate_done, 1)
                dot(hd, 1, 1)
                dve.wait_ge(gate_done, hd + 1)
                if more:
                    choose_sums(hd + 1)
                dve.wait_ge(gelu_done, hd + 1)
                dve.tensor_tensor(wts, dots, gate, ALU.mult).then_inc(w_done, 1)
                dve.wait_ge(w_done, hd + (TT + 1))
                weigh(hd, 0, 0)
                if more:
                    choose_index(hd + 1)
                weigh(hd, 0, 1)
                weigh(hd, 1, 0)
                weigh(hd, 1, 1)

            for part in (choose_halves, choose_rest, choose_sums, choose_index):
                part(0)
            for t in range(TT):
                dve.memset(acc[:, t, :], 0.0).then_inc(w_done, 1)
            dve.wait_ge(tok_ev, 4)
            with dve.Fori(0, HEADS - 1) as hd:
                head(hd, True)
            head(HEADS - 1, False)
            for t in range(TT):
                dve.wait_ge(row_used, HEADS * 2 * TT * GR - (TT - 1 - t) * GR)
                if t == 0:
                    dve.wait_ge(tok_ev, 10)
                    dve.wait_ge(final_in, 16)
                then(dve.tensor_tensor(acc[:, t, :], acc[:, t, :], y_gain, ALU.mult), fin_step)
                then(dve.tensor_tensor(acc[:, t, :], acc[:, t, :], h_tok[:, t, :], ALU.add), fin_step)
                then(dve.tensor_tensor_reduce(hf[:, t, :], acc[:, t, :], acc[:, t, :], 1.0, 0.0, ALU.mult, ALU.add,
                                              fin[:, 2 * t:2 * t + 1]), fin_step)
                dve.wait_ge(fin_act, t + 1)
                then(dve.reciprocal(fin[:, 8 + t:9 + t], fin[:, 2 * t + 1:2 * t + 2]), fin_step)
                then(dve.tensor_scalar(acc[:, t, :], acc[:, t, :], fin[:, 8 + t:9 + t], None, ALU.mult), fin_step)
                then(dve.tensor_tensor(acc[:, t, :], acc[:, t, :], final_g[:, :], ALU.mult), fin_step)

        @block.tensor
        def _(pe):
            def arrived(piece, slot):
                turn = piece // RING if isinstance(piece, int) else None
                if turn is not None:
                    pe.wait_ge(landed[slot], 16 * turn + 16)
                return turn

            def each(base, n, body, peel=0):
                for at, turns in runs(base, n, peel):
                    if not turns:
                        pe.wait_ge(landed[at % RING], at // RING * 16 + 16)
                        body(at, at % RING).then_inc(used, 1)
                        continue
                    with pe.Fori(0, turns) as i:
                        for slot in range(RING):
                            pe.wait_ge(landed[slot], i * 16 + (at // RING * 16 + 16))
                            body(i * RING + (at + slot), slot).then_inc(used, 1)

            def blk(slot, b):
                return ring[:, slot, b * P:(b + 1) * P]

            def norm(n):
                w = NORM_COLS[n].stop - NORM_COLS[n].start
                src = sq if n < 3 else sq2
                for k in range(KT):
                    pe.wait_ge(sq_done, KT * n + k + 1)
                    mm = pe.matmul(ps[:, 0, 0:w], C("mean_d"), src[:, k, 0:w], start=(k == 0), stop=(k == KT - 1))
                mm.then_inc(ss_done, 1)

            def ffn(k):
                base = BASE["ffn2" if k else "ffn1"]
                w = SEQ if k else T
                def up(piece, slot):
                    f = piece - (base - FT * k)
                    if k and isinstance(piece, int) and piece == base + 1:
                        pe.wait_ge(ada_done, 1)
                    if not (k == 0 and isinstance(piece, int) and piece < RING):
                        pe.wait_ge(glu_done, f - (RING - 1))
                    for e in range(2):
                        for b in range(KT):
                            if e == 0 and isinstance(piece, int) and piece == base:
                                pe.wait_ge(u_done, KT * 2 * k + b + 1)
                            mm = pe.matmul(ps[:, 2 * slot + e, 0:w], blk(slot, e * KT + b), u[:, b, 0:w],
                                           start=(b == 0), stop=(b == KT - 1))
                        if e == 0:
                            mm.then_inc(gate_mm, 1)
                    return mm

                each(base, FT, up, peel=0 if k else RING)
                pe.wait_ge(glu_done, FT * (k + 1))

                def down(piece, slot):
                    f = (piece - (base + FT)) * 2
                    for e in range(2):
                        for m in range(KT):
                            first = isinstance(f, int) and f + e == 0
                            final = isinstance(f, int) and f + e == FT - 1
                            mm = pe.matmul(ps[:, m, 0:w], blk(slot, e * KT + m),
                                           glu[:, bass.ds(f + e, 1), 0:w].rearrange("p o t -> p (o t)"),
                                           start=first, stop=final)
                    return mm

                each(base + FT, FFN_P - FT - 1, down, peel=1)
                last = base + FFN_P - 1
                pe.wait_ge(landed[last % RING], last // RING * 16 + 16)
                down(last, last % RING).then_inc(down_mm, 1)
                pe.wait_ge(down_mm, k + 1)
                pe.sem_inc(used, 1)

            def dense(name, rhs, done):
                def body(piece, slot):
                    for e in range(2):
                        m = (piece - BASE[name]) * 2 + e
                        for b in range(KT):
                            mm = pe.matmul(ps[:, m, 0:SEQ], blk(slot, e * KT + b), rhs[:, b, 0:SEQ],
                                           start=(b == 0), stop=(b == KT - 1))
                        if e == 0:
                            mm.then_inc(done, 1)
                    return mm

                for piece in range(BASE[name], BASE[name] + 4):
                    pe.wait_ge(landed[piece % RING], piece // RING * 16 + 16)
                    body(piece, piece % RING).then_inc(done, 1)
                    pe.wait_ge(done, done_count(done, 2))
                    pe.sem_inc(used, 1)

            counts = {}

            def done_count(s, n):
                counts[s.name] = counts.get(s.name, 0) + n
                return counts[s.name]

            pe.wait_ge(con_in, 16)
            norm(0)
            ffn(0)
            norm(1)
            def token_tiles(first, n):
                return [(first + s * P, min(P, T - first - s * P)) for s in range(n)]

            for p in range(6):
                piece = BASE["w_in"] + p
                slot = piece % RING
                pe.wait_ge(landed[slot], piece // RING * 16 + 16)
                for e in range(2):
                    i = 2 * p + e
                    if i >= PROJ_BANKS:
                        pe.wait_ge(proj_ev, i - PROJ_BANKS + 1)
                    for b in range(KT):
                        if i == 0:
                            pe.wait_ge(u_done, KT + b + 1)
                        mm = pe.matmul(ps[:, i % PROJ_BANKS, 0:T], blk(slot, e * KT + b), u[:, b, :],
                                       start=(b == 0), stop=(b == KT - 1))
                    mm.then_inc(proj_mm, 1)
                pe.wait_ge(proj_mm, 2 * p + 2)
                pe.sem_inc(used, 1)
                if p == 2:
                    pe.wait_ge(proj_ev, 3)
                    for k in range(2):
                        pe.matmul(ps[:, 6, 0:T], C("mean_256"), lat_sq[:, k, :], start=(k == 0), stop=(k == 1))
                    pe.matmul(ps[:, 7, 0:T], C("mean_128"), lat_sq[:, 2, :], start=True, stop=True).then_inc(lat_mm, 1)
            pe.wait_ge(proj_ev, 9)
            for p in range(2):
                piece = BASE["w_in"] + 6 + p
                slot = piece % RING
                pe.wait_ge(landed[slot], piece // RING * 16 + 16)
                for b in range(4):
                    k = p * 4 + b
                    for t, (at, n) in enumerate(token_tiles(0, 3)):
                        mm = pe.matmul(ps[0:n, t, :], u[:, k, at:at + n], ring[:, slot, b * 512:(b + 1) * 512],
                                       start=(k == 0), stop=(k == KT - 1))
                if p == 0:
                    mm.then_inc(used, 1)
                else:
                    mm.then_inc(fv_mm, 1)
                    pe.wait_ge(fv_mm, 1)
                    pe.sem_inc(used, 1)
            pe.wait_ge(proj_ev, 12)
            pe.wait_ge(lat_sqrt, 2)
            two = C("mean_64").rearrange("p (e d) -> p d e", e=2)[:, 0, :]
            for kind, tiles in ((0, token_tiles(X0, 2)), (1, token_tiles(0, 3))):
                for s, (at, n) in enumerate(tiles):
                    for j in range(4):
                        col = 16 * kind + s * 8 + j * 2
                        mm = pe.matmul(ps[0:n, 6, col:col + 2], sq[:, 4 * kind + j, at:at + n], two, start=True, stop=True)
            mm.then_inc(fstat_mm, 1)
            pe.wait_ge(small_in, 16 * 5)
            pe.wait_ge(lat_done, 3)
            for b in range(4):
                for i in range(2):
                    hd = 2 * b + i
                    for k in range(2):
                        mm = pe.matmul(ps[0:QK, HEAD_BANKS[b], i * SEQ:(i + 1) * SEQ], wuq[:, k, hd * QK:(hd + 1) * QK],
                                       cqn[:, k, :], start=(k == 0), stop=(k == 1))
                mm.then_inc(q_raw_mm, 1)

            def spread(dst, rms, kind, j, tiles):
                for s, (at, n) in enumerate(tiles):
                    for e in range(2):
                        col = 16 * kind + s * 8 + j * 2 + e
                        mm = pe.matmul(dst[HD * e:HD * e + HD, s * P:s * P + n], rms[0:n, col:col + 1].broadcast_to([n, HD]),
                                       ident[0:n, 0:n], start=True, stop=True)
                return mm

            pe.wait_ge(frec, 1)
            pe.wait_ge(fv_ev, 3)
            for j in range(4):
                mm = spread(ps[:, j // 2, j % 2 * SEQ:j % 2 * SEQ + SEQ], frms, 0, j, token_tiles(X0, 2))
                if j % 2:
                    mm.then_inc(fq_mm, 1)
            for j in range(4):
                if j:
                    pe.wait_ge(fox_done, (4, 8, 9)[j - 1])
                spread(ps[:, FK_BANKS[j], :], frms, 1, j, token_tiles(0, 3)).then_inc(fk_mm, 1)
            for hd in range(HEADS):
                if hd < 4:
                    pe.wait_ge(q_raw_ev, hd + 1)
                else:
                    pe.wait_ge(k_raw_ev, hd - 3)
                pe.matmul(ps[0:NOPE, HEAD_BANKS[hd % 4], 0:T], wuk[:, hd * NOPE:(hd + 1) * NOPE], ckvn, start=True, stop=True
                          ).then_inc(k_raw_mm, 1)
            pe.wait_ge(fox_done, 12)
            for t, (at, n) in enumerate(token_tiles(0, 3)):
                mm = pe.matmul(ps[0:n, t, :], ckvn[:, at:at + n], wuv, start=True, stop=True)
            mm.then_inc(vm_mm, 1)
            pe.wait_ge(fstat_sqrt, 2)
            pe.wait_ge(q_raw_ev, 4)
            one = C("mean_96")[0:QK, 0:1]
            for s, (at, n) in enumerate(token_tiles(0, 2)):
                for hd in range(HEADS):
                    pe.matmul(ps[0:n, 6, s * 8 + hd:s * 8 + hd + 1], qsq[0:QK, hd, at:at + n], one, start=True, stop=True)
            pe.wait_ge(k_raw_ev, HEADS)
            for s, (at, n) in enumerate(token_tiles(0, 3)):
                for hd in range(HEADS):
                    col = 16 + s * 8 + hd
                    mm = pe.matmul(ps[0:n, 6, col:col + 1], ksq[0:QK, hd, at:at + n], one, start=True, stop=True)
            mm.then_inc(mstat_mm, 1)
            for b in range(4):
                pe.matmul(ps[0:QK, HEAD_BANKS[b], :], C("rot")[0:QK, 0:QK],
                          qm[0:QK, 2 * b:2 * b + 2, :].rearrange("p a t -> p (a t)"), start=True, stop=True).then_inc(qrot_mm, 1)
            pe.wait_ge(mrec2, 1)
            pe.wait_ge(vm_ev, 3)

            def key_norm(hd):
                if hd >= 4:
                    pe.wait_ge(kn_done, hd - 3)
                for s, (at, n) in enumerate(token_tiles(0, 3)):
                    col = 16 + s * 8 + hd
                    mm = pe.matmul(ps[0:QK, NORM_BANKS[hd % 4], at:at + n], mrms[0:n, col:col + 1].broadcast_to([n, QK]),
                                   ident[0:n, 0:n], start=True, stop=True)
                mm.then_inc(kn_mm, 1)

            key_norm(0)
            for hd in range(HEADS):
                if hd + 1 < HEADS:
                    key_norm(hd + 1)
                pe.wait_ge(kn_done, hd + 1)
                pe.wait_ge(rope_step, 3 * hd + 1)
                pe.matmul(ps[0:QK, HEAD_BANKS[hd % 4], 0:T], C("rot")[0:QK, 0:QK], km[0:QK, hd, :], start=True, stop=True
                          ).then_inc(krot_mm, 1)
            pe.wait_ge(rope_step, 3 * (4 + HEADS))
            pe.wait_ge(cum_done, 3)
            pe.wait_ge(fox_done, 12)
            units = 2 * HEADS * TT

            def scores_of(n):
                hd, t = divmod(n, TT)
                keys_n = X0 + P * (t + 1)
                q = slice(t * P, (t + 1) * P)
                dst = ps[:, n % 3, 0:keys_n]
                if n >= 3:
                    pe.wait_ge(exp_done, n - 2)
                if hd < HEADS:
                    pe.matmul(dst, qm[0:QK, hd, q], km[0:QK, hd, 0:keys_n], start=True, stop=False)
                else:
                    f = hd - HEADS
                    pe.matmul(dst, fqz[:, f, q], fk[f // 2][:, 0:keys_n], start=True, stop=False)
                    pe.matmul(dst, cumz[:, X0 + t * P:X0 + (t + 1) * P], sel[:, f, 0:keys_n], start=False, stop=False)
                    pe.matmul(dst, sel[:, f, 0:P], ncumz[:, 0:keys_n], start=False, stop=False)
                pe.matmul(ps[:, n % 3, keys_n - P:keys_n], ident, C("neg_mask"), start=False, stop=True).then_inc(s_mm, 1)

            def turn_probs(n):
                t = n % TT
                full = t + 1
                bank = 3 + n % 2
                pe.wait_ge(p_done, n + 1)
                if n >= 2:
                    pe.wait_ge(pT_ev, n - 1)
                for s in range(full):
                    pe.transpose(ps[:, bank, s * P:(s + 1) * P], probs[:, n % 4, s * P:(s + 1) * P], ident)
                pe.transpose(ps[0:N_META, bank, full * P:(full + 1) * P],
                             probs[:, n % 4, full * P:full * P + N_META], ident).then_inc(pT_mm, 1)

            def weigh(n):
                hd, t = divmod(n, TT)
                full = t + 1
                v = (vM if hd < HEADS else vF)
                pair = (hd % HEADS) // 2
                c = slice(pair * P, pair * P + P)
                pe.wait_ge(pT_ev, n + 1)
                if n >= 2:
                    pe.wait_ge(o_ev, n - 1)
                for s in range(full):
                    pe.matmul(ps[:, 5 + n % 2, 0:P], v[:, s, c], probsT[:, n % 2, s, :], start=(s == 0), stop=False)
                pe.matmul(ps[:, 5 + n % 2, 0:P], v[0:N_META, full, c], probsT[0:N_META, n % 2, full, :],
                          start=False, stop=True).then_inc(o_mm, 1)

            scores_of(0)
            scores_of(1)
            for n in range(units):
                if n + 2 < units:
                    scores_of(n + 2)
                turn_probs(n)
                if n:
                    weigh(n - 1)
            weigh(units - 1)
            pe.wait_ge(o_ev, units)
            dense("w_out", oT, wo_mm)
            norm(2)
            pe.wait_ge(ada_step, KT * ADA_Q)
            flat = ada_acc.rearrange("p q w -> p (q w)")
            pe.wait_ge(h_done, 2 * KT)
            for m in range(48):
                mm = pe.matmul(ps[:, 7, 256 + m:257 + m], flat[:, m * P:(m + 1) * P], C("ones")[:, 0:1], start=True, stop=True)
            mm.then_inc(ada_mm, 1)
            ffn(1)
            norm(3)
            def z_tile(m, slot, e):
                for b in range(KT):
                    mm = pe.matmul(ps[:, Z_BANKS[m % 4], 0:SEQ], blk(slot, e * KT + b), u[:, b, 0:SEQ],
                                   start=(b == 0), stop=(b == KT - 1))
                mm.then_inc(z_mm, 1)

            def z_turn(n, first):
                for pair in range(4):
                    slot = (BASE["z"] + pair) % RING
                    turn0 = (BASE["z"] + pair) // RING
                    pe.wait_ge(landed[slot], n * 16 + (turn0 * 16 + 16))
                    for e in range(2):
                        m = 2 * pair + e
                        if not first or m >= 4:
                            pe.wait_ge(z_ev, n * KT + m - 3)
                        z_tile(m, slot, e)
                    pe.wait_ge(z_mm, n * KT + (2 * pair + 2))
                    pe.sem_inc(used, 1)

            pe.wait_ge(u_done, 4 * KT)
            z_turn(0, True)
            with pe.Fori(1, 4) as n:
                z_turn(n, False)
            for p in range(4):
                piece = BASE["zi"] + p
                slot = piece % RING
                half = p // 2
                pe.wait_ge(landed[slot], piece // RING * 16 + 16)
                for b in range(4):
                    k = (p % 2) * 4 + b
                    for t in range(TT):
                        mm = pe.matmul(ps[:, t * 2 + half, :], u[:, k, t * P:(t + 1) * P], ring[:, slot, b * 512:(b + 1) * 512],
                                       start=(k == 0), stop=(k == KT - 1))
                if p < 3:
                    mm.then_inc(used, 1)
                else:
                    mm.then_inc(zi_mm, 1)
                    pe.wait_ge(zi_mm, 1)
                    pe.sem_inc(used, 1)

            def gate_piece(p):
                piece = BASE["z_gate"] + p
                slot = piece % RING
                pe.wait_ge(landed[slot], piece // RING * 16 + 16)
                for e in range(2):
                    m = 4 * KT + 2 * p + e
                    pe.wait_ge(z_ev, m - 3)
                    z_tile(m, slot, e)
                pe.wait_ge(z_mm, 4 * KT + 2 * p + 2)
                pe.sem_inc(used, 1)

            def level(n):
                pe.wait_ge(lev_in, 2 * n + 1)
                if n >= 2:
                    pe.wait_ge(lev_out, n)
                kk = k_even[:, n % 2] if n else key
                bank = LEVEL_BANKS[n % 2]
                for hd in range(HEADS):
                    if LEVELS[n] < P:
                        for half in range(TT):
                            at = hd * TT + half
                            mm = pe.matmul(ps[:, bank + at // 8, at % 8 * HD:at % 8 * HD + HD], kk[:, hd, half * P:half * P + P],
                                           q_odd[:, n % 2, at * HD:at * HD + HD], start=True, stop=True)
                    else:
                        mm = pe.matmul(ps[:, bank + hd // 4, hd % 4 * P:hd % 4 * P + P], kk[:, hd, 0:P],
                                       q_odd[:, n % 2, hd * P:hd * P + P], start=True, stop=True)
                mm.then_inc(lev_mm, 1)

            gate_piece(0)
            pe.wait_ge(zi_ev, 4)
            for m in range(KT):
                pe.wait_ge(conv_step, (CONV_K - 1) * KT + m + 1)
                mm = pe.matmul(ps[:, 0, 0:SEQ], C("mean_d"), z[:, 0, m, :], start=(m == 0), stop=(m == KT - 1))
            mm.then_inc(ln_mm, 1)
            pe.wait_ge(qk_done, 1)
            for hd in range(HEADS):
                for t in range(TT):
                    mm = pe.matmul(ps[:, 1, hd * TT + t:hd * TT + t + 1], qk[:, hd, t * P:(t + 1) * P], C("ones")[:, 0:1],
                                   start=True, stop=True)
            mm.then_inc(diag_mm, 1)
            pe.wait_ge(f_done, KT + 1)
            level(0)
            gate_piece(1)
            pe.wait_ge(ln_act, 1)
            for m in range(KT):
                mm = pe.matmul(ps[:, 0, 0:SEQ], C("mean_d"), sq2[:, m, :], start=(m == 0), stop=(m == KT - 1))
            mm.then_inc(ln_mm, 1)
            gate_piece(2)
            pe.wait_ge(ln_act, 2)
            pe.wait_ge(lev_out, 1)
            for n in range(1, len(LEVELS)):
                level(n)
                gate_piece(n + 2)
            pe.wait_ge(lev_out, len(LEVELS) + 1)
            for hd in range(HEADS):
                c = slice(hd * P, hd * P + P)
                at = hd % 2 * SEQ
                pe.matmul(ps[:, hd // 2, at:at + P], zi[:, 0, c], AT[:, hd, 0, :], start=True, stop=True)
                pe.matmul(ps[:, hd // 2, at + P:at + 2 * P], zi[:, 0, c], AT[:, hd, 2, :], start=True, stop=False)
                mm = pe.matmul(ps[:, hd // 2, at + P:at + 2 * P], zi[:, 1, c], AT[:, hd, 1, :], start=False, stop=True)
                if hd % 2:
                    mm.then_inc(oh_mm, 1)
            gate_piece(10)
            pe.wait_ge(oh_ev, 8)
            for t in range(TT):
                for hd in range(HEADS):
                    mm = pe.matmul(ps[:, 0, t * HEADS + hd:t * HEADS + hd + 1], sq2[:, hd, t * P:(t + 1) * P],
                                   C("mean_128")[:, 0:1], start=True, stop=True)
            mm.then_inc(on_mm, 1)
            gate_piece(11)

            def dense2(name, first, rhs, ready):
                for p in range(4):
                    piece = BASE[name] + p
                    slot = piece % RING
                    pe.wait_ge(landed[slot], piece // RING * 16 + 16)
                    for e in range(2):
                        m = 2 * p + e
                        if first + m < 4:
                            pe.wait_ge(z_ev, 7 * KT - 3 + m)
                        elif first < 2 * KT or m < 4:
                            pe.wait_ge(dense_ev, first + m - 3)
                        else:
                            pe.wait_ge(h_done, 3 * KT + m - 3)
                        for b in range(KT):
                            if m == 0:
                                ready(b)
                            mm = pe.matmul(ps[:, Z_BANKS[m % 4], 0:SEQ], blk(slot, e * KT + b), rhs[:, b, :],
                                           start=(b == 0), stop=(b == KT - 1))
                        mm.then_inc(dense_mm, 1)
                    if name == "w_b" and p == 0:
                        pe.wait_ge(on_rec, 1)
                        for hd in range(HEADS):
                            for t in range(TT):
                                mm = pe.matmul(ps[:, hd // 2, hd % 2 * SEQ + t * P:hd % 2 * SEQ + t * P + P],
                                               o_rms[:, t * HEADS + hd:t * HEADS + hd + 1].broadcast_to([P, P]), ident,
                                               start=True, stop=True)
                            if hd % 2:
                                mm.then_inc(on_mm, 1)
                    pe.wait_ge(dense_mm, first + 2 * p + 2)
                    pe.sem_inc(used, 1)

            dense2("w_b", 0, z[:, 0], lambda b: pe.wait_ge(ln_act, 2 + b + 1))
            dense2("w_a", KT, o_h, lambda b: pe.wait_ge(o_done, b + 1))
            dense2("w_out_2", 2 * KT, z[:, 5], lambda b: pe.wait_ge(merged, b + 1))
            norm(4)
            pe.wait_ge(u_done, 5 * KT)

            def tok_turn(n):
                t, half = n // 2 % 2, n % 2
                if n >= 2:
                    pe.wait_ge(tok_ev, n - 1)
                for i in range(4):
                    k = half * 4 + i
                    x = u[:, k, t * P:(t + 1) * P] if n < 4 else h[:, k, X0 + t * P:X0 + (t + 1) * P]
                    mm = pe.transpose(ps[:, 6 + n % 2, i * P:(i + 1) * P], x, ident)
                mm.then_inc(tok_mm, 1)

            for hd in range(HEADS):
                piece = BASE["wq"] + hd
                slot = piece % RING
                pe.wait_ge(landed[slot], piece // RING * 16 + 16)
                for e in range(2):
                    if hd >= 2:
                        pe.wait_ge(q_ev, (hd - 2) * 2 + e + 1)
                    for b in range(KT):
                        mm = pe.matmul(ps[:, hd % 2 * 2 + e, 0:SEQ], blk(slot, e * KT + b), u[:, b, 0:SEQ],
                                       start=(b == 0), stop=(b == KT - 1))
                    mm.then_inc(q_mm, 1)
                if hd < HEADS - 1:
                    pe.wait_ge(q_mm, 2 * hd + 2)
                    pe.sem_inc(used, 1)
                if hd == 0:
                    tok_turn(0)
                    tok_turn(1)
                pe.wait_ge(q_ev, 2 * hd + 2)
                if hd >= 2:
                    pe.wait_ge(sc_ev, hd - 1)
                for t in range(TT):
                    for e in range(2):
                        mm = pe.matmul(ps[:, 4 + hd % 2, (t * 2 + e) * NKEYS:(t * 2 + e + 1) * NKEYS],
                                       qh[:, hd % 2, e, t * P:(t + 1) * P], keys[:, hd * 2 + e, :], start=True, stop=True)
                mm.then_inc(sc_mm, 1)
                if hd == 0:
                    tok_turn(2)
                    tok_turn(3)
            for n in range(4, 8):
                tok_turn(n)
            pe.wait_ge(q_ev, 2 * HEADS)
            for k in range(KT):
                mm = pe.matmul(ps[:, k // 4, k % 4 * P:k % 4 * P + P], ada[:, 40 + k:41 + k].broadcast_to([P, P]), ident,
                               start=True, stop=True)
            mm.then_inc(gain_mm, 1)


def _blocks(w):
    k, m = w.shape
    return w.reshape(k // P, P, m // P, P).transpose(0, 2, 1, 3)


def _pieces(blocks):
    n = blocks.shape[0]
    return blocks.reshape(n // BLOCKS, BLOCKS, P, P).transpose(0, 2, 1, 3).reshape(n // BLOCKS, P, PIECE)


def _by_output(w):
    b = _blocks(w)
    return _pieces(b.transpose(1, 0, 2, 3).reshape(-1, P, P))


def _by_input(w):
    return _pieces(_blocks(w).reshape(-1, P, P))


def _wide(w):
    k, m = w.shape
    b = w.reshape(k // P, P, m // 512, 4, P).transpose(2, 0, 3, 1, 4)
    return _pieces(b.reshape(-1, P, P))


def layout(x):
    f = {k: np.asarray(v) for k, v in x.items()}

    def ffn(n):
        g, up, dn = f[f"w{n}_gate"][0], f[f"w{n}_up"][0], f[f"w{n}_down"][0]
        gu = np.stack([_blocks(g).transpose(1, 0, 2, 3), _blocks(up).transpose(1, 0, 2, 3)], 1)
        return np.concatenate([_pieces(gu.reshape(-1, P, P)), _by_input(dn)])

    w_in = f["w_in"][0]
    misc = np.zeros((D, P), np.float32)
    misc[:, PE_ROW:PE_ROW + ROPE] = w_in[:, 384:416]
    misc[:, FL_ROW:FL_ROW + HEADS] = w_in[:, 1952:1960]
    w_proj = np.concatenate([w_in[:, 0:384], misc, w_in[:, 416:416 + 1024]], 1)
    zs = np.split(f["w_in_2"][0], 8, axis=1)
    zq, zf, zi, zg, zca, zcb, zga, zgb = zs
    stream = np.concatenate(
        [ffn(1), _by_output(w_proj), _wide(w_in[:, 1440:1952]), _by_output(f["w_out"][0]), ffn(2)]
        + [_by_output(w) for w in (zca, zcb, zf, zq)] + [_wide(zi)] + [_by_output(w) for w in (zg, zga, zgb)]
        + [_by_output(f[n][0]) for n in ("w_b_2", "w_a_2", "w_out_2", "peer_wq_2")])
    assert stream.shape == (N_PIECES, P, PIECE)
    ada = f["ada_w_2"][0].reshape(KT, P, ADA_Q, ADA_W).transpose(0, 2, 1, 3).reshape(KT * ADA_Q, P, ADA_W)
    cols = np.zeros((P, N_COLS), np.float32)

    def put(name, v):
        v = v.reshape(-1, P).T
        cols[:, COL[name]:COL[name] + v.shape[1]] = v

    for name, key in (("g_ffn1", "g_ffn1"), ("g_mix", "g_mix"), ("g_ffn2", "g_ffn2"), ("norm1", "norm1_g_2"),
                      ("hg_g", "hg_norm_g_2"), ("conv_b", "conv_b_2"), ("ln_g", "conv_ln_g_2"),
                      ("ln_b", "conv_ln_b_2"), ("norm2", "norm2_g_2"), ("c", "c_2"), ("ada_b", "ada_b_2"),
                      ("g_cq", "g_cq"), ("g_ckv", "g_ckv"), ("conv_w", "conv_w_2")):
        put(name, f[key])
    put("lb0", f["lb_logits_2"][0])
    put("lb1", f["lb_logits_2"][1])
    cols[0:QK, COL["g_q"]] = f["g_q_mla"][0]
    cols[0:QK, COL["g_k"]] = f["g_k_mla"][0]
    for e in range(2):
        cols[HD * e:HD * e + HD, COL["g_fq"]] = f["g_q_fox"][0]
        cols[HD * e:HD * e + HD, COL["g_fk"]] = f["g_k_fox"][0]
    cols[FL_ROW:FL_ROW + HEADS, COL["b_f"]] = f["b_forget"][0]
    wukv = f["w_ukv"][0].reshape(P, HEADS, NOPE + HD)
    con, sel, masks = constants()
    tokens = np.concatenate([f["meta_tokens"], f["x"][0]], 0)
    return {
        "x_t": tokens.T.reshape(KT, P, T).transpose(1, 0, 2),
        "stream": stream, "ada": ada, "cols": cols, "con": con, "sel": sel, "masks": masks,
        "wuq": f["w_uq"][0].reshape(2, P, HEADS * QK).transpose(1, 0, 2),
        "wuk": wukv[:, :, :NOPE].reshape(P, HEADS * NOPE),
        "wuv": wukv[:, :, NOPE:].reshape(P, HEADS * HD),
        "keys": f["peer_keys_2"][0].reshape(2 * HEADS, NKEYS, P).transpose(2, 0, 1),
        "peer_u": f["peer_u_2"][0], "peer_v": f["peer_v_2"][0], "final_g": f["final_g_2"],
    }


def kernel(**inputs):
    import concourse.bacc as bacc
    from concourse.bass_utils import run_bass_kernel_spmd

    nc = bacc.Bacc("TRN2", target_bir_lowering=False, num_devices=1)
    arrays = {f"in_{k}": np.ascontiguousarray(v) for k, v in layout(inputs).items()}
    args = {k[3:]: nc.dram_tensor(k, v.shape, mybir.dt.from_np(v.dtype), kind="ExternalInput").ap()
            for k, v in arrays.items()}
    out = nc.dram_tensor("out", (1, SEQ, D), F32, kind="ExternalOutput").ap()
    program(nc, args, out)
    r = run_bass_kernel_spmd(nc, [arrays], core_ids=[0])
    return r.results[0]["out"]
```

```python
from contextlib import ExitStack

import numpy as np

import concourse.bass as bass
from concourse import mybir

F32 = mybir.dt.float32
F32R = mybir.dt.float32r
U32 = mybir.dt.uint32
I32 = mybir.dt.int32
ACT = mybir.ActivationFunctionType
ALU = mybir.AluOpType
AX_X = mybir.AxisListType.X

P = 128
D = 1024
KT = D // P
SEQ = 256
N_META = 16
T = N_META + SEQ
X0 = N_META
TT = SEQ // P
D_FF = 2816
FT = D_FF // P
EPS = 1e-6
HEADS = 8
QK = 96
NOPE = 64
ROPE = 32
HD = 64
PE_ROW = 64
FL_ROW = 96
CONV_K = 31
PAD = CONV_K - 1
TOPK = 16
NKEYS = 128
SLOTS = HEADS * TOPK
RING = 4
BLOCKS = 16
PIECE = BLOCKS * P
HALF = PIECE // 2
ADA_Q = 4
ADA_W = 6 * D // ADA_Q
GR = 16
CHOOSE_STEPS = 43
FOX_SCALE = HD ** -0.5
MLA_SCALE = QK ** -0.5
NEG = -1e30

FFN_P = FT + FT * KT // BLOCKS
PARTS = [("ffn1", FFN_P), ("w_in", 8), ("w_out", 4), ("ffn2", FFN_P), ("z", 16), ("zi", 4), ("z_gate", 12),
         ("w_b", 4), ("w_a", 4), ("w_out_2", 4), ("wq", 8)]
BASE = {}
_at = 0
for _name, _n in PARTS:
    BASE[_name] = _at
    _at += _n
N_PIECES = _at

VECS = [("g_ffn1", 8), ("g_mix", 8), ("g_ffn2", 8), ("norm1", 8), ("lb0", 8), ("lb1", 8), ("hg_g", 8),
        ("conv_b", 8), ("ln_g", 8), ("ln_b", 8), ("norm2", 8), ("c", 8), ("ada_b", 48), ("g_cq", 2),
        ("g_ckv", 1), ("g_q", 1), ("g_k", 1), ("g_fq", 1), ("g_fk", 1), ("b_f", 1), ("conv_w", 8 * CONV_K)]
COL = {}
_at = 0
for _name, _n in VECS:
    COL[_name] = _at
    _at += _n
N_COLS = _at

CONSTS = [("ident", P), ("mean_d", P), ("mean_256", P), ("mean_128", P), ("mean_64", P), ("mean_96", P),
          ("ones", P), ("rot", P), ("cos", T), ("sin", T), ("neg_mask", P), ("iota", TOPK), ("sel", HEADS)]
CON = {}
_at = 0
for _name, _n in CONSTS:
    CON[_name] = (_at, _n)
    _at += _n
N_CONSTS = _at
LEVELS = [1, 2, 4, 8, 16, 32, 64, P]


def constants():
    c = np.zeros((P, N_CONSTS), np.float32)

    def put(name, a):
        at = CON[name][0]
        c[:a.shape[0], at:at + a.shape[1]] = a

    put("ident", np.eye(P, dtype=np.float32))
    for name, n in (("mean_d", D), ("mean_256", 256), ("mean_128", 128)):
        put(name, np.full((P, P), 1.0 / n, np.float32))
    put("mean_96", np.full((QK, QK), 1.0 / QK, np.float32))
    put("mean_64", np.kron(np.eye(2), np.full((HD, HD), 1.0 / HD)).astype(np.float32))
    put("ones", np.ones((P, P), np.float32))
    half = ROPE // 2
    rot = np.zeros((QK, QK), np.float32)
    for i in range(half):
        rot[NOPE + half + i, NOPE + i] = -1.0
        rot[NOPE + i, NOPE + half + i] = 1.0
    put("rot", rot)
    freq = (1.0 / (np.float32(10000.0) ** (np.arange(half, dtype=np.float32) / np.float32(half)))).astype(np.float32)
    ang = (np.arange(T, dtype=np.float32)[None, :] * freq[:, None]).astype(np.float32).astype(np.float64)
    cos = np.ones((QK, T), np.float32)
    sin = np.zeros((QK, T), np.float32)
    for at in (NOPE, NOPE + half):
        cos[at:at + half] = np.cos(ang)
        sin[at:at + half] = np.sin(ang)
    put("cos", cos)
    put("sin", sin)
    put("neg_mask", np.where(np.arange(P)[None, :] > np.arange(P)[:, None], NEG, 0.0).astype(np.float32))
    sel = np.zeros((P, HEADS), np.float32)
    for h in range(HEADS):
        sel[FL_ROW + h, h] = 1.0 / FOX_SCALE
    put("sel", sel)
    put("iota", np.broadcast_to(np.arange(TOPK, dtype=np.float32), (P, TOPK)))
    masks = np.zeros((P, len(LEVELS) - 1, 2, HD), np.uint32)
    s = np.arange(P)[:, None]
    for n, b in enumerate(LEVELS[:-1]):
        t = np.arange(P).reshape(-1, 2, b)[:, 1].reshape(1, HD)
        masks[:, n] = (s // b == t // b - 1)[:, None, :]
    return c, masks.reshape(P, -1)


def runs(base, n, peel=0):
    at, out = base, []
    while at < base + n:
        left = base + n - at
        if at % RING == 0 and left >= 2 * RING and at - base >= peel:
            out.append((at, left // RING))
            at += left // RING * RING
        else:
            out.append((at, 0))
            at += 1
    return out


def each_piece(eng, base, n, body, peel=0):
    for at, turns in runs(base, n, peel):
        if not turns:
            body(at, at % RING, at // RING)
            continue
        with eng.Fori(0, turns) as i:
            for slot in range(RING):
                body(i * RING + (at + slot), slot, i + at // RING)


def each_turn(eng, n, body):
    with eng.Fori(0, n) as i:
        body(i)


def program(nc, a, out):
    ctx = ExitStack()
    with ctx:
        def sb(name, shape, dt=F32):
            return ctx.enter_context(nc.sbuf_tensor(name, shape, dt))

        def sem(name):
            return ctx.enter_context(nc.semaphore(name))

        ps = ctx.enter_context(nc.psum_tensor("ps", [P, 8, 512], F32))
        ring = sb("ring", [P, RING, PIECE])
        h = sb("h", [P, KT, T])
        u_all = sb("u", [P, KT * T])
        u = u_all[:, :].rearrange("p (k t) -> p k t", t=T)
        cols = sb("cols", [P, N_COLS])
        con = sb("con", [P, N_CONSTS])
        masks = sb("masks", [P, (len(LEVELS) - 1) * P], U32)
        rstd = sb("rstd", [P, T])
        silu_c = sb("silu_c", [P, KT])
        ada = sb("ada", [P, 48])
        lb = sb("lb", [P, 6, KT])
        gain1 = sb("gain1", [P, KT])
        gain2 = sb("gain2", [P, KT])
        eps = sb("eps", [P, 1])
        ARENA = 34816
        arena_at = -(-nc.sbuf_base // 32) * 32
        arena = sb("arena", [P, ARENA])
        spot = [0]

        def place(at=None):
            if at is not None:
                spot[0] = at

        def view(*shape):
            n = int(np.prod(shape))
            assert spot[0] + n <= ARENA, (spot[0], n)
            v = arena[:, spot[0]:spot[0] + n]
            spot[0] += n
            names = "abcd"[:len(shape)]
            if len(shape) == 1:
                return v
            return v.rearrange(f"p ({' '.join(names)}) -> p {' '.join(names)}",
                               **dict(zip(names, shape)))

        def parts(name, *shape):
            t = nc.alloc_sbuf_tensor_at(name, [P] + list(shape), F32R, offset=arena_at + 4 * spot[0])
            view(*shape)
            return t[:, :, :], t[:, :, :].bitcast(F32)

        def C(name):
            at, n = CON[name]
            return con[:, at:at + n]

        def V(name, k=0, n=1):
            return cols[:, COL[name] + k:COL[name] + k + n]

        ident = C("ident")

        place(0)
        ada_acc = view(ADA_Q, ADA_W)
        ada_ring = view(2, ADA_W)
        phase = spot[0]
        glu_hi, glu_hi_f = parts("glu_hi", FT, T)
        split = spot[0]
        w_hi, w_hi_f = parts("w_hi", 4, HALF)
        w_lo, _ = parts("w_lo", 4, HALF)
        u_hi, u_hi_f = parts("u_hi", KT, T)
        u_lo, _ = parts("u_lo", KT, T)
        parts_end = spot[0]
        glu_lo, _ = parts("glu_lo", FT, T)
        act_g = view(RING, T)
        act_end = spot[0]
        place(phase)
        sq = view(KT, T)
        praw = view(12, T)
        assert spot[0] <= split, "the second feed-forward's first weights are split while the heads' outputs are used"
        lat_sq = act_g
        place(parts_end)
        wuq = view(2, HEADS * QK)
        wuk = view(HEADS * NOPE)
        wuv = view(HEADS * HD)
        lat_rms = view(2, T)
        cqn = view(2, SEQ)
        ckvn = view(T)
        cumz = view(T)
        ncumz = view(T)
        logf = view(4, T)
        pe_sq = view(T)
        assert spot[0] <= act_end - RING * T
        place(split)
        fqz = view(HEADS, SEQ)
        fk = view(HEADS // 2, T)
        vM = view(3, HEADS * HD)
        vF = view(3, HEADS * HD)
        qm = view(HEADS, SEQ)
        km = view(HEADS, T)
        turned = view(2, T)
        frms = view(40)
        mrms = view(40)
        qscale = view(16)
        mx = view(64)
        nmx = view(64)
        rsum = view(64)
        rinv = view(64)
        assert spot[0] <= parts_end
        probs = act_g
        qsq = sq[:, :, 0:SEQ]
        ksq = praw[:, 0:HEADS, :]
        probsT = sq[:, 2:8, 0:P].rearrange("p (a b) t -> p a b t", a=2)
        oT = praw[:, 0:KT, 0:SEQ]

        place(0)
        z = view(4, KT, SEQ)
        pad_glu = view(KT, PAD + SEQ)
        zi_at = spot[0]
        zi = view(TT, D)
        suf = view(KT, SEQ)
        pre = z[:, 2]
        key = z[:, 1]
        gates = view(3, KT, SEQ)
        assert spot[0] - 3 * KT * SEQ >= phase
        q_odd_at = spot[0]
        q_odd = view(2, KT * P)
        k_even_at = spot[0]
        k_even = view(2, KT, SEQ)
        AT_at = spot[0]
        AT = view(HEADS, 3, P)
        sq2 = view(KT, SEQ)
        qk = sq2
        o_rms = view(2 * HEADS)
        o_h = suf
        place(KT * SEQ)
        late_hi, late_hi_f = parts("late_hi", 4, HALF)
        late_lo, _ = parts("late_lo", 4, HALF)
        assert spot[0] <= zi_at
        place(zi_at)
        m_hi, m_hi_f = parts("m_hi", KT, SEQ)
        m_lo, _ = parts("m_lo", KT, SEQ)
        place(q_odd_at)
        o_hi, o_hi_f = parts("o_hi", KT, SEQ)
        place(k_even_at)
        cv_hi, cv_hi_f = parts("cv_hi", KT, SEQ)
        cv_lo, _ = parts("cv_lo", KT, SEQ)
        place(AT_at)
        o_lo, _ = parts("o_lo", KT, SEQ)
        place(0)
        rows = view(GR, D)
        hf = view(TT, D)
        h_tok = view(TT, D)
        acc = view(TT, D)
        y_gain = view(D)
        final_g = view(D)
        qh = y_gain.rearrange("p (a e t) -> p a e t", a=2, e=2)
        scores = view(HEADS, TT, 2, NKEYS)
        left = view(TT, 2, NKEYS)
        left2 = left.rearrange("p t e n -> p t (e n)")
        cand = view(TT, TOPK * TOPK)
        onehot = cand.rearrange("p t (i j) -> p t i j", i=TOPK)
        top = view(TT, 2, TOPK)
        top_i = view(TT, 2, TOPK)
        pos = view(2, TT, TOPK)
        part_i = view(2, TT, TOPK)
        own_scores = view(TT, 2, NKEYS)
        own_best = view(TT, TOPK)
        own_gate = view(TT, TOPK)
        gate_s = view(TT)
        gate = view(TT, TOPK)
        dots = view(TT, TOPK)
        wts = view(TT, TOPK)
        fin = view(16)
        assert spot[0] <= act_end - 2 * HEADS * NKEYS
        place(act_end - 2 * HEADS * NKEYS)
        keys = view(2 * HEADS, NKEYS)
        top_u = sb("top_u", [P, TT, 2, TOPK], U32)
        pos_u = sb("pos_u", [P, TT, TOPK], U32)
        part_u = sb("part_u", [P, 2, TT, TOPK], U32)
        eidx = sb("eidx", [P, HEADS * TT * TOPK], U32)
        stage = sb("stage", [P, 2, 8], U32)

        landed = [sem(f"weights_landed{i}") for i in range(RING)]
        used = sem("weights_used")
        x_in = sem("x_in")
        cols_in = sem("cols_in")
        con_in = sem("con_in")
        mask_in = sem("mask_in")
        small_in = sem("small_in")
        final_in = sem("final_in")
        ada_in = [sem(f"ada_in{i}") for i in range(2)]
        ada_step = sem("ada_step")
        ada_mm = sem("ada_mm")
        ada_done = sem("ada_done")
        set_up = sem("set_up")
        lb_e = sem("lb_e")
        lb_step = sem("lb_step")
        silu_c_done = sem("silu_c_done")
        sq_done = sem("sq_done")
        ss_done = sem("ss_done")
        sqrt_done = sem("sqrt_done")
        rstd_done = sem("rstd_done")
        u_scaled = sem("u_scaled")
        u_done = sem("u_done")
        hi_done = sem("hi_done")
        lo_done = sem("lo_done")
        half_used = sem("half_used")
        u_hi_done = sem("u_hi_done")
        u_lo_done = sem("u_lo_done")
        glu_made = sem("glu_made")
        glu_high = sem("glu_high")
        keys_in = sem("keys_in")
        silu_done = sem("silu_done")
        glu_done = sem("glu_done")
        down_done = sem("down_done")
        h_done = sem("h_done")
        proj_ev = sem("proj_ev")
        fv_ev = sem("fv_ev")
        lat_mm = sem("lat_mm")
        lat_sqrt = sem("lat_sqrt")
        mrec_done = sem("mrec_done")
        mstep = sem("mstep")
        fstat_mm = sem("fstat_mm")
        fstat_sqrt = sem("fstat_sqrt")
        frec = sem("frec")
        fq_mm = sem("fq_mm")
        fk_mm = sem("fk_mm")
        mstat_mm = sem("mstat_mm")
        mstat_sqrt = sem("mstat_sqrt")
        mrec2 = sem("mrec2")
        q_raw_mm = sem("q_raw_mm")
        q_raw_ev = sem("q_raw_ev")
        k_raw_mm = sem("k_raw_mm")
        k_raw_ev = sem("k_raw_ev")
        qrot_mm = sem("qrot_mm")
        krot_mm = sem("krot_mm")
        kn_mm = sem("kn_mm")
        kn_done = sem("kn_done")
        lat_done = sem("lat_done")
        fox_done = sem("fox_done")
        z_done = sem("z_done")
        f_exp = sem("f_exp")
        f_ln = sem("f_ln")
        cum_done = sem("cum_done")
        kpe_done = sem("kpe_done")
        rope_step = sem("rope_step")
        vm_mm = sem("vm_mm")
        vm_ev = sem("vm_ev")
        s_mm = sem("s_mm")
        max_done = sem("max_done")
        nmax_done = sem("nmax_done")
        exp_done = sem("exp_done")
        rinv_done = sem("rinv_done")
        p_done = sem("p_done")
        pT_mm = sem("pT_mm")
        pT_ev = sem("pT_ev")
        o_mm = sem("o_mm")
        o_ev = sem("o_ev")
        wo_mm = sem("wo_mm")
        zi_mm = sem("zi_mm")
        zi_ev = sem("zi_ev")
        z_mm = sem("z_mm")
        z_ev = sem("z_ev")
        sig_done = sem("sig_done")
        lb_done = sem("lb_done")
        f_done = sem("f_done")
        suf_set = sem("suf_set")
        qk_done = sem("qk_done")
        diag_mm = sem("diag_mm")
        pad_done = sem("pad_done")
        cv_step = sem("cv_step")
        on_rec = sem("on_rec")
        o_step = sem("o_step")
        o_done = sem("o_done")
        merged = sem("merged")
        conv_step = sem("conv_step")
        ln_mm = sem("ln_mm")
        ln_act = sem("ln_act")
        lev_mm = sem("lev_mm")
        lev_in = sem("lev_in")
        lev_out = sem("lev_out")
        lev_up = sem("lev_up")
        oh_mm = sem("oh_mm")
        oh_ev = sem("oh_ev")
        on_mm = sem("on_mm")
        on_act = sem("on_act")
        cv_hi_done = sem("cv_hi_done")
        cv_lo_done = sem("cv_lo_done")
        o_hi_done = sem("o_hi_done")
        o_lo_done = sem("o_lo_done")
        m_hi_done = sem("m_hi_done")
        m_lo_done = sem("m_lo_done")
        dense_ev = sem("dense_ev")
        q_mm = sem("q_mm")
        q_ev = sem("q_ev")
        tok_mm = sem("tok_mm")
        tok_ev = sem("tok_ev")
        sc_mm = sem("sc_mm")
        sc_ev = sem("sc_ev")
        tk = sem("topk_step")
        choose_passed = sem("choose_passed")
        idx_done = sem("idx_done")
        gate_sub = sem("gate_sub")
        gate_e = sem("gate_e")
        gate_done = sem("gate_done")
        rows_free = sem("rows_free")
        staged = sem("staged")
        idx_staged = sem("idx_staged")
        row_in = [sem(f"row_in{i}") for i in range(GR)]
        row_used = sem("row_used")
        gelu_done = sem("gelu_done")
        w_done = sem("w_done")
        fin_step = sem("fin_step")
        fin_act = sem("fin_act")
        gain_mm = sem("gain_mm")
        out_done = sem("out_done")
        assert N_PIECES % RING == 2

        block = ctx.enter_context(nc.Block())
        xc = slice(X0, T)
        PROJ_BANKS = 6
        HEAD_BANKS = [3, 4, 5, 7]
        FK_BANKS = [2, 0, 1, 2]
        NORM_BANKS = [0, 1, 2, 6]
        GATES = [ACT.Silu, ACT.Sigmoid, ACT.Sigmoid]
        Z_BANKS = [4, 5, 6, 7]
        LEVEL_BANKS = [2, 0]

        GAPS = [0]
        GAPS.append(BASE["ffn2"] - BASE["w_out"])
        GAPS.append(GAPS[1] + BASE["w_b"] - (BASE["z"] + 8))

        def half_number(part, piece, e):
            return (piece - GAPS[part]) * 2 + e

        def w_parts(part):
            return (late_hi, late_lo, late_hi_f) if part == 2 else (w_hi, w_lo, w_hi_f)

        def q_scale(hd, t):
            return qscale[:, t * HEADS + hd:t * HEADS + hd + 1] if hd < HEADS else FOX_SCALE

        NORM_COLS = [slice(0, T), slice(0, T), xc, xc, xc]

        @block.sync
        def _(sp):
            sp.dma_start(h[:, :, :], a["x_t"]).then_inc(x_in, 16)

            def load(piece, slot):
                sp.wait_ge(used, piece - (RING - 1))
                src = a["stream"][piece] if isinstance(piece, int) else \
                    a["stream"][bass.ds(piece, 1)].rearrange("o p m -> p (o m)")
                sp.dma_start(ring[:, slot, :], src).then_inc(landed[slot], 16)

            def load_ada(kt, q):
                sp.wait_ge(ada_step, kt * ADA_Q + (q + 3))
                n = kt * ADA_Q + q
                src = a["ada"][n] if isinstance(n, int) else a["ada"][bass.ds(n, 1)].rearrange("o p w -> p (o w)")
                sp.dma_start(ada_ring[:, q % 2, :], src).then_inc(ada_in[q % 2], 16)

            def load_pieces(first, end):
                each_piece(sp, first, end - first, lambda piece, slot, turn: load(piece, slot))

            for n in range(RING):
                sp.dma_start(ring[:, n, :], a["stream"][n]).then_inc(landed[n], 16)
            with sp.Fori(0, KT // 2) as i:
                for j in range(2 * RING):
                    load(i * (2 * RING) + (RING + j), j % RING)
                    if j % 2:
                        load_ada(i, j // 2)
            load_pieces(RING + KT // 2 * 2 * RING, BASE["ffn2"])
            with sp.Fori(KT // 2, KT) as kt:
                for q in range(ADA_Q):
                    load_ada(kt, q)
            load_pieces(BASE["ffn2"], N_PIECES)
            sp.wait_ge(fin_step, 2 * 6)
            for t in range(TT):
                sp.dma_start(out[0, t * P:(t + 1) * P, :], acc[:, t, :]).then_inc(out_done, 16)
            sp.wait_ge(out_done, 16 * TT)

        @block.gpsimd
        def _(pool):
            pool.memset(eps[:, :], EPS).then_inc(set_up, 1)

            for q in range(ADA_Q):
                pool.memset(ada_acc[:, q, :], 0.0).then_inc(ada_step, 1)

            def low(k, piece, slot, e):
                half = slot % 2 * 2 + e
                pool.wait_ge(hi_done, half_number(k, piece, e + 1))
                if e:
                    pool.wait_ge(lo_done, piece + (1 - GAPS[k]))
                    if isinstance(piece, int) and piece in (BASE["ffn2"], BASE["w_b"]):
                        pool.wait_ge(used, piece)
                _, lo, hi = w_parts(k)
                pool.tensor_tensor(lo[:, half, :], ring[:, slot, e * HALF:(e + 1) * HALF], hi[:, half, :], ALU.subtract
                                   ).then_inc(used if e else lo_done, 1)

            each_piece(pool, 0, FFN_P + 2, lambda piece, slot, turn: low(0, piece, slot, 1))
            for piece in range(BASE["w_in"] + 2, BASE["w_out"]):
                for e in range(2):
                    low(0, piece, piece % RING, e)
            each_piece(pool, BASE["ffn2"], FFN_P + 8, lambda piece, slot, turn: low(1, piece, slot, 1), peel=1)

            pool.wait_ge(h_done, 3 * KT)
            pool.memset(suf[:, :, :], 1.0).then_inc(suf_set, 1)
            pool.wait_ge(z_ev, 4 * KT)
            pool.wait_ge(f_done, KT + 1)
            pool.tensor_tensor(qk, z[:, 3], key, ALU.mult).then_inc(qk_done, 1)
            for piece in range(BASE["w_b"], BASE["wq"]):
                for e in range(2):
                    low(2, piece, piece % RING, e)

            def gather(table, n, slot0):
                par = slot0[1]
                if not isinstance(n, int) or n >= 2:
                    pool.wait_ge(row_used, n * 8 - GR + 8)
                    pool.sem_inc(rows_free, 1)
                pool.tensor_copy(stage[:, par, :], eidx[:, bass.ds(slot0[0], 8)]).then_inc(staged, 1)
                pool.wait_ge(staged, n + 1)
                pool.sem_inc(idx_staged, 1)
                for j in range(8):
                    r = par * 8 + j
                    pool.indirect_dma_start(rows[:, r, :], None, table,
                                            bass.IndirectOffsetOnAxis(ap=stage[:, par, j:j + 1], axis=0)
                                            ).then_inc(row_in[r], 16)

            def gather_head(hd):
                pool.wait_ge(idx_done, hd + 1)
                for g in range(4 * TT):
                    table = a["peer_u"] if g < 2 * TT else a["peer_v"]
                    gather(table, hd * (4 * TT) + g, (hd * (TT * TOPK) + g % (2 * TT) * 8, g % 2))

            gather_head(0)
            with pool.Fori(1, HEADS) as hd:
                gather_head(hd)

        @block.scalar
        def _(act):
            act.dma_start(con[:, :], a["con"]).then_inc(con_in, 16)
            act.dma_start(cols[:, :], a["cols"]).then_inc(cols_in, 16)

            def high(k, piece, slot, turn, e):
                n = half_number(k, piece, e)
                if e == 0:
                    act.wait_ge(landed[slot], turn * 16 + 16)
                if not isinstance(n, int) or n >= 4:
                    act.wait_ge(half_used, n - 3)
                half = slot % 2 * 2 + e
                act.activation(w_parts(k)[0][:, half, :], ring[:, slot, e * HALF:(e + 1) * HALF], ACT.Copy).then_inc(hi_done, 1)

            def high2(k, piece, slot, turn):
                for e in range(2):
                    high(k, piece + 2, (slot + 2) % RING, turn + (slot + 2) // RING, e)

            def u_high(n):
                w = NORM_COLS[n].stop - NORM_COLS[n].start
                for k in range(KT):
                    act.wait_ge(u_done, KT * n + k + 1)
                    act.activation(u_hi[:, k, 0:w], u[:, k, 0:w], ACT.Copy).then_inc(u_hi_done, 1)

            def norm(n, between=(), before=()):
                c = NORM_COLS[n]
                w = c.stop - c.start
                if n == 0:
                    act.wait_ge(x_in, 16)
                    act.wait_ge(set_up, 1)
                dst = sq if n < 3 else sq2
                for k in range(KT):
                    if k < len(before):
                        before[k]()
                    if n:
                        act.wait_ge(h_done, KT * (n - 1) + k + 1)
                    act.activation(dst[:, k, 0:w], h[:, k, c], ACT.Square).then_inc(sq_done, 1)
                for part in between:
                    part()
                act.wait_ge(ss_done, n + 1)
                act.activation(rstd[:, 0:w], ps[:, 0, 0:w], ACT.Sqrt, bias=eps[:, :]).then_inc(sqrt_done, 1)

            def ffn(k):
                base = BASE["ffn2" if k else "ffn1"]
                w = SEQ if k else T

                def body(piece, slot, turn):
                    act.wait_ge(half_used, half_number(k, piece, 1))
                    act.activation(act_g[:, slot, 0:w], ps[:, 2 * slot, 0:w], ACT.Silu).then_inc(silu_done, 1)
                    high2(k, piece, slot, turn)

                each_piece(act, base, FT, body, peel=0 if k else RING)
                each_piece(act, base + FT, FFN_P - FT - 1, lambda *piece: high2(k, *piece))

            def attn_evac(act, n):
                hd, t = divmod(n, TT)
                half = HD * (hd % 2)
                act.wait_ge(pT_mm, n + 1)
                if n >= 2:
                    act.wait_ge(o_mm, n - 1)
                full = t + 1
                bank = 3 + n % 2
                act.activation(probsT[:, n % 2, 0:full, :],
                               ps[:, bank, 0:full * P].rearrange("p (a b) -> p a b", b=P), ACT.Copy)
                act.activation(probsT[0:N_META, n % 2, full, :], ps[0:N_META, bank, full * P:full * P + P], ACT.Copy
                               ).then_inc(pT_ev, 1)
                act.wait_ge(o_mm, n + 1)
                act.activation(oT[half:half + HD, hd // 2, t * P:(t + 1) * P],
                               ps[half:half + HD, 5 + n % 2, 0:P], ACT.Copy).then_inc(o_ev, 1)

            norm(0, [lambda: high(0, 0, 0, 0, 0), lambda: high(0, 0, 0, 0, 1)])
            u_high(0)
            for e in range(2):
                high(0, 1, 1, 0, e)
            act.wait_ge(cols_in, 16)
            act.activation(silu_c[:, :], V("c", 0, KT), ACT.Silu).then_inc(silu_c_done, 1)
            ffn(0)
            norm(1, [lambda: high2(0, BASE["w_in"] - 1, (BASE["w_in"] - 1) % RING, (BASE["w_in"] - 1) // RING)])
            act.dma_start(wuq[:, :, :], a["wuq"]).then_inc(small_in, 16)
            act.dma_start(wuk, a["wuk"]).then_inc(small_in, 16)
            act.dma_start(wuv, a["wuv"]).then_inc(small_in, 16)
            act.dma_start(masks[:, :], a["masks"]).then_inc(mask_in, 16)
            u_high(1)
            for i in range(12):
                piece = BASE["w_in"] + i // 2
                act.wait_ge(half_used, half_number(0, piece, i % 2 + 1))
                src = ps[:, i % PROJ_BANKS, 0:T]
                copy = act.activation(praw[:, i, :], src, ACT.Copy)
                if i == 3:
                    copy.then_inc(proj_ev, 1)
                else:
                    act.activation(lat_sq[:, i, :] if i < 3 else sq[:, i - 4, :], src, ACT.Square).then_inc(proj_ev, 1)
                high(0, piece + 2, (piece + 2) % RING, (piece + 2) // RING, i % 2)
                if i == 8:
                    act.wait_ge(lat_mm, 1)
                    act.activation(lat_rms[:, 0, :], ps[:, 6, 0:T], ACT.Sqrt, bias=eps[:, :]).then_inc(lat_sqrt, 1)
                    act.activation(lat_rms[:, 1, :], ps[:, 7, 0:T], ACT.Sqrt, bias=eps[:, :]).then_inc(lat_sqrt, 1)
            act.wait_ge(half_used, half_number(0, BASE["w_out"], 0))
            for t in range(3):
                n = P if t < 2 else N_META
                act.activation(vF[0:n, t, :], ps[0:n, t, :], ACT.Copy).then_inc(fv_ev, 1)
            act.wait_ge(fstat_mm, 1)
            act.activation(frms[:, 0:32], ps[:, 6, 0:32], ACT.Sqrt, bias=eps[:, :]).then_inc(fstat_sqrt, 1)
            act.activation(frms[0:N_META, 32:40], ps[0:N_META, 6, 32:40], ACT.Sqrt, bias=eps[0:N_META, :]
                           ).then_inc(fstat_sqrt, 1)
            for b in range(4):
                act.wait_ge(q_raw_mm, b + 1)
                src = ps[0:QK, HEAD_BANKS[b], :].rearrange("p (a t) -> p a t", a=2)
                act.activation(qm[0:QK, 2 * b:2 * b + 2, :], src, ACT.Copy, scale=V("g_q")[0:QK])
                act.activation(qsq[0:QK, 2 * b:2 * b + 2, :], src, ACT.Square).then_inc(q_raw_ev, 1)
            fr = slice(FL_ROW, FL_ROW + HEADS)
            act.wait_ge(z_done, 3)
            act.activation(logf[fr, 1, :], logf[fr, 1, :], ACT.Exp, scale=-1.0).then_inc(f_exp, 1)
            act.wait_ge(f_exp, 1)
            act.activation(logf[fr, 2, :], logf[fr, 1, :], ACT.Ln, bias=1.0).then_inc(f_ln, 1)
            for hd in range(HEADS):
                act.wait_ge(k_raw_mm, hd + 1)
                if hd == 0:
                    act.wait_ge(fox_done, 12)
                    act.wait_ge(kpe_done, 2)
                src = ps[0:NOPE, HEAD_BANKS[hd % 4], 0:T]
                act.activation(km[0:NOPE, hd, :], src, ACT.Copy, scale=V("g_k")[0:NOPE])
                act.activation(ksq[0:NOPE, hd, :], src, ACT.Square).then_inc(k_raw_ev, 1)
            act.wait_ge(vm_mm, 1)
            for t in range(3):
                n = P if t < 2 else N_META
                act.activation(vM[0:n, t, :], ps[0:n, t, :], ACT.Copy).then_inc(vm_ev, 1)
            act.wait_ge(mstat_mm, 1)
            act.activation(mrms[:, 0:32], ps[:, 6, 0:32], ACT.Sqrt, bias=eps[:, :]).then_inc(mstat_sqrt, 1)
            act.activation(mrms[0:N_META, 32:40], ps[0:N_META, 6, 32:40], ACT.Sqrt, bias=eps[0:N_META, :]
                           ).then_inc(mstat_sqrt, 1)
            for n in range(2 * HEADS * TT):
                hd, t = divmod(n, TT)
                keys_n = X0 + P * (t + 1)
                act.wait_ge(nmax_done, n + 1)
                if n >= 4:
                    act.wait_ge(pT_mm, n - 3)
                act.activation(probs[:, n % 4, 0:keys_n], ps[:, n % 3, 0:keys_n], ACT.Exp,
                               bias=nmx[:, n:n + 1], scale=q_scale(hd, t),
                               accum_out=rsum[:, n:n + 1]).then_inc(exp_done, 1)
                if n >= 2:
                    attn_evac(act, n - 2)
            attn_evac(act, 2 * HEADS * TT - 2)
            attn_evac(act, 2 * HEADS * TT - 1)
            for piece in range(BASE["ffn2"], BASE["ffn2"] + 2):
                for e in range(2):
                    high(1, piece, piece % RING, piece // RING, e)
            norm(2)
            u_high(2)
            ffn(1)
            norm(3, [lambda: high2(1, BASE["z"] - 1, (BASE["z"] - 1) % RING, (BASE["z"] - 1) // RING)])
            act.wait_ge(lb_step, 3)
            for r in (1, 2):
                act.activation(lb[:, r], lb[:, r], ACT.Exp).then_inc(lb_e, 1)
            act.dma_start(keys, a["keys"]).then_inc(keys_in, 16)
            u_high(3)

            def z_copy(seg, m):
                act.activation(z[:, bass.ds(seg, 1), m, :].rearrange("p o t -> p (o t)"),
                               ps[:, Z_BANKS[m % 4], 0:SEQ], ACT.Copy).then_inc(z_ev, 1)

            def gate_copy(i, fn):
                act.wait_ge(z_mm, 2 * KT + i + 1)
                act.activation(gates[:, i // KT, i % KT, :], ps[:, Z_BANKS[i % 4], 0:SEQ], fn).then_inc(z_ev, 1)

            for m in range(2 * KT):
                piece = BASE["z"] + m // 2
                act.wait_ge(half_used, half_number(1, piece, m % 2 + 1))
                z_copy(m // KT, m % KT)
                if m < 2 * KT - 4:
                    high(1, piece + 2, (piece + 2) % RING, (piece + 2) // RING, m % 2)
            act.wait_ge(z_ev, 2 * KT)
            act.activation(z[:, 1], z[:, 1], ACT.Sigmoid).then_inc(sig_done, 1)
            with act.Fori(0, 2) as i:
                for m in range(KT):
                    act.wait_ge(z_mm, i * KT + (m + 1))
                    z_copy(i + 2, m)
            act.wait_ge(z_ev, 4 * KT)
            act.activation(z[:, 2], z[:, 2], ACT.Sigmoid).then_inc(sig_done, 1)
            act.wait_ge(lb_done, 1)
            act.wait_ge(sig_done, 2)
            for m in range(KT):
                act.activation(pre[:, m, :], pre[:, m, :], ACT.Identity, scale=lb[:, 1, m:m + 1], bias=lb[:, 0, m:m + 1]
                               ).then_inc(f_done, 1)
            act.wait_ge(f_done, KT)
            act.wait_ge(pad_done, 1)
            act.activation(key, pre, ACT.Identity, scale=-1.0, bias=1.0).then_inc(f_done, 1)
            act.wait_ge(zi_mm, 1)
            for t in range(TT):
                for half in range(2):
                    act.activation(zi[:, t, half * 512:(half + 1) * 512], ps[:, t * 2 + half, :], ACT.Copy
                                   ).then_inc(zi_ev, 1)
            for i in range(4):
                gate_copy(i, GATES[0])
            act.wait_ge(cv_step, 1)
            act.wait_ge(diag_mm, 1)
            act.activation(sq2[:, :, :], z[:, 0], ACT.Square).then_inc(ln_act, 1)
            for i in range(4, 6):
                gate_copy(i, GATES[0])
            act.wait_ge(ln_mm, 2)
            act.activation(rstd[:, 0:SEQ], ps[:, 0, 0:SEQ], ACT.Sqrt, bias=eps[:, :]).then_inc(ln_act, 1)
            for i in range(6, 10):
                gate_copy(i, GATES[i // KT])
            act.wait_ge(cv_step, 3)
            for m in range(KT):
                act.activation(z[:, 0, m, :], z[:, 0, m, :], ACT.Silu, scale=V("ln_g", m), bias=V("ln_b", m)
                               ).then_inc(ln_act, 1)
            for i in range(10, 20):
                gate_copy(i, GATES[i // KT])
            for b in range(4):
                act.wait_ge(oh_mm, b + 1)
                flat = slice(2 * b, 2 * b + 2)
                act.activation(o_h[:, flat, :].rearrange("p h t -> p (h t)"), ps[:, b, :], ACT.Copy).then_inc(oh_ev, 1)
                act.activation(sq2[:, flat, :].rearrange("p h t -> p (h t)"), ps[:, b, :], ACT.Square).then_inc(oh_ev, 1)
            act.activation(cv_hi[:, :, :], z[:, 0], ACT.Copy).then_inc(cv_hi_done, 1)

            def late(n):
                piece = BASE["w_b"] + n // 2
                high(2, piece, piece % RING, piece // RING, n % 2)

            act.wait_ge(lev_in, 2 * len(LEVELS) - 1)
            for i in range(20, 24):
                gate_copy(i, GATES[i // KT])
                late(i - 20)
            act.wait_ge(on_mm, 1)
            act.activation(o_rms, ps[:, 0, 0:2 * HEADS], ACT.Sqrt, bias=eps[:, :]).then_inc(on_act, 1)
            late(4)
            late(5)
            for m in range(KT):
                act.wait_ge(o_done, m + 1)
                act.activation(o_hi[:, m, :], o_h[:, m, :], ACT.Copy).then_inc(o_hi_done, 1)
            for n in range(6, 12):
                late(n)
            for m in range(KT):
                late(12 + m)
                act.wait_ge(merged, m + 1)
                act.activation(m_hi[:, m, :], gates[:, 1, m, :], ACT.Copy).then_inc(m_hi_done, 1)
            norm(4, before=[lambda n=n: late(n) for n in range(20, 24)])
            act.dma_start(final_g, a["final_g"].rearrange("(o d) -> o d", o=1).broadcast_to([P, D])
                          ).then_inc(final_in, 16)

            def tok_copy(n):
                act.wait_ge(tok_mm, n + 1)
                act.activation((hf, h_tok)[n // 4][:, n // 2 % 2, n % 2 * 512:n % 2 * 512 + 512], ps[:, 6 + n % 2, :], ACT.Copy
                               ).then_inc(tok_ev, 1)

            for hd in range(HEADS):
                for e in range(2):
                    act.wait_ge(q_mm, hd * 2 + e + 1)
                    if hd >= 2:
                        act.wait_ge(sc_mm, hd - 1)
                    act.activation(qh[:, hd % 2, e, :], ps[:, hd % 2 * 2 + e, 0:SEQ], ACT.Copy).then_inc(q_ev, 1)
                if hd == 0:
                    tok_copy(0)
                    tok_copy(1)
                act.wait_ge(sc_mm, hd + 1)
                act.activation(scores[:, hd].rearrange("p t e n -> p (t e n)"), ps[:, 4 + hd % 2, :], ACT.Copy
                               ).then_inc(sc_ev, 1)
                if hd == 0:
                    tok_copy(2)
                    tok_copy(3)
            for n in range(4, 8):
                tok_copy(n)
            act.wait_ge(gain_mm, 1)
            for half in range(2):
                act.activation(y_gain[:, half * 512:half * 512 + 512], ps[:, half, :], ACT.Copy).then_inc(tok_ev, 1)
            def weights(hd):
                act.wait_ge(gate_sub, hd + 1)
                act.activation(own_gate, own_gate, ACT.Exp).then_inc(gate_e, 1)
                act.wait_ge(row_used, hd * (2 * TT * GR) + TT * GR)
                act.activation(dots, dots, ACT.Gelu).then_inc(gelu_done, 1)

            each_turn(act, HEADS, weights)
            for t in range(TT):
                act.wait_ge(fin_step, 6 * t + 3)
                act.activation(fin[:, 2 * t + 1:2 * t + 2], fin[:, 2 * t:2 * t + 1], ACT.Sqrt, bias=eps[:, :],
                               scale=1.0 / D).then_inc(fin_act, 1)

        @block.vector
        def _(dve):
            steps = {}

            def then(ins, s):
                steps[s.name] = steps.get(s.name, 0) + 1
                ins.then_inc(s, 1)
                dve.wait_ge(s, steps[s.name])

            dve.wait_ge(cols_in, 16)
            then(dve.tensor_tensor(lb[:, 0], V("lb0", 0, KT), V("lb1", 0, KT), ALU.max), lb_step)
            then(dve.tensor_tensor(lb[:, 1], V("lb0", 0, KT), lb[:, 0], ALU.subtract), lb_step)
            then(dve.tensor_tensor(lb[:, 2], V("lb1", 0, KT), lb[:, 0], ALU.subtract), lb_step)

            def norm(n, gain, shift=None, split=True):
                c = NORM_COLS[n]
                w = c.stop - c.start

                def u_low(k):
                    dve.wait_ge(u_hi_done, KT * n + k + 1)
                    dve.tensor_tensor(u_lo[:, k, 0:w], u[:, k, 0:w], u_hi_f[:, k, 0:w], ALU.subtract).then_inc(u_lo_done, 1)

                dve.wait_ge(sqrt_done, n + 1)
                dve.reciprocal(rstd[:, 0:w], rstd[:, 0:w]).then_inc(rstd_done, 1)
                dve.wait_ge(rstd_done, n + 1)
                for k in range(KT):
                    ins = dve.scalar_tensor_tensor(u[:, k, 0:w], h[:, k, c], gain(k), rstd[:, 0:w], ALU.mult, ALU.mult)
                    if shift is None:
                        ins.then_inc(u_done, 1)
                        if k >= 2:
                            u_low(k - 2)
                    else:
                        ins.then_inc(u_scaled, 1)
                if shift is not None:
                    for k in range(KT):
                        dve.wait_ge(u_scaled, KT * (n - 3) + k + 1)
                        dve.tensor_scalar(u[:, k, 0:w], u[:, k, 0:w], shift(k), None, ALU.add).then_inc(u_done, 1)
                        if split and k >= 2:
                            u_low(k - 2)
                if split:
                    for k in range(KT - 2, KT):
                        u_low(k)

            def low(k, piece, slot):
                half = slot % 2 * 2
                dve.wait_ge(hi_done, half_number(k, piece, 1))
                dve.tensor_tensor(w_lo[:, half, :], ring[:, slot, 0:HALF], w_hi_f[:, half, :], ALU.subtract).then_inc(lo_done, 1)

            def low2(k, piece, slot):
                low(k, piece + 2, (slot + 2) % RING)

            def ada_add(kt, q):
                dve.wait_ge(ada_in[q % 2], kt * 32 + (q // 2 * 16 + 16))
                dve.wait_ge(ada_step, kt * ADA_Q + (q + 1))
                dve.scalar_tensor_tensor(ada_acc[:, q, :], ada_ring[:, q % 2, :], silu_c[:, bass.ds(kt, 1)],
                                         ada_acc[:, q, :], ALU.mult, ALU.add).then_inc(ada_step, 1)

            def ffn(k):
                base = BASE["ffn2" if k else "ffn1"]
                w = SEQ if k else T

                def body(piece, slot):
                    f = piece - (base - FT * k)
                    g = act_g[:, slot, 0:w]
                    dve.wait_ge(silu_done, f + 1)
                    dve.wait_ge(half_used, half_number(k, piece, 2))
                    dve.tensor_tensor(g, g, ps[:, 2 * slot + 1, 0:w], ALU.mult).then_inc(glu_made, 1)
                    dve.wait_ge(glu_made, f + 1)
                    dve.tensor_copy(glu_hi[:, bass.ds(piece - base, 1), 0:w].rearrange("p o t -> p (o t)"), g).then_inc(glu_high, 1)
                    dve.wait_ge(glu_high, f + 1)
                    dve.tensor_tensor(glu_lo[:, bass.ds(piece - base, 1), 0:w].rearrange("p o t -> p (o t)"), g,
                                      glu_hi_f[:, bass.ds(piece - base, 1), 0:w].rearrange("p o t -> p (o t)"), ALU.subtract
                                      ).then_inc(glu_done, 1)
                    low2(k, piece, slot)

                if k:
                    each_piece(dve, base, FT, lambda piece, slot, turn: body(piece, slot))
                    for piece in range(base + FT, base + FFN_P - 1):
                        low2(k, piece, piece % RING)
                else:
                    n = FT // (2 * RING)
                    with dve.Fori(0, n) as i:
                        for j in range(2 * RING):
                            body(i * (2 * RING) + j, j % RING)
                            if j % 2:
                                ada_add(i, j // 2)
                    for piece in range(n * 2 * RING, FFN_P):
                        if piece < FT:
                            body(piece, piece % RING)
                        elif piece < FFN_P - 1:
                            low2(k, piece, piece % RING)
                        if piece % 2 and piece < KT * ADA_Q:
                            ada_add(piece // (2 * RING), piece % (2 * RING) // 2)
                c = slice(0, T) if k == 0 else xc
                for m in range(KT):
                    dve.wait_ge(down_done, KT * k + m + 1)
                    dve.scalar_tensor_tensor(h[:, m, c], ps[:, m, 0:w], 0.5, h[:, m, c], ALU.mult, ALU.add
                                             ).then_inc(h_done, 1)
                low2(k, base + FFN_P - 1, (base + FFN_P - 1) % RING)

            low(0, 0, 0)
            norm(0, lambda k: V("g_ffn1", k))
            low(0, 1, 1)
            dve.wait_ge(silu_c_done, 1)
            ffn(0)
            norm(1, lambda k: V("g_mix", k))

            dve.wait_ge(lat_sqrt, 2)
            dve.reciprocal(lat_rms[:, :, :], lat_rms[:, :, :]).then_inc(mrec_done, 1)
            dve.wait_ge(mrec_done, 1)
            for k in range(2):
                dve.scalar_tensor_tensor(cqn[:, k, :], praw[:, k, xc], V("g_cq", k), lat_rms[:, 0, xc], ALU.mult, ALU.mult
                                         ).then_inc(lat_done, 1)
            dve.scalar_tensor_tensor(ckvn, praw[:, 2, :], V("g_ckv"), lat_rms[:, 1, :], ALU.mult, ALU.mult
                                     ).then_inc(lat_done, 1)
            fr = slice(FL_ROW, FL_ROW + HEADS)
            then(dve.tensor_scalar(logf[fr, 1, :], praw[fr, 3, :], V("b_f")[fr], None, ALU.add), z_done)
            then(dve.tensor_scalar(logf[fr, 0, :], logf[fr, 1, :], 0.0, None, ALU.min), z_done)
            then(dve.scalar_tensor_tensor(logf[fr, 1, :], logf[fr, 0, :], -2.0, logf[fr, 1, :], ALU.mult, ALU.add), z_done)
            pr = slice(PE_ROW, PE_ROW + ROPE)
            pe_all = praw[pr, 3:4, :].broadcast_to([ROPE, HEADS, T])
            then(dve.tensor_tensor(pe_sq[pr, :], praw[pr, 3, :], praw[pr, 3, :], ALU.mult), lb_step)
            then(dve.memset(cumz, 0.0), lb_step)
            dve.wait_ge(half_used, half_number(0, BASE["w_out"], 0))
            dve.tensor_scalar(km[pr, :, :], pe_all, V("g_k")[pr], None, ALU.mult).then_inc(kpe_done, 1)
            then(dve.memset(fqz[:, :, :], 0.0), lb_step)
            dve.wait_ge(fstat_sqrt, 2)
            then(dve.reciprocal(frms[:, 0:32], frms[:, 0:32]), mstep)
            dve.reciprocal(frms[0:N_META, 32:40], frms[0:N_META, 32:40]).then_inc(frec, 1)
            for j in range(4):
                dve.wait_ge(fq_mm, j // 2 + 1)
                for e in range(2):
                    r = slice(HD * e, HD * e + HD)
                    dve.scalar_tensor_tensor(fqz[r, 2 * j + e, :], praw[r, 4 + j, xc], V("g_fq")[r],
                                             ps[r, j // 2, j % 2 * SEQ:j % 2 * SEQ + SEQ], ALU.mult, ALU.mult
                                             ).then_inc(fox_done, 1)
            for j in range(4):
                dve.wait_ge(fk_mm, j + 1)
                dve.scalar_tensor_tensor(fk[:, j, :], praw[:, 8 + j, :], V("g_fk"), ps[:, FK_BANKS[j], 0:T],
                                         ALU.mult, ALU.mult).then_inc(fox_done, 1)
            dve.wait_ge(f_ln, 1)
            then(dve.tensor_tensor(logf[fr, 3, :], logf[fr, 0, :], logf[fr, 2, :], ALU.subtract), cum_done)
            then(dve.tensor_tensor_scan(cumz[fr, :], C("ones")[fr, 0:1].broadcast_to([HEADS, T]), logf[fr, 3, :], 0.0,
                                        ALU.mult, ALU.add), cum_done)
            dve.tensor_scalar(ncumz, cumz, -1.0, None, ALU.mult).then_inc(cum_done, 1)
            dve.wait_ge(fox_done, 12)
            dve.wait_ge(kpe_done, 1)
            dve.tensor_copy(ksq[pr, :, :], pe_sq[pr, None, :].broadcast_to([ROPE, HEADS, T])).then_inc(kpe_done, 1)

            def rope(x, rotated, c, n):
                shape = list(x.shape)
                cos = C("cos")[0:QK, None, c].broadcast_to(shape)
                sin = C("sin")[0:QK, None, c].broadcast_to(shape)
                tmp = turned[0:QK, 0:shape[1], 0:shape[2]]
                if n:
                    dve.wait_ge(rope_step, 3 * n)
                dve.tensor_tensor(tmp, rotated, sin, ALU.mult).then_inc(rope_step, 1)
                dve.tensor_tensor(x, x, cos, ALU.mult).then_inc(rope_step, 1)
                dve.wait_ge(rope_step, 3 * n + 2)
                dve.tensor_tensor(x, x, tmp, ALU.add).then_inc(rope_step, 1)

            dve.wait_ge(mstat_sqrt, 2)
            then(dve.reciprocal(mrms[:, 0:32], mrms[:, 0:32]), mstep)
            then(dve.reciprocal(mrms[0:N_META, 32:40], mrms[0:N_META, 32:40]), mstep)
            dve.tensor_scalar(qscale, mrms[:, 0:16], MLA_SCALE, None, ALU.mult).then_inc(mrec2, 1)
            for b in range(4):
                dve.wait_ge(qrot_mm, b + 1)
                rope(qm[0:QK, 2 * b:2 * b + 2, :], ps[0:QK, HEAD_BANKS[b], :].rearrange("p (a t) -> p a t", a=2),
                     slice(X0, T), b)
            for hd in range(HEADS):
                dve.wait_ge(kn_mm, hd + 1)
                dve.tensor_tensor(km[0:QK, hd, :], km[0:QK, hd, :], ps[0:QK, NORM_BANKS[hd % 4], 0:T], ALU.mult
                                  ).then_inc(kn_done, 1)
                if hd:
                    dve.wait_ge(krot_mm, hd)
                    rope(km[0:QK, hd - 1:hd, :], ps[0:QK, None, HEAD_BANKS[(hd - 1) % 4], 0:T], slice(0, T), 4 + hd - 1)
            dve.wait_ge(krot_mm, HEADS)
            rope(km[0:QK, HEADS - 1:HEADS, :], ps[0:QK, None, HEAD_BANKS[(HEADS - 1) % 4], 0:T], slice(0, T), 4 + HEADS - 1)

            def soft_max(n):
                hd, t = divmod(n, TT)
                keys_n = X0 + P * (t + 1)
                dve.wait_ge(s_mm, n + 1)
                dve.reduce_max(mx[:, n:n + 1], ps[:, n % 3, 0:keys_n], AX_X).then_inc(max_done, 1)
                dve.wait_ge(max_done, n + 1)
                dve.tensor_scalar(nmx[:, n:n + 1], mx[:, n:n + 1], q_scale(hd, t), -1.0, ALU.mult, ALU.mult
                                  ).then_inc(nmax_done, 1)

            def scale_p(n):
                t = n % TT
                keys_n = X0 + P * (t + 1)
                dve.wait_ge(exp_done, n + 1)
                dve.reciprocal(rinv[:, n:n + 1], rsum[:, n:n + 1]).then_inc(rinv_done, 1)
                dve.wait_ge(rinv_done, n + 1)
                dve.tensor_scalar(probs[:, n % 4, 0:keys_n], probs[:, n % 4, 0:keys_n], rinv[:, n:n + 1], None, ALU.mult
                                  ).then_inc(p_done, 1)

            units = 2 * HEADS * TT
            soft_max(0)
            for n in range(units):
                if n + 1 < units:
                    soft_max(n + 1)
                scale_p(n)
                if n % 2:
                    ada_add(KT // 2 + n // 8, n // 2 % ADA_Q)
            for m in range(KT):
                dve.wait_ge(wo_mm, m + 1)
                dve.tensor_tensor(h[:, m, xc], h[:, m, xc], ps[:, m, 0:SEQ], ALU.add).then_inc(h_done, 1)
            for piece in range(BASE["ffn2"], BASE["ffn2"] + 2):
                low(1, piece, piece % RING)
            norm(2, lambda k: V("g_ffn2", k))
            dve.wait_ge(ada_mm, 1)
            then(dve.tensor_tensor(ada[:, 0:24], ps[:, 1, 0:24], V("ada_b", 0, 24), ALU.add), ada_done)
            then(dve.scalar_tensor_tensor(gain1[:, :], ada[:, 8:16], 1.0, V("norm1", 0, KT), ALU.add, ALU.mult), ada_done)
            ffn(1)
            norm(3, lambda k: gain1[:, k:k + 1], lambda k: ada[:, k:k + 1])
            dve.wait_ge(ada_mm, 2)
            then(dve.tensor_tensor(ada[:, 24:48], ps[:, 1, 24:48], V("ada_b", 24, 24), ALU.add), ada_done)
            then(dve.scalar_tensor_tensor(gain2[:, :], ada[:, 32:40], 1.0, V("norm2", 0, KT), ALU.add, ALU.mult), ada_done)
            for piece in range(BASE["z"] + 2, BASE["z"] + 8):
                low(1, piece, piece % RING)

            dve.wait_ge(lb_e, 2)
            then(dve.tensor_tensor(lb[:, 3], lb[:, 1], lb[:, 2], ALU.add), lb_step)
            then(dve.reciprocal(lb[:, 4], lb[:, 3]), lb_step)
            then(dve.tensor_tensor(lb[:, 0], lb[:, 1], lb[:, 4], ALU.mult), lb_step)
            dve.tensor_scalar(lb[:, 1], lb[:, 0], -1.0, 1.0, ALU.mult, ALU.add).then_inc(lb_done, 1)
            then(dve.memset(pad_glu[:, :, 0:PAD], 0.0), lb_step)
            dve.wait_ge(sig_done, 1)
            dve.tensor_tensor(pad_glu[:, :, PAD:PAD + SEQ], z[:, 0], z[:, 1], ALU.mult).then_inc(pad_done, 1)
            dve.wait_ge(pad_done, 1)
            cv = z[:, 0]
            for m in range(KT):
                dve.tensor_scalar(cv[:, m, :], pad_glu[:, m, 0:SEQ], V("conv_w", m), V("conv_b", m), ALU.mult, ALU.add
                                  ).then_inc(conv_step, 1)
            with dve.Fori(1, CONV_K) as tap:
                for m in range(KT):
                    dve.wait_ge(conv_step, tap * KT + (m + 1 - KT))
                    dve.scalar_tensor_tensor(cv[:, m, :], pad_glu[:, m, bass.ds(tap, SEQ)],
                                             cols[:, bass.ds(tap * KT + (COL["conv_w"] + m), 1)], cv[:, m, :],
                                             ALU.mult, ALU.add).then_inc(conv_step, 1)

            def blocks(x, b, e):
                v = x.rearrange("p h t -> p (h t)").rearrange("p (n e b) -> p n e b", e=2, b=b)
                return v[:, :, e, :]

            def last(x, b, e):
                v = x.rearrange("p h t -> p (h t)").rearrange("p (n e b) -> p n e b", e=2, b=b)
                return v[:, :, e, b - 1:b].broadcast_to([P, KT * SEQ // (2 * b), b])

            q = z[:, 3]

            def level_in(n):
                b = LEVELS[n]
                buf = n % 2
                if n >= 2:
                    dve.wait_ge(lev_mm, n - 1)
                dve.tensor_tensor(q_odd[:, buf].rearrange("p (n b) -> p n b", b=b), blocks(q, b, 1), blocks(pre, b, 1), ALU.mult
                                  ).then_inc(lev_in, 1)
                if n in (1, 2):
                    dve.tensor_tensor(k_even[:, buf], key, suf[:, :, :], ALU.mult).then_inc(lev_in, 1)
                elif n:
                    dve.tensor_tensor(blocks(k_even[:, buf], b, 0), blocks(key, b, 0), blocks(suf[:, :, :], b, 0), ALU.mult
                                      ).then_inc(lev_in, 1)
                if b < P:
                    dve.wait_ge(lev_in, 2 * n + 1 if n else 1)
                    then(dve.tensor_tensor(blocks(suf[:, :, :], b, 0), blocks(suf[:, :, :], b, 0), last(pre, b, 1),
                                           ALU.mult), lev_up)
                    then(dve.tensor_tensor(blocks(pre, b, 1), blocks(pre, b, 1), last(pre, b, 0), ALU.mult), lev_up)

            def level_out(n):
                b = LEVELS[n]
                dve.wait_ge(lev_mm, n + 1)
                dve.wait_ge(lev_out, n + 1)
                src = ps[:, LEVEL_BANKS[n % 2]:LEVEL_BANKS[n % 2] + 2, :].rearrange("p k t -> p (k t)")
                if b < P:
                    m = masks[:, n * P:(n + 1) * P].rearrange("p (n b) -> p n b", b=b)
                    per = P // b
                    dst = AT[:, :, 0:2, :].rearrange("p h c t -> p h (c t)").rearrange("p h (n e b) -> p h n e b", e=2, b=b)
                    dve.copy_predicated(dst[:, :, :, 1, :], m[:, None, :, :].broadcast_to([P, HEADS, per, b]),
                                        src.rearrange("p (h n b) -> p h n b", h=HEADS, b=b)).then_inc(lev_out, 1)
                else:
                    dve.tensor_copy(AT[:, :, 2, :], src.rearrange("p (h t) -> p h t", t=P)).then_inc(lev_out, 1)

            dve.wait_ge(f_done, KT + 1)
            dve.wait_ge(suf_set, 1)
            level_in(0)
            dve.wait_ge(ln_mm, 1)
            mean = ps[:, 0, None, 0:SEQ].broadcast_to([P, KT, SEQ])
            dve.tensor_tensor(cv, cv, mean, ALU.subtract).then_inc(cv_step, 1)
            dve.wait_ge(diag_mm, 1)
            dve.tensor_tensor(AT[:, :, 0:2, :].rearrange("p h c t -> p h (c t)").rearrange("p h (c t) -> p h c t", c=2),
                              ident[:, None, None, :].broadcast_to([P, HEADS, TT, P]),
                              ps[:, 1, 0:2 * HEADS].rearrange("p (h c) -> p h c", c=2)[:, :, :, None].broadcast_to([P, HEADS, TT, P]),
                              ALU.mult).then_inc(lev_out, 1)
            dve.wait_ge(mask_in, 16)
            level_in(1)
            level_out(0)
            dve.wait_ge(ln_act, 2)
            dve.reciprocal(rstd[:, 0:SEQ], rstd[:, 0:SEQ]).then_inc(cv_step, 1)
            level_in(2)
            level_out(1)
            dve.wait_ge(cv_step, 2)
            dve.tensor_tensor(cv, cv, rstd[:, None, 0:SEQ].broadcast_to([P, KT, SEQ]), ALU.mult).then_inc(cv_step, 1)
            for n in range(3, len(LEVELS)):
                level_in(n)
                level_out(n - 1)
            level_out(len(LEVELS) - 1)
            dve.wait_ge(cv_hi_done, 1)
            dve.tensor_tensor(cv_lo[:, :, :], cv, cv_hi_f, ALU.subtract).then_inc(cv_lo_done, 1)
            dve.wait_ge(on_act, 1)
            dve.reciprocal(o_rms, o_rms).then_inc(on_rec, 1)
            for m in range(KT):
                dve.wait_ge(on_mm, 2 + m // 2)
                dve.scalar_tensor_tensor(o_h[:, m, :], o_h[:, m, :], V("hg_g", m), ps[:, m // 2, m % 2 * SEQ:m % 2 * SEQ + SEQ],
                                         ALU.mult, ALU.mult).then_inc(o_step, 1)
            for m in range(KT):
                dve.wait_ge(o_step, m + 1)
                dve.wait_ge(z_ev, 5 * KT)
                dve.tensor_tensor(o_h[:, m, :], o_h[:, m, :], gates[:, 0, m, :], ALU.mult).then_inc(o_done, 1)
            def tile_made(name, m):
                dve.wait_ge(half_used, half_number(2, BASE[name], m + 1))

            for m in range(KT):
                if m == KT // 2:
                    for k in range(KT):
                        dve.wait_ge(o_hi_done, k + 1)
                        dve.tensor_tensor(o_lo[:, k, :], o_h[:, k, :], o_hi_f[:, k, :], ALU.subtract).then_inc(o_lo_done, 1)
                tile_made("w_b", m)
                dve.tensor_tensor(gates[:, 2, m, :], gates[:, 2, m, :], ps[:, Z_BANKS[m % 4], 0:SEQ], ALU.mult).then_inc(dense_ev, 1)

            def merged_low(m):
                dve.wait_ge(m_hi_done, m + 1)
                dve.tensor_tensor(m_lo[:, m, :], gates[:, 1, m, :], m_hi_f[:, m, :], ALU.subtract).then_inc(m_lo_done, 1)

            for m in range(KT):
                tile_made("w_a", m)
                dve.tensor_tensor(gates[:, 1, m, :], gates[:, 1, m, :], ps[:, Z_BANKS[m % 4], 0:SEQ], ALU.mult).then_inc(dense_ev, 1)
                dve.wait_ge(dense_ev, KT + m + 1)
                dve.tensor_tensor(gates[:, 1, m, :], gates[:, 1, m, :], gates[:, 2, m, :], ALU.add).then_inc(merged, 1)
                if m:
                    merged_low(m - 1)
            merged_low(KT - 1)
            for m in range(KT):
                tile_made("w_out_2", m)
                dve.scalar_tensor_tensor(h[:, m, xc], ps[:, Z_BANKS[m % 4], 0:SEQ], ada[:, 16 + m:17 + m], h[:, m, xc], ALU.mult, ALU.add
                                         ).then_inc(h_done, 1)
            norm(4, lambda k: gain2[:, k:k + 1], lambda k: ada[:, 24 + k:25 + k], split=False)

            tile_shape = [P, TT, TOPK, TOPK]
            count = [0]

            def step(ins):
                ins.then_inc(tk, 1)
                count[0] += 1
                return count[0]

            def passed(hd, n):
                dve.wait_ge(tk, hd * CHOOSE_STEPS + n)
                dve.sem_inc(choose_passed, 1)

            def eight(hd, chains, at):
                for v, _, src in chains:
                    n = step(dve.max(v[:, at:at + 8], src))
                passed(hd, n)
                for v, where, src in chains:
                    step(dve.max_index(where[:, at:at + 8], v[:, at:at + 8], src))

            def without(chains, rests):
                for (v, _, src), rest in zip(chains, rests):
                    n = step(dve.match_replace(rest, v[:, 0:8], src, -3.0e38))
                return n

            halves = [(t, e) for t in range(TT) for e in range(2)]

            def choose_halves(hd):
                count[0] = 0
                dve.wait_ge(sc_ev, hd + 1)
                if not isinstance(hd, int) or hd:
                    dve.sem_inc(choose_passed, 1)
                    dve.wait_ge(tk, hd * CHOOSE_STEPS)
                    dve.sem_inc(choose_passed, 1)
                passed(hd, step(dve.tensor_copy(own_scores, scores[:, bass.ds(hd, 1)].rearrange("p o t e n -> p (o t) e n"))))
                chains = [(top[:, t, e], top_u[:, t, e], own_scores[:, t, e]) for t, e in halves]
                eight(hd, chains, 0)
                without(chains, [left[:, t, e] for t, e in halves])

            def choose_rest(hd):
                passed(hd, count[0])
                eight(hd, [(top[:, t, e], top_u[:, t, e], left[:, t, e]) for t, e in halves], TOPK // 2)
                step(dve.tensor_tensor(cand.rearrange("p t (i j) -> p t i j", i=TOPK),
                                       top[:, :, 0, :, None].broadcast_to(tile_shape),
                                       top[:, :, 1, None, :].broadcast_to(tile_shape), ALU.add))

            def choose_sums(hd):
                passed(hd, count[0])
                step(dve.tensor_copy(top_i, top_u[:, :, :, :]))
                chains = [(own_best[:, t], pos_u[:, t], cand[:, t]) for t in range(TT)]
                eight(hd, chains, 0)
                passed(hd, without(chains, [left2[:, t] for t in range(TT)]))
                eight(hd, [(own_best[:, t], pos_u[:, t], left2[:, t]) for t in range(TT)], TOPK // 2)
                dve.tensor_tensor(own_gate, own_best, own_best[:, :, 0:1].broadcast_to([P, TT, TOPK]), ALU.subtract
                                  ).then_inc(gate_sub, 1)

            def choose_index(hd):
                passed(hd, count[0])
                step(dve.tensor_scalar(part_u[:, 0], pos_u[:, :, :], 4, None, ALU.logical_shift_right))
                passed(hd, step(dve.tensor_scalar(part_u[:, 1], pos_u[:, :, :], TOPK - 1, None, ALU.bitwise_and)))
                passed(hd, step(dve.tensor_copy(pos, part_u[:, :, :, :])))
                iota = C("iota")[:, None, None, :].broadcast_to(tile_shape)
                for e in range(2):
                    passed(hd, step(dve.tensor_tensor(onehot, pos[:, e, :, :, None].broadcast_to(tile_shape), iota, ALU.is_equal)))
                    passed(hd, step(dve.tensor_tensor(onehot, onehot, top_i[:, :, e, None, :].broadcast_to(tile_shape), ALU.mult)))
                    passed(hd, step(dve.reduce_sum(part_i[:, e], onehot, AX_X)))
                passed(hd, step(dve.scalar_tensor_tensor(part_i[:, 0], part_i[:, 0], float(NKEYS), part_i[:, 1], ALU.mult, ALU.add)))
                dve.tensor_copy(eidx[:, bass.ds(hd * (TT * TOPK), TT * TOPK)],
                                part_i[:, 0].rearrange("p t k -> p (t k)")).then_inc(idx_done, 1)
                assert count[0] == CHOOSE_STEPS, count

            def dot(hd, t, par):
                turn = hd * (2 * TT) + t
                for r in range(par * 8, par * 8 + 8):
                    dve.wait_ge(row_in[r], turn * 16 + 16)
                    dve.tensor_tensor_reduce(rows[:, r, :], rows[:, r, :], hf[:, t, :], 1.0, 0.0, ALU.mult, ALU.add,
                                             dots[:, t, r:r + 1]).then_inc(row_used, 1)

            def weigh(hd, t, par):
                turn = hd * (2 * TT) + (TT + t)
                for r in range(par * 8, par * 8 + 8):
                    dve.wait_ge(row_in[r], turn * 16 + 16)
                    dve.wait_ge(row_used, turn * GR + r)
                    dve.scalar_tensor_tensor(acc[:, t, :], rows[:, r, :], wts[:, t, r:r + 1], acc[:, t, :], ALU.mult, ALU.add
                                             ).then_inc(row_used, 1)

            def head(hd, more):
                dot(hd, 0, 0)
                if more:
                    choose_halves(hd + 1)
                dot(hd, 0, 1)
                if more:
                    choose_rest(hd + 1)
                dot(hd, 1, 0)
                dve.wait_ge(gate_e, hd * 3 + 1)
                dve.reduce_sum(gate_s, own_gate, AX_X).then_inc(gate_e, 1)
                dve.wait_ge(gate_e, hd * 3 + 2)
                dve.reciprocal(gate_s, gate_s).then_inc(gate_e, 1)
                dve.wait_ge(gate_e, hd * 3 + 3)
                dve.tensor_tensor(gate, own_gate, gate_s[:, :, None].broadcast_to([P, TT, TOPK]), ALU.mult).then_inc(gate_done, 1)
                dot(hd, 1, 1)
                dve.wait_ge(gate_done, hd + 1)
                if more:
                    choose_sums(hd + 1)
                dve.wait_ge(gelu_done, hd + 1)
                dve.tensor_tensor(wts, dots, gate, ALU.mult).then_inc(w_done, 1)
                dve.wait_ge(w_done, hd + (TT + 1))
                weigh(hd, 0, 0)
                if more:
                    choose_index(hd + 1)
                weigh(hd, 0, 1)
                weigh(hd, 1, 0)
                weigh(hd, 1, 1)

            for part in (choose_halves, choose_rest, choose_sums, choose_index):
                part(0)
            for t in range(TT):
                dve.memset(acc[:, t, :], 0.0).then_inc(w_done, 1)
            dve.wait_ge(tok_ev, 4)
            with dve.Fori(0, HEADS - 1) as hd:
                head(hd, True)
            head(HEADS - 1, False)
            for t in range(TT):
                dve.wait_ge(row_used, HEADS * 2 * TT * GR - (TT - 1 - t) * GR)
                if t == 0:
                    dve.wait_ge(tok_ev, 10)
                    dve.wait_ge(final_in, 16)
                then(dve.tensor_tensor(acc[:, t, :], acc[:, t, :], y_gain, ALU.mult), fin_step)
                then(dve.tensor_tensor(acc[:, t, :], acc[:, t, :], h_tok[:, t, :], ALU.add), fin_step)
                then(dve.tensor_tensor_reduce(hf[:, t, :], acc[:, t, :], acc[:, t, :], 1.0, 0.0, ALU.mult, ALU.add,
                                              fin[:, 2 * t:2 * t + 1]), fin_step)
                dve.wait_ge(fin_act, t + 1)
                then(dve.reciprocal(fin[:, 8 + t:9 + t], fin[:, 2 * t + 1:2 * t + 2]), fin_step)
                then(dve.tensor_scalar(acc[:, t, :], acc[:, t, :], fin[:, 8 + t:9 + t], None, ALU.mult), fin_step)
                then(dve.tensor_tensor(acc[:, t, :], acc[:, t, :], final_g[:, :], ALU.mult), fin_step)

        @block.tensor
        def _(pe):
            def arrived(piece, slot):
                turn = piece // RING if isinstance(piece, int) else None
                if turn is not None:
                    pe.wait_ge(landed[slot], 16 * turn + 16)
                return turn

            def each(base, n, body, peel=0):
                for at, turns in runs(base, n, peel):
                    if not turns:
                        pe.wait_ge(landed[at % RING], at // RING * 16 + 16)
                        body(at, at % RING).then_inc(used, 1)
                        continue
                    with pe.Fori(0, turns) as i:
                        for slot in range(RING):
                            pe.wait_ge(landed[slot], i * 16 + (at // RING * 16 + 16))
                            body(i * RING + (at + slot), slot).then_inc(used, 1)

            def parts_ready(k, piece, e):
                if e:
                    pe.wait_ge(used, piece + 1)
                else:
                    pe.wait_ge(lo_done, piece + (1 - GAPS[k]))

            def split_tile(dst, k, piece, slot, e, w, ready=None, x=(u_hi, u_lo)):
                half = slot % 2 * 2 + e
                hi, lo, _ = w_parts(k)
                parts_ready(k, piece, e)
                for b in range(KT):
                    if ready:
                        ready(b)
                    block = slice(b * P, (b + 1) * P)
                    pe.matmul(dst, hi[:, half, block], x[0][:, b, 0:w], start=(b == 0), stop=False)
                    pe.matmul(dst, hi[:, half, block], x[1][:, b, 0:w], start=False, stop=False)
                    mm = pe.matmul(dst, lo[:, half, block], x[0][:, b, 0:w], start=False, stop=(b == KT - 1))
                mm.then_inc(half_used, 1)

            def blk(slot, b):
                return ring[:, slot, b * P:(b + 1) * P]

            LAG = 3

            def square_mean(n, k):
                w = NORM_COLS[n].stop - NORM_COLS[n].start
                src = sq if n < 3 else sq2
                pe.wait_ge(sq_done, KT * n + k + 1)
                mm = pe.matmul(ps[:, 0, 0:w], C("mean_d"), src[:, k, 0:w], start=(k == 0), stop=(k == KT - 1))
                if k == KT - 1:
                    mm.then_inc(ss_done, 1)

            def norm(n, first=0):
                for k in range(first, KT):
                    square_mean(n, k)

            def ffn(k):
                base = BASE["ffn2" if k else "ffn1"]
                w = SEQ if k else T

                def up(piece, slot, turn):
                    f = piece - (base - FT * k)
                    if not (k == 0 and isinstance(piece, int) and piece < RING):
                        pe.wait_ge(glu_done, f - (RING - 1))
                    first = isinstance(piece, int) and piece == base
                    if k and isinstance(piece, int) and piece == base + 2:
                        pe.wait_ge(ada_done, 1)
                    for e in range(2):
                        split_tile(ps[:, 2 * slot + e, 0:w], k, piece, slot, e, w,
                                   (lambda b: pe.wait_ge(u_lo_done, KT * 2 * k + b + 1)) if first and e == 0 else None)

                each_piece(pe, base, FT, up, peel=0 if k else RING)
                pe.wait_ge(glu_done, FT * (k + 1))

                def down(piece, slot, turn):
                    f = (piece - (base + FT)) * 2
                    for e in range(2):
                        half = slot % 2 * 2 + e
                        parts_ready(k, piece, e)
                        first = isinstance(f, int) and f + e == 0
                        hi = glu_hi[:, bass.ds(f + e, 1), 0:w].rearrange("p o t -> p (o t)")
                        lo = glu_lo[:, bass.ds(f + e, 1), 0:w].rearrange("p o t -> p (o t)")
                        for m in range(KT):
                            block = slice(m * P, (m + 1) * P)
                            pe.matmul(ps[:, m, 0:w], w_hi[:, half, block], hi, start=first, stop=False)
                            pe.matmul(ps[:, m, 0:w], w_hi[:, half, block], lo, start=False, stop=False)
                            mm = pe.matmul(ps[:, m, 0:w], w_lo[:, half, block], hi, start=False, stop=False)
                        mm.then_inc(half_used, 1)

                each_piece(pe, base + FT, FFN_P - FT - 1, down, peel=1)
                last = base + FFN_P - 1
                for e in range(2):
                    parts_ready(k, last, e)
                for m in range(KT):
                    block = slice(m * P, (m + 1) * P)
                    for e in range(2):
                        half = last % 2 * 2 + e
                        hi, lo = glu_hi[:, FT - 2 + e, 0:w], glu_lo[:, FT - 2 + e, 0:w]
                        pe.matmul(ps[:, m, 0:w], w_hi[:, half, block], hi, start=False, stop=False)
                        pe.matmul(ps[:, m, 0:w], w_hi[:, half, block], lo, start=False, stop=False)
                        mm = pe.matmul(ps[:, m, 0:w], w_lo[:, half, block], hi, start=False, stop=(e == 1))
                    mm.then_inc(down_done, 1)
                    if m >= LAG:
                        square_mean(2 * k + 1, m - LAG)
                pe.wait_ge(down_done, KT * (k + 1))
                pe.sem_inc(half_used, 1)
                pe.sem_inc(half_used, 1)

            def ada_sums(first, end):
                pe.wait_ge(ada_step, KT * ADA_Q + ADA_Q)
                flat = ada_acc.rearrange("p q w -> p (q w)")
                for m in range(first, end):
                    mm = pe.matmul(ps[:, 1, m:m + 1], flat[:, m * P:(m + 1) * P], C("ones")[:, 0:1], start=True, stop=True)
                mm.then_inc(ada_mm, 1)

            def dense(name, rhs, done):
                def body(piece, slot):
                    for e in range(2):
                        m = (piece - BASE[name]) * 2 + e
                        for b in range(KT):
                            mm = pe.matmul(ps[:, m, 0:SEQ], blk(slot, e * KT + b), rhs[:, b, 0:SEQ],
                                           start=(b == 0), stop=(b == KT - 1))
                        if e == 0:
                            mm.then_inc(done, 1)
                    return mm

                for piece in range(BASE[name], BASE[name] + 4):
                    pe.wait_ge(landed[piece % RING], piece // RING * 16 + 16)
                    body(piece, piece % RING).then_inc(done, 1)
                    pe.wait_ge(done, done_count(done, 2))
                    pe.sem_inc(used, 1)

            counts = {}

            def done_count(s, n):
                counts[s.name] = counts.get(s.name, 0) + n
                return counts[s.name]

            pe.wait_ge(con_in, 16)
            norm(0)
            ffn(0)
            norm(1, KT - LAG)
            def token_tiles(first, n):
                return [(first + s * P, min(P, T - first - s * P)) for s in range(n)]

            for p in range(6):
                piece = BASE["w_in"] + p
                for e in range(2):
                    i = 2 * p + e
                    if i >= PROJ_BANKS:
                        pe.wait_ge(proj_ev, i - PROJ_BANKS + 1)
                    split_tile(ps[:, i % PROJ_BANKS, 0:T], 0, piece, piece % RING, e, T,
                               (lambda b: pe.wait_ge(u_lo_done, KT + b + 1)) if i == 0 else None)
                if p == 2:
                    pe.wait_ge(proj_ev, 3)
                    for k in range(2):
                        pe.matmul(ps[:, 6, 0:T], C("mean_256"), lat_sq[:, k, :], start=(k == 0), stop=(k == 1))
                    pe.matmul(ps[:, 7, 0:T], C("mean_128"), lat_sq[:, 2, :], start=True, stop=True).then_inc(lat_mm, 1)
            pe.wait_ge(proj_ev, 9)
            for p in range(2):
                piece = BASE["w_in"] + 6 + p
                for e in range(2):
                    half = piece % 2 * 2 + e
                    parts_ready(0, piece, e)
                    for b in range(2):
                        k = p * 4 + e * 2 + b
                        wide = slice(b * 512, (b + 1) * 512)
                        for t, (at, n) in enumerate(token_tiles(0, 3)):
                            pe.matmul(ps[0:n, t, :], u_hi[:, k, at:at + n], w_hi[:, half, wide], start=(k == 0), stop=False)
                            pe.matmul(ps[0:n, t, :], u_lo[:, k, at:at + n], w_hi[:, half, wide], start=False, stop=False)
                            mm = pe.matmul(ps[0:n, t, :], u_hi[:, k, at:at + n], w_lo[:, half, wide], start=False, stop=(k == KT - 1))
                    mm.then_inc(half_used, 1)
            pe.wait_ge(proj_ev, 12)
            pe.wait_ge(lat_sqrt, 2)
            two = C("mean_64").rearrange("p (e d) -> p d e", e=2)[:, 0, :]
            for kind, tiles in ((0, token_tiles(X0, 2)), (1, token_tiles(0, 3))):
                for s, (at, n) in enumerate(tiles):
                    for j in range(4):
                        col = 16 * kind + s * 8 + j * 2
                        mm = pe.matmul(ps[0:n, 6, col:col + 2], sq[:, 4 * kind + j, at:at + n], two, start=True, stop=True)
            mm.then_inc(fstat_mm, 1)
            pe.wait_ge(small_in, 16 * 3)
            pe.wait_ge(lat_done, 3)
            for b in range(4):
                for i in range(2):
                    hd = 2 * b + i
                    for k in range(2):
                        mm = pe.matmul(ps[0:QK, HEAD_BANKS[b], i * SEQ:(i + 1) * SEQ], wuq[:, k, hd * QK:(hd + 1) * QK],
                                       cqn[:, k, :], start=(k == 0), stop=(k == 1))
                mm.then_inc(q_raw_mm, 1)

            def spread(dst, rms, kind, j, tiles):
                for s, (at, n) in enumerate(tiles):
                    for e in range(2):
                        col = 16 * kind + s * 8 + j * 2 + e
                        mm = pe.matmul(dst[HD * e:HD * e + HD, s * P:s * P + n], rms[0:n, col:col + 1].broadcast_to([n, HD]),
                                       ident[0:n, 0:n], start=True, stop=True)
                return mm

            pe.wait_ge(frec, 1)
            pe.wait_ge(fv_ev, 3)
            for j in range(4):
                mm = spread(ps[:, j // 2, j % 2 * SEQ:j % 2 * SEQ + SEQ], frms, 0, j, token_tiles(X0, 2))
                if j % 2:
                    mm.then_inc(fq_mm, 1)
            for j in range(4):
                if j:
                    pe.wait_ge(fox_done, (4, 8, 9)[j - 1])
                spread(ps[:, FK_BANKS[j], :], frms, 1, j, token_tiles(0, 3)).then_inc(fk_mm, 1)
            for hd in range(HEADS):
                if hd < 4:
                    pe.wait_ge(q_raw_ev, hd + 1)
                else:
                    pe.wait_ge(k_raw_ev, hd - 3)
                pe.matmul(ps[0:NOPE, HEAD_BANKS[hd % 4], 0:T], wuk[:, hd * NOPE:(hd + 1) * NOPE], ckvn, start=True, stop=True
                          ).then_inc(k_raw_mm, 1)
            pe.wait_ge(fox_done, 12)
            for t, (at, n) in enumerate(token_tiles(0, 3)):
                mm = pe.matmul(ps[0:n, t, :], ckvn[:, at:at + n], wuv, start=True, stop=True)
            mm.then_inc(vm_mm, 1)
            pe.wait_ge(fstat_sqrt, 2)
            pe.wait_ge(q_raw_ev, 4)
            one = C("mean_96")[0:QK, 0:1]
            for s, (at, n) in enumerate(token_tiles(0, 2)):
                for hd in range(HEADS):
                    pe.matmul(ps[0:n, 6, s * 8 + hd:s * 8 + hd + 1], qsq[0:QK, hd, at:at + n], one, start=True, stop=True)
            pe.wait_ge(k_raw_ev, HEADS)
            for s, (at, n) in enumerate(token_tiles(0, 3)):
                for hd in range(HEADS):
                    col = 16 + s * 8 + hd
                    mm = pe.matmul(ps[0:n, 6, col:col + 1], ksq[0:QK, hd, at:at + n], one, start=True, stop=True)
            mm.then_inc(mstat_mm, 1)
            for b in range(4):
                pe.matmul(ps[0:QK, HEAD_BANKS[b], :], C("rot")[0:QK, 0:QK],
                          qm[0:QK, 2 * b:2 * b + 2, :].rearrange("p a t -> p (a t)"), start=True, stop=True).then_inc(qrot_mm, 1)
            pe.wait_ge(mrec2, 1)
            pe.wait_ge(vm_ev, 3)

            def key_norm(hd):
                if hd >= 4:
                    pe.wait_ge(kn_done, hd - 3)
                for s, (at, n) in enumerate(token_tiles(0, 3)):
                    col = 16 + s * 8 + hd
                    mm = pe.matmul(ps[0:QK, NORM_BANKS[hd % 4], at:at + n], mrms[0:n, col:col + 1].broadcast_to([n, QK]),
                                   ident[0:n, 0:n], start=True, stop=True)
                mm.then_inc(kn_mm, 1)

            key_norm(0)
            for hd in range(HEADS):
                if hd + 1 < HEADS:
                    key_norm(hd + 1)
                pe.wait_ge(kn_done, hd + 1)
                pe.wait_ge(rope_step, 3 * hd + 1)
                pe.matmul(ps[0:QK, HEAD_BANKS[hd % 4], 0:T], C("rot")[0:QK, 0:QK], km[0:QK, hd, :], start=True, stop=True
                          ).then_inc(krot_mm, 1)
            pe.wait_ge(rope_step, 3 * (4 + HEADS))
            pe.wait_ge(cum_done, 3)
            pe.wait_ge(fox_done, 12)
            units = 2 * HEADS * TT

            def scores_of(n):
                hd, t = divmod(n, TT)
                keys_n = X0 + P * (t + 1)
                q = slice(t * P, (t + 1) * P)
                dst = ps[:, n % 3, 0:keys_n]
                if n >= 3:
                    pe.wait_ge(exp_done, n - 2)
                if hd < HEADS:
                    pe.matmul(dst, qm[0:QK, hd, q], km[0:QK, hd, 0:keys_n], start=True, stop=False)
                else:
                    f = hd - HEADS
                    pe.matmul(dst, fqz[:, f, q], fk[:, f // 2, 0:keys_n], start=True, stop=False)
                    pe.matmul(dst, cumz[:, X0 + t * P:X0 + (t + 1) * P], C("sel")[:, f:f + 1].broadcast_to([P, keys_n]), start=False, stop=False)
                    pe.matmul(dst, C("sel")[:, f:f + 1].broadcast_to([P, P]), ncumz[:, 0:keys_n], start=False, stop=False)
                pe.matmul(ps[:, n % 3, keys_n - P:keys_n], ident, C("neg_mask"), start=False, stop=True).then_inc(s_mm, 1)

            def turn_probs(n):
                t = n % TT
                full = t + 1
                bank = 3 + n % 2
                pe.wait_ge(p_done, n + 1)
                if n >= 2:
                    pe.wait_ge(pT_ev, n - 1)
                for s in range(full):
                    pe.transpose(ps[:, bank, s * P:(s + 1) * P], probs[:, n % 4, s * P:(s + 1) * P], ident)
                pe.transpose(ps[0:N_META, bank, full * P:(full + 1) * P],
                             probs[:, n % 4, full * P:full * P + N_META], ident).then_inc(pT_mm, 1)

            def weigh(n):
                hd, t = divmod(n, TT)
                full = t + 1
                v = (vM if hd < HEADS else vF)
                pair = (hd % HEADS) // 2
                c = slice(pair * P, pair * P + P)
                pe.wait_ge(pT_ev, n + 1)
                if n >= 2:
                    pe.wait_ge(o_ev, n - 1)
                for s in range(full):
                    pe.matmul(ps[:, 5 + n % 2, 0:P], v[:, s, c], probsT[:, n % 2, s, :], start=(s == 0), stop=False)
                pe.matmul(ps[:, 5 + n % 2, 0:P], v[0:N_META, full, c], probsT[0:N_META, n % 2, full, :],
                          start=False, stop=True).then_inc(o_mm, 1)

            scores_of(0)
            scores_of(1)
            for n in range(units):
                if n + 2 < units:
                    scores_of(n + 2)
                turn_probs(n)
                if n:
                    weigh(n - 1)
            weigh(units - 1)
            pe.wait_ge(o_ev, units)
            dense("w_out", oT, wo_mm)
            norm(2)
            ada_sums(0, 24)
            ffn(1)
            norm(3, KT - LAG)
            ada_sums(24, 48)
            def z_tile(m, slot, e):
                for b in range(KT):
                    mm = pe.matmul(ps[:, Z_BANKS[m % 4], 0:SEQ], blk(slot, e * KT + b), u[:, b, 0:SEQ],
                                   start=(b == 0), stop=(b == KT - 1))
                mm.then_inc(z_mm, 1)

            for m in range(2 * KT):
                piece = BASE["z"] + m // 2
                if m >= 4:
                    pe.wait_ge(z_ev, m - 3)
                split_tile(ps[:, Z_BANKS[m % 4], 0:SEQ], 1, piece, piece % RING, m % 2, SEQ,
                           (lambda b: pe.wait_ge(u_lo_done, 3 * KT + b + 1)) if m == 0 else None)
            with pe.Fori(0, 2) as i:
                for pair in range(4):
                    at = BASE["z"] + 8 + pair
                    pe.wait_ge(landed[at % RING], i * 16 + (at // RING * 16 + 16))
                    for e in range(2):
                        m = 2 * pair + e
                        pe.wait_ge(z_ev, i * KT + (2 * KT + m - 3))
                        z_tile(m, at % RING, e)
                    pe.wait_ge(z_mm, i * KT + (2 * pair + 2))
                    pe.sem_inc(used, 1)
            for p in range(4):
                piece = BASE["zi"] + p
                slot = piece % RING
                half = p // 2
                pe.wait_ge(landed[slot], piece // RING * 16 + 16)
                for b in range(4):
                    k = (p % 2) * 4 + b
                    for t in range(TT):
                        mm = pe.matmul(ps[:, t * 2 + half, :], u[:, k, t * P:(t + 1) * P], ring[:, slot, b * 512:(b + 1) * 512],
                                       start=(k == 0), stop=(k == KT - 1))
                if p < 3:
                    mm.then_inc(used, 1)
                else:
                    mm.then_inc(zi_mm, 1)
                    pe.wait_ge(zi_mm, 1)
                    pe.sem_inc(used, 1)

            def gate_piece(p):
                piece = BASE["z_gate"] + p
                slot = piece % RING
                pe.wait_ge(landed[slot], piece // RING * 16 + 16)
                for e in range(2):
                    m = 4 * KT + 2 * p + e
                    pe.wait_ge(z_ev, m - 3)
                    z_tile(m, slot, e)
                pe.wait_ge(z_mm, 2 * KT + 2 * p + 2)
                pe.sem_inc(used, 1)

            def level(n):
                pe.wait_ge(lev_in, 2 * n + 1)
                if n >= 2:
                    pe.wait_ge(lev_out, n)
                kk = k_even[:, n % 2] if n else key
                bank = LEVEL_BANKS[n % 2]
                for hd in range(HEADS):
                    if LEVELS[n] < P:
                        for half in range(TT):
                            at = hd * TT + half
                            mm = pe.matmul(ps[:, bank + at // 8, at % 8 * HD:at % 8 * HD + HD], kk[:, hd, half * P:half * P + P],
                                           q_odd[:, n % 2, at * HD:at * HD + HD], start=True, stop=True)
                    else:
                        mm = pe.matmul(ps[:, bank + hd // 4, hd % 4 * P:hd % 4 * P + P], kk[:, hd, 0:P],
                                       q_odd[:, n % 2, hd * P:hd * P + P], start=True, stop=True)
                mm.then_inc(lev_mm, 1)

            gate_piece(0)
            pe.wait_ge(zi_ev, 4)
            for m in range(KT):
                pe.wait_ge(conv_step, (CONV_K - 1) * KT + m + 1)
                mm = pe.matmul(ps[:, 0, 0:SEQ], C("mean_d"), z[:, 0, m, :], start=(m == 0), stop=(m == KT - 1))
            mm.then_inc(ln_mm, 1)
            pe.wait_ge(ada_done, 4)
            pe.wait_ge(qk_done, 1)
            for hd in range(HEADS):
                for t in range(TT):
                    mm = pe.matmul(ps[:, 1, hd * TT + t:hd * TT + t + 1], qk[:, hd, t * P:(t + 1) * P], C("ones")[:, 0:1],
                                   start=True, stop=True)
            mm.then_inc(diag_mm, 1)
            pe.wait_ge(f_done, KT + 1)
            level(0)
            gate_piece(1)
            pe.wait_ge(ln_act, 1)
            for m in range(KT):
                mm = pe.matmul(ps[:, 0, 0:SEQ], C("mean_d"), sq2[:, m, :], start=(m == 0), stop=(m == KT - 1))
            mm.then_inc(ln_mm, 1)
            gate_piece(2)
            pe.wait_ge(ln_act, 2)
            pe.wait_ge(lev_out, 1)
            for n in range(1, len(LEVELS)):
                level(n)
                gate_piece(n + 2)
            pe.wait_ge(lev_out, len(LEVELS) + 1)
            for hd in range(HEADS):
                c = slice(hd * P, hd * P + P)
                at = hd % 2 * SEQ
                pe.matmul(ps[:, hd // 2, at:at + P], zi[:, 0, c], AT[:, hd, 0, :], start=True, stop=True)
                pe.matmul(ps[:, hd // 2, at + P:at + 2 * P], zi[:, 0, c], AT[:, hd, 2, :], start=True, stop=False)
                mm = pe.matmul(ps[:, hd // 2, at + P:at + 2 * P], zi[:, 1, c], AT[:, hd, 1, :], start=False, stop=True)
                if hd % 2:
                    mm.then_inc(oh_mm, 1)
            gate_piece(10)
            pe.wait_ge(oh_ev, 8)
            for t in range(TT):
                for hd in range(HEADS):
                    mm = pe.matmul(ps[:, 0, t * HEADS + hd:t * HEADS + hd + 1], sq2[:, hd, t * P:(t + 1) * P],
                                   C("mean_128")[:, 0:1], start=True, stop=True)
            mm.then_inc(on_mm, 1)
            gate_piece(11)

            def last_product(name, first, x, ready):
                for m in range(KT):
                    piece = BASE[name] + m // 2
                    if first + m < 4:
                        pe.wait_ge(z_ev, 7 * KT - 3 + m)
                    elif first < 2 * KT or m < 4:
                        pe.wait_ge(dense_ev, first + m - 3)
                    else:
                        pe.wait_ge(h_done, 3 * KT + m - 3)
                    split_tile(ps[:, Z_BANKS[m % 4], 0:SEQ], 2, piece, piece % RING, m % 2, SEQ, x=x,
                               ready=(lambda b: pe.wait_ge(ready, b + 1)) if m == 0 and ready is not cv_lo_done else None)
                    if name == "w_b" and m == 1:
                        pe.wait_ge(on_rec, 1)
                        for hd in range(HEADS):
                            for t in range(TT):
                                mm = pe.matmul(ps[:, hd // 2, hd % 2 * SEQ + t * P:hd % 2 * SEQ + t * P + P],
                                               o_rms[:, t * HEADS + hd:t * HEADS + hd + 1].broadcast_to([P, P]), ident,
                                               start=True, stop=True)
                            if hd % 2:
                                mm.then_inc(on_mm, 1)
                    if name == "w_out_2" and m >= LAG - 1:
                        square_mean(4, m - (LAG - 1))

            pe.wait_ge(cv_lo_done, 1)
            last_product("w_b", 0, (cv_hi, cv_lo), cv_lo_done)
            last_product("w_a", KT, (o_hi, o_lo), o_lo_done)
            last_product("w_out_2", 2 * KT, (m_hi, m_lo), m_lo_done)
            norm(4, KT - (LAG - 1))
            pe.wait_ge(u_done, 5 * KT)
            pe.wait_ge(keys_in, 16)

            def tok_turn(n):
                t, half = n // 2 % 2, n % 2
                if n >= 2:
                    pe.wait_ge(tok_ev, n - 1)
                for i in range(4):
                    k = half * 4 + i
                    x = u[:, k, t * P:(t + 1) * P] if n < 4 else h[:, k, X0 + t * P:X0 + (t + 1) * P]
                    mm = pe.transpose(ps[:, 6 + n % 2, i * P:(i + 1) * P], x, ident)
                mm.then_inc(tok_mm, 1)

            for hd in range(HEADS):
                piece = BASE["wq"] + hd
                slot = piece % RING
                pe.wait_ge(landed[slot], piece // RING * 16 + 16)
                for e in range(2):
                    if hd >= 2:
                        pe.wait_ge(q_ev, (hd - 2) * 2 + e + 1)
                    for b in range(KT):
                        mm = pe.matmul(ps[:, hd % 2 * 2 + e, 0:SEQ], blk(slot, e * KT + b), u[:, b, 0:SEQ],
                                       start=(b == 0), stop=(b == KT - 1))
                    mm.then_inc(q_mm, 1)
                if hd < HEADS - 1:
                    pe.wait_ge(q_mm, 2 * hd + 2)
                    pe.sem_inc(used, 1)
                if hd == 0:
                    tok_turn(0)
                    tok_turn(1)
                pe.wait_ge(q_ev, 2 * hd + 2)
                if hd >= 2:
                    pe.wait_ge(sc_ev, hd - 1)
                for t in range(TT):
                    for e in range(2):
                        mm = pe.matmul(ps[:, 4 + hd % 2, (t * 2 + e) * NKEYS:(t * 2 + e + 1) * NKEYS],
                                       qh[:, hd % 2, e, t * P:(t + 1) * P], keys[:, hd * 2 + e, :], start=True, stop=True)
                mm.then_inc(sc_mm, 1)
                if hd == 0:
                    tok_turn(2)
                    tok_turn(3)
            for n in range(4, 8):
                tok_turn(n)
            pe.wait_ge(q_ev, 2 * HEADS)
            for k in range(KT):
                mm = pe.matmul(ps[:, k // 4, k % 4 * P:k % 4 * P + P], ada[:, 40 + k:41 + k].broadcast_to([P, P]), ident,
                               start=True, stop=True)
            mm.then_inc(gain_mm, 1)


def _blocks(w):
    k, m = w.shape
    return w.reshape(k // P, P, m // P, P).transpose(0, 2, 1, 3)


def _pieces(blocks):
    n = blocks.shape[0]
    return blocks.reshape(n // BLOCKS, BLOCKS, P, P).transpose(0, 2, 1, 3).reshape(n // BLOCKS, P, PIECE)


def _by_output(w):
    b = _blocks(w)
    return _pieces(b.transpose(1, 0, 2, 3).reshape(-1, P, P))


def _by_input(w):
    return _pieces(_blocks(w).reshape(-1, P, P))


def _wide(w):
    k, m = w.shape
    b = w.reshape(k // P, P, m // 512, 4, P).transpose(2, 0, 3, 1, 4)
    return _pieces(b.reshape(-1, P, P))


def layout(x):
    f = {k: np.asarray(v) for k, v in x.items()}

    def ffn(n):
        g, up, dn = f[f"w{n}_gate"][0], f[f"w{n}_up"][0], f[f"w{n}_down"][0]
        gu = np.stack([_blocks(g).transpose(1, 0, 2, 3), _blocks(up).transpose(1, 0, 2, 3)], 1)
        return np.concatenate([_pieces(gu.reshape(-1, P, P)), _by_input(dn)])

    w_in = f["w_in"][0]
    misc = np.zeros((D, P), np.float32)
    misc[:, PE_ROW:PE_ROW + ROPE] = w_in[:, 384:416]
    misc[:, FL_ROW:FL_ROW + HEADS] = w_in[:, 1952:1960]
    w_proj = np.concatenate([w_in[:, 0:384], misc, w_in[:, 416:416 + 1024]], 1)
    zs = np.split(f["w_in_2"][0], 8, axis=1)
    zq, zf, zi, zg, zca, zcb, zga, zgb = zs
    stream = np.concatenate(
        [ffn(1), _by_output(w_proj), _wide(w_in[:, 1440:1952]), _by_output(f["w_out"][0]), ffn(2)]
        + [_by_output(w) for w in (zca, zcb, zf, zq)] + [_wide(zi)] + [_by_output(w) for w in (zg, zga, zgb)]
        + [_by_output(f[n][0]) for n in ("w_b_2", "w_a_2", "w_out_2", "peer_wq_2")])
    assert stream.shape == (N_PIECES, P, PIECE)
    ada = f["ada_w_2"][0].reshape(KT, P, ADA_Q, ADA_W).transpose(0, 2, 1, 3).reshape(KT * ADA_Q, P, ADA_W)
    cols = np.zeros((P, N_COLS), np.float32)

    def put(name, v):
        v = v.reshape(-1, P).T
        cols[:, COL[name]:COL[name] + v.shape[1]] = v

    for name, key in (("g_ffn1", "g_ffn1"), ("g_mix", "g_mix"), ("g_ffn2", "g_ffn2"), ("norm1", "norm1_g_2"),
                      ("hg_g", "hg_norm_g_2"), ("conv_b", "conv_b_2"), ("ln_g", "conv_ln_g_2"),
                      ("ln_b", "conv_ln_b_2"), ("norm2", "norm2_g_2"), ("c", "c_2"), ("ada_b", "ada_b_2"),
                      ("g_cq", "g_cq"), ("g_ckv", "g_ckv"), ("conv_w", "conv_w_2")):
        put(name, f[key])
    put("lb0", f["lb_logits_2"][0])
    put("lb1", f["lb_logits_2"][1])
    cols[0:QK, COL["g_q"]] = f["g_q_mla"][0]
    cols[0:QK, COL["g_k"]] = f["g_k_mla"][0]
    for e in range(2):
        cols[HD * e:HD * e + HD, COL["g_fq"]] = f["g_q_fox"][0]
        cols[HD * e:HD * e + HD, COL["g_fk"]] = f["g_k_fox"][0]
    cols[FL_ROW:FL_ROW + HEADS, COL["b_f"]] = f["b_forget"][0]
    wukv = f["w_ukv"][0].reshape(P, HEADS, NOPE + HD)
    con, masks = constants()
    tokens = np.concatenate([f["meta_tokens"], f["x"][0]], 0)
    return {
        "x_t": tokens.T.reshape(KT, P, T).transpose(1, 0, 2),
        "stream": stream, "ada": ada, "cols": cols, "con": con, "masks": masks,
        "wuq": f["w_uq"][0].reshape(2, P, HEADS * QK).transpose(1, 0, 2),
        "wuk": wukv[:, :, :NOPE].reshape(P, HEADS * NOPE),
        "wuv": wukv[:, :, NOPE:].reshape(P, HEADS * HD),
        "keys": f["peer_keys_2"][0].reshape(2 * HEADS, NKEYS, P).transpose(2, 0, 1),
        "peer_u": f["peer_u_2"][0], "peer_v": f["peer_v_2"][0], "final_g": f["final_g_2"],
    }


def kernel(**inputs):
    import concourse.bacc as bacc
    from concourse.bass_utils import run_bass_kernel_spmd

    nc = bacc.Bacc("TRN2", target_bir_lowering=False, num_devices=1)
    arrays = {f"in_{k}": np.ascontiguousarray(v) for k, v in layout(inputs).items()}
    args = {k[3:]: nc.dram_tensor(k, v.shape, mybir.dt.from_np(v.dtype), kind="ExternalInput").ap()
            for k, v in arrays.items()}
    out = nc.dram_tensor("out", (1, SEQ, D), F32, kind="ExternalOutput").ap()
    program(nc, args, out)
    r = run_bass_kernel_spmd(nc, [arrays], core_ids=[0])
    return r.results[0]["out"]
```
